# Optimizing a Trainium2 kernel written in Bass

```python
import math
import jax
import jax.numpy as jnp
from jax import lax
import numpy as np

D_MODEL = 2048
BATCH = 1
SEQ = 256
DEPTH = 2

N_MIXERS = 2
N_HEADS = 8
HEAD_DIM = 128
V_DIM = 2 * HEAD_DIM
ATTN_WIDTH = N_HEADS * V_DIM
DIFF_QKV_COLS = 2 * N_HEADS * HEAD_DIM * 2 + N_HEADS * V_DIM
SW_GROUPS = ((128, 1), (512, 4), (2048, 16))
N_SW_GROUPS = len(SW_GROUPS)
SW_STEPS = 128
SW_GROUP_COLS = 2 * N_HEADS * HEAD_DIM + N_HEADS * V_DIM
BLOCK = 128
NUM_BUCKETS = 32
MAX_DISTANCE = 2048
D_FF = 5632
CONV_WIDTH = 3
EPS = 1e-6
NEG = -1e30
N_DIFF_LAYERS = (DEPTH + 1) // 2
N_DIL_LAYERS = DEPTH // 2

kernel_name = "hybrid_diffattn_dilated_convffn"

def rmsnorm(x, g):
    xf = x.astype(jnp.float32)
    y = xf * lax.rsqrt(jnp.mean(xf * xf, axis=-1, keepdims=True) + EPS)
    return (y * g.astype(jnp.float32)).astype(x.dtype)

def t5_bucket(dist):
    max_exact = NUM_BUCKETS // 2
    n = jnp.maximum(dist, 0)
    nf = jnp.maximum(n, 1).astype(jnp.float32)
    large = max_exact + (jnp.log(nf / max_exact) / math.log(MAX_DISTANCE / max_exact)
                         * (NUM_BUCKETS - max_exact)).astype(jnp.int32)
    large = jnp.minimum(large, NUM_BUCKETS - 1)
    return jnp.where(n < max_exact, n, large)

def diff_attention(h, w_qkv, q_gain, k_gain, lam, subln_g, w_o, rel_bias, layer_idx):
    B, S, _ = h.shape
    qkv = h @ w_qkv
    nqk = 2 * N_HEADS * HEAD_DIM
    q, k, v = jnp.split(qkv, [nqk, 2 * nqk], axis=-1)
    q = rmsnorm(q.reshape(B, S, N_HEADS, 2, HEAD_DIM), q_gain)
    k = rmsnorm(k.reshape(B, S, N_HEADS, 2, HEAD_DIM), k_gain)
    v = v.reshape(B, S, N_HEADS, V_DIM)
    lam_init = 0.8 - 0.6 * math.exp(-0.3 * layer_idx)
    lf = lam.astype(jnp.float32)
    lam_full = jnp.exp(jnp.sum(lf[0] * lf[1])) - jnp.exp(jnp.sum(lf[2] * lf[3])) + lam_init
    scale = HEAD_DIM ** -0.5
    nq = S // BLOCK
    q_blocks = q.reshape(B, nq, BLOCK, N_HEADS, 2, HEAD_DIM).transpose(1, 0, 2, 3, 4, 5)
    k_pos = jnp.arange(S)

    def block_fn(args):
        qb, start = args
        q_pos = start + jnp.arange(BLOCK)
        dist = q_pos[:, None] - k_pos[None, :]
        bias = jnp.moveaxis(rel_bias[t5_bucket(dist)], -1, 0).astype(jnp.float32)
        logits = jnp.einsum('bqhme,bkhme->bhmqk', qb, k).astype(jnp.float32) * scale + bias[:, None]
        logits = jnp.where(dist >= 0, logits, NEG)
        p = jax.nn.softmax(logits, axis=-1)
        a = p[:, :, 0] - lam_full * p[:, :, 1]
        return jnp.einsum('bhqk,bkhe->bqhe', a.astype(v.dtype), v)

    o = lax.map(block_fn, (q_blocks, jnp.arange(nq, dtype=jnp.int32) * BLOCK))
    o = o.transpose(1, 0, 2, 3, 4).reshape(B, S, N_HEADS, V_DIM)
    o = rmsnorm(o, subln_g) * (1.0 - lam_init)
    return o.reshape(B, S, ATTN_WIDTH) @ w_o

def dilated_attention(h, w_qkv, q_gain, k_gain, w_o, rel_bias):
    B, S, _ = h.shape
    qkv = (h @ w_qkv).reshape(B, S, N_SW_GROUPS, SW_GROUP_COLS)
    nqk = N_HEADS * HEAD_DIM
    scale = HEAD_DIM ** -0.5
    a_idx = jnp.arange(BLOCK)
    b_idx = jnp.arange(2 * BLOCK)
    dist_sub = a_idx[:, None] + BLOCK - b_idx[None, :]
    in_window = (dist_sub >= 0) & (dist_sub <= SW_STEPS)
    outs, lses = [], []
    for g, (window, dil) in enumerate(SW_GROUPS):
        q, k, v = jnp.split(qkv[:, :, g], [nqk, 2 * nqk], axis=-1)
        q = rmsnorm(q.reshape(B, S, N_HEADS, HEAD_DIM), q_gain[g])
        k = rmsnorm(k.reshape(B, S, N_HEADS, HEAD_DIM), k_gain[g])
        v = v.reshape(B, S, N_HEADS, V_DIM)
        L = S // dil
        nb = -(-L // BLOCK)
        Lp = nb * BLOCK

        def to_blocks(t):
            e = t.shape[-1]
            t = t.reshape(B, L, dil, N_HEADS, e)
            t = jnp.pad(t, ((0, 0), (0, Lp - L), (0, 0), (0, 0), (0, 0)))
            return t.reshape(B, nb, BLOCK, dil, N_HEADS, e)

        def with_prev(t):
            prev = jnp.pad(t[:, :-1], ((0, 0), (1, 0), (0, 0), (0, 0), (0, 0), (0, 0)))
            return jnp.concatenate([prev, t], axis=2)

        qb = to_blocks(q)
        kk = with_prev(to_blocks(k))
        vv = with_prev(to_blocks(v))
        bias = jnp.moveaxis(rel_bias[t5_bucket(dist_sub * dil)], -1, 0).astype(jnp.float32)
        key_valid = (jnp.arange(nb)[:, None] * BLOCK - BLOCK + b_idx[None, :]) >= 0
        mask = in_window[None] & key_valid[:, None, :]
        logits = jnp.einsum('bnqrhe,bnkrhe->bnrhqk', qb, kk).astype(jnp.float32) * scale + bias
        logits = jnp.where(mask[None, :, None, None], logits, NEG)
        m = jnp.max(logits, axis=-1, keepdims=True)
        p = jnp.exp(logits - m)
        l = jnp.sum(p, axis=-1, keepdims=True)
        o = jnp.einsum('bnrhqk,bnkrhe->bnqrhe', (p / l).astype(v.dtype), vv)
        lse = (m + jnp.log(l))[..., 0]
        o = o.reshape(B, Lp, dil, N_HEADS, V_DIM)[:, :L].reshape(B, S, N_HEADS, V_DIM)
        lse = lse.transpose(0, 1, 4, 2, 3).reshape(B, Lp, dil, N_HEADS)[:, :L].reshape(B, S, N_HEADS)
        outs.append(o)
        lses.append(lse)
    alpha = jax.nn.softmax(jnp.stack(lses, axis=0), axis=0)
    o = alpha[0][..., None] * outs[0] + alpha[1][..., None] * outs[1] + alpha[2][..., None] * outs[2]
    return o.astype(h.dtype).reshape(B, S, ATTN_WIDTH) @ w_o

def conv_ffn(h, w_up, conv_w, conv_b, w_down):
    u = h @ w_up
    c = u.shape[-1]
    u = lax.conv_general_dilated(u, conv_w[:, None, :].astype(u.dtype), window_strides=(1,),
                                 padding=[(CONV_WIDTH - 1, 0)],
                                 dimension_numbers=('NWC', 'WIO', 'NWC'),
                                 feature_group_count=c) + conv_b
    gate, val = jnp.split(u, 2, axis=-1)
    return (jax.nn.silu(gate) * val) @ w_down

def setup_inputs(seed: int = 0) -> dict:
    key = jax.random.key(seed)
    ks = jax.random.split(key, 20)
    f32 = jnp.float32
    nrm = lambda k, shape, s: jax.random.normal(k, shape, f32) * s
    gain = lambda k, shape: 1.0 + 0.02 * jax.random.normal(k, shape, f32)
    return {
        "x": jax.random.normal(ks[0], (BATCH, SEQ, D_MODEL), f32),
        "rel_bias": nrm(ks[1], (NUM_BUCKETS, N_HEADS), 0.2),
        "ln_mix": gain(ks[2], (DEPTH, D_MODEL)),
        "ln_ffn": gain(ks[3], (DEPTH, D_MODEL)),
        "a_w_qkv": nrm(ks[4], (N_DIFF_LAYERS, D_MODEL, DIFF_QKV_COLS), D_MODEL ** -0.5),
        "a_q_norm": gain(ks[5], (N_DIFF_LAYERS, HEAD_DIM)),
        "a_k_norm": gain(ks[6], (N_DIFF_LAYERS, HEAD_DIM)),
        "a_lambda": nrm(ks[7], (N_DIFF_LAYERS, 4, HEAD_DIM), 0.1),
        "a_subln": gain(ks[8], (N_DIFF_LAYERS, V_DIM)),
        "a_w_o": nrm(ks[9], (N_DIFF_LAYERS, ATTN_WIDTH, D_MODEL), ATTN_WIDTH ** -0.5),
        "b_w_qkv": nrm(ks[10], (N_DIL_LAYERS, D_MODEL, N_SW_GROUPS * SW_GROUP_COLS), D_MODEL ** -0.5),
        "b_q_norm": gain(ks[11], (N_DIL_LAYERS, N_SW_GROUPS, HEAD_DIM)),
        "b_k_norm": gain(ks[12], (N_DIL_LAYERS, N_SW_GROUPS, HEAD_DIM)),
        "b_w_o": nrm(ks[13], (N_DIL_LAYERS, ATTN_WIDTH, D_MODEL), ATTN_WIDTH ** -0.5),
        "f_w_up": nrm(ks[14], (DEPTH, D_MODEL, 2 * D_FF), D_MODEL ** -0.5),
        "f_conv_w": nrm(ks[15], (DEPTH, CONV_WIDTH, 2 * D_FF), CONV_WIDTH ** -0.5),
        "f_conv_b": nrm(ks[16], (DEPTH, 2 * D_FF), 0.02),
        "f_w_down": nrm(ks[17], (DEPTH, D_FF, D_MODEL), D_FF ** -0.5),
    }

def reference(x, rel_bias, ln_mix, ln_ffn, a_w_qkv, a_q_norm, a_k_norm, a_lambda, a_subln, a_w_o,
              b_w_qkv, b_q_norm, b_k_norm, b_w_o, f_w_up, f_conv_w, f_conv_b, f_w_down):
    h = x
    for i in range(DEPTH):
        y = rmsnorm(h, ln_mix[i])
        j = i // N_MIXERS
        if i % N_MIXERS == 0:
            h = h + diff_attention(y, a_w_qkv[j], a_q_norm[j], a_k_norm[j], a_lambda[j],
                                   a_subln[j], a_w_o[j], rel_bias, i)
        else:
            h = h + dilated_attention(y, b_w_qkv[j], b_q_norm[j], b_k_norm[j], b_w_o[j], rel_bias)
        h = h + conv_ffn(rmsnorm(h, ln_ffn[i]), f_w_up[i], f_conv_w[i], f_conv_b[i], f_w_down[i])
    return h


_drawn_inputs = setup_inputs


def setup_inputs(seed=0):
    import zlib

    import numpy as np

    out = dict(_drawn_inputs(seed))
    spreads = {}
    factors = {'ln_ffn': 3.289,
     'a_q_norm': 3.63,
     'a_k_norm': 4.001,
     'a_subln': 3.91,
     'b_q_norm': 23.109,
     'b_k_norm': 25.391,
     'f_conv_b': 3.319}
    for name, (base, spread) in spreads.items():
        noise = np.random.default_rng([zlib.crc32(name.encode()), seed]).standard_normal(out[name].shape)
        drawn = base * np.exp(spread * noise) if base else spread * noise
        out[name] = jnp.asarray(drawn.astype(out[name].dtype))
    for name, factor in factors.items():
        out[name] = (out[name] * factor).astype(out[name].dtype)
    return out
```

```python
import math
from contextlib import ExitStack, contextmanager

import numpy as np

import concourse.bass as bass
from concourse import mybir

F32 = mybir.dt.float32
F32R = mybir.dt.float32r
I32 = mybir.dt.int32
ALU = mybir.AluOpType
ACT = mybir.ActivationFunctionType
AX = mybir.AxisListType

P = 128
SEQ, D = 256, 2048
M = SEQ // P
KB = D // P
H, HD, VD = 8, 128, 256
F = 5632
FB = F // P
EPS = 1e-6
SCALE = HD ** -0.5
BUCKETS, MAX_DISTANCE = 32, 2048
GROUPS = ((128, 1), (512, 4), (2048, 16))
G = len(GROUPS)
MASKED = -1e30
LAM_INIT = 0.8 - 0.6 * math.exp(-0.3 * 0)

W = 2048
SLOTS = 4
LEAD = 2

A_HEAD, B_HEAD, OUT, UP_PAIR, UP_PAIRS, DOWN = 8, 12, 16, 8, FB // 4, FB
A0 = 0
AO0 = A0 + H * A_HEAD
UP0 = (AO0 + OUT, 0)
DN0 = (UP0[0] + UP_PAIR * UP_PAIRS, 0)
B0 = DN0[0] + DOWN
BO0 = B0 + H * B_HEAD
UP0 = (UP0[0], BO0 + OUT)
DN0 = (DN0[0], UP0[1] + UP_PAIR * UP_PAIRS)
END = DN0[1] + DOWN
assert all(x % SLOTS == 0 for x in (AO0, *UP0, *DN0, B0, BO0, A_HEAD, B_HEAD, OUT, UP_PAIR, DOWN))



def loads_of(c):
    if A0 <= c < AO0:
        return 2 if (c - A0) % A_HEAD < 4 else 1
    if AO0 <= c < AO0 + LEAD:
        return 2
    if B0 <= c < BO0 + LEAD:
        return 3
    return 1


def landed(c):
    return 16 * sum(loads_of(i) for i in range(c % SLOTS, c + 1, SLOTS))


A_RATE, B_RATE, RATE = 16 * 3 // A_HEAD, 16 * 9 // B_HEAD, 16 // SLOTS

G_MIX, G_FFN, G_AQ, G_AK, G_BQ, G_BK, G_SUB = 0, 32, 64, 65, 66, 69, 72
GAINS = 74

ROW = 384
KINDS = 1 + G

MAGIC = 0x5F3759DF
NEWTON = 3
RSQRT_STEPS = 3 + 3 * NEWTON


def bucket_of(dist):
    exact = BUCKETS // 2
    n = max(dist, 0)
    if n < exact:
        return n
    return min(exact + int(math.log(n / exact) / math.log(MAX_DISTANCE / exact) * (BUCKETS - exact)), BUCKETS - 1)


def shape_tables():
    onehot = np.zeros((BUCKETS, ROW), np.float32)
    for i in range(ROW):
        onehot[bucket_of(SEQ - 1 - i), i] = 1.0
    dist = P + np.arange(P)[:, None] - np.arange(SEQ)[None, :]
    masks = np.zeros((P, KINDS, SEQ), np.float32)
    masks[:, 0][dist < 0] = MASKED
    for g, (_, dil) in enumerate(GROUPS):
        masks[:, 1 + g][(dist < 0) | (dist % dil != 0) | (dist > P * dil)] = MASKED
    return {"identity": np.eye(P, dtype=np.float32), "onehot": onehot, "masks": masks}


class Chain:

    def __init__(self, engine, sem):
        self.engine, self.sem, self.n, self.offset = engine, sem, 0, 0

    def step(self, instruction):
        instruction.then_inc(self.sem, 1)
        self.n += 1

    def settle(self):
        self.engine.wait_ge(self.sem, self.n + self.offset)

    @contextmanager
    def loop(self, turn, turns, steps):
        start, self.offset = self.n, turn * steps
        yield
        assert self.n - start == steps, (self.n - start, steps)
        self.n, self.offset = start + steps * turns, 0


def trunk(nc, x, rel_bias, ln_mix, ln_ffn, a_w_qkv, a_q_norm, a_k_norm, a_lambda, a_subln, a_w_o,
          b_w_qkv, b_q_norm, b_k_norm, b_w_o, f_w_up, f_conv_w, f_conv_b, f_w_down,
          identity, onehot, masks, out):
    bias_rows = nc.dram_tensor("bias_rows", (H, ROW), F32)
    bias_wide = nc.dram_tensor("bias_wide", (P, H, ROW), F32)

    with ExitStack() as ctx:
        def sb(name, shape, dt=F32):
            return ctx.enter_context(nc.sbuf_tensor(name, shape, dt))

        def sem(name):
            return ctx.enter_context(nc.semaphore(name))

        w_raw = sb("w_raw", [P, SLOTS, W])
        w_hi = sb("w_hi", [P, SLOTS, W], F32R)
        w_lo = sb("w_lo", [P, SLOTS, W], F32R)
        xT = sb("xT", [P, KB, 2, SEQ], F32R)
        resid = sb("resid", [P, M, D])
        ident = sb("ident", [P, P])
        gains = sb("gains", [P, GAINS])
        conv = sb("conv", [P, 2, 4, 2 * FB])
        sub_g = sb("sub_g", [P, 2])
        nlam = sb("nlam", [P, 1])
        small = sb("small", [P, 96])
        psum = ctx.enter_context(nc.psum_tensor("psum", [P, 8, 512], F32))

        phase = sb("phase", [P, 14848])

        def part(at, *dims):
            n = int(np.prod(dims))
            assert at + n <= 14848
            v = phase[:, at:at + n]
            if len(dims) == 2:
                v = v.rearrange("p (a b) -> p a b", b=dims[1])
            if len(dims) == 3:
                v = v.rearrange("p (a b c) -> p a b c", b=dims[1], c=dims[2])
            return v

        y = part(0, M, D)
        a_qk = part(0, M, 512)
        a_sq = part(1024, M, 512)
        a_qT = part(2048, 2, SEQ)
        a_kT = part(2560, 2, SEQ)
        a_v = part(3072, M, VD)
        a_lg = part(3584, 768)
        a_a = part(4352, 384)
        a_aT = part(4736, 3, P)
        a_o = part(5120, M, VD)
        a_oT = part(5632, KB, SEQ)
        a_bias = part(9728, H, SEQ)
        b_raw = part(0, G * M, 512)
        b_qT = part(3072, G, SEQ)
        b_kT = part(3840, G, SEQ)
        b_v = part(4608, G * M, VD)
        b_lg = part(6144, 1152)
        b_pT = part(7296, 9, P)
        b_o = part(8448, M, VD)
        b_sq = part(7296, G * M, 256)
        b_bias = part(8960, G, SEQ)
        b_mask = part(9728, G, SEQ)
        b_row = part(10496, SEQ)
        b_oT = part(10752, KB, SEQ)
        hT = part(0, FB, SEQ)
        u = part(11264, 4, SEQ + 2)
        c_gate = part(12296, 4, SEQ)
        c_val = part(13320, 4, SEQ)
        t_onehot = part(5632, ROW)
        t_mask = part(6016, 1, SEQ)
        t_rows = part(6272, ROW)
        t_rel = part(6656, H)
        t_lam = part(11776, 4, HD)
        t_gain = part(12288, P)
        t_conv = part(12416, 8, P)
        t_prod = part(13440, 2, HD)

        ssp = small[:, 0:8]
        r_ss, r_r, r_t = small[:, 8:10], small[:, 10:12], small[:, 12:14]
        n_ss, n_r, n_t = small[:, 16:28], small[:, 28:40], small[:, 40:52]
        mx, nmx = small[:, 52:56], small[:, 56:60]
        den, rden, rneg = small[:, 60:64], small[:, 64:68], small[:, 68:70]
        o_ss, o_r, o_t = small[:, 70:72], small[:, 72:74], small[:, 74:76]
        lam_s, lam_e = small[:, 76:78], small[:, 78:80]

        x_in, ident_in, onehot_in, mask_in, rel_in, lam_in, gain_in, conv_in = (
            sem(n) for n in ("x_in", "ident_in", "onehot_in", "mask_in", "rel_in", "lam_in", "gain_in", "conv_in"))
        pe_setup, bias_rows_made, bias_rows_out, bias_wide_out, a_row_in, a_bias_ready, b_mask_in, gains_ready, lam_prod, lam_exp, lam_ready, consts_ready = (
            sem(n) for n in ("pe_setup", "bias_rows_made", "bias_rows_out", "bias_wide_out", "a_row_in",
                             "a_bias_ready", "b_mask_in", "gains_ready", "lam_prod",
                             "lam_exp", "lam_ready", "consts_ready"))
        w_in = [sem(f"w_in{s}") for s in range(SLOTS)]
        hi_ready, lo_ready, used = sem("w_hi_ready"), sem("w_lo_ready"), sem("w_used")
        act_chain, dve_chain = sem("act_chain"), sem("dve_chain")
        r_add, r_sq, r_rstd, y_act, y_dve = (sem(n) for n in ("r_add", "r_sq", "r_rstd", "y_act", "y_dve"))
        xT_ps, xT_hi, xT_lo = sem("xT_ps"), sem("xT_hi"), sem("xT_lo")
        xs_hi, xs_lo = sem("xs_hi"), sem("xs_lo")
        (a_qk_act, a_qk_dve, a_sq_ready, a_qkn, a_tqk, a_qT_ready, a_kT_ready, a_v_act, a_v_dve, a_scores,
         a_lg_ready, a_nmx, a_probs, a_diff, a_ta, a_aT_ready, a_pv, a_oss, a_orstd, a_on, a_to, a_oT_act,
         a_oT_dve) = (sem(n) for n in (
             "a_qk_act", "a_qk_dve", "a_sq_ready", "a_qkn", "a_tqk", "a_qT_ready", "a_kT_ready", "a_v_act", "a_v_dve",
             "a_scores", "a_lg_ready", "a_nmx", "a_probs", "a_diff", "a_ta", "a_aT_ready", "a_pv", "a_oss", "a_orstd",
             "a_on", "a_to", "a_oT_act", "a_oT_dve"))
        (b_raw_act, b_raw_dve, b_sq_ready, b_qkn, b_vheld, b_tqk, b_qT_ready, b_kT_ready, b_scores, b_row_in, b_bias_ready,
         b_lg_ready, b_nmx, b_probs, b_rden, b_tp, b_pT_act, b_pT_dve, b_pv, b_on, b_to, b_oT_act,
         b_oT_dve) = (sem(n) for n in (
             "b_raw_act", "b_raw_dve", "b_sq_ready", "b_qkn", "b_vheld", "b_tqk", "b_qT_ready", "b_kT_ready",
             "b_scores", "b_row_in", "b_bias_ready", "b_lg_ready", "b_nmx", "b_probs", "b_rden", "b_tp", "b_pT_act", "b_pT_dve",
             "b_pv", "b_on", "b_to", "b_oT_act", "b_oT_dve"))
        gate_low, val_low, gate_read, val_read, gate_init, val_init, gate_taps, silu_ready, h_ready = (sem(n) for n in (
            "gate_low", "val_low", "gate_read", "val_read", "gate_init", "val_init", "gate_taps", "silu_ready", "h_ready"))
        down_quarter = sem("down_quarter")
        out_done = sem("out_done")

        block = ctx.enter_context(nc.Block())

        def at_least(engine, s, value):
            if not (isinstance(value, int) and value <= 0):
                engine.wait_ge(s, value)

        def chunk_used(engine, c, more=0):
            engine.wait_ge(used, c + 1 + more)

        @block.sync
        def _(sp):
            for m in range(M):
                sp.dma_start(resid[:, m, :], x[0, m * P:(m + 1) * P, :]).then_inc(x_in, 16)

            def free_slot(c, more=0):
                at_least(sp, lo_ready, c - SLOTS + 1 + more)

            def load_a_head(c, h, more=0):
                for j in range(A_HEAD):
                    free_slot(c + j, more)
                    rows = a_w_qkv[0, 512 * (j % 4):512 * (j % 4 + 1), :]
                    slot = (c + j) % SLOTS
                    if j < 4:
                        tile = w_raw[:, slot, :].rearrange("p (k c) -> p k c", k=4)
                        for s in range(2):
                            src = rows[:, 2048 * s:2048 * (s + 1)].rearrange("(k p) c -> p k c", p=P)
                            sp.dma_start(tile[:, :, 256 * s:256 * (s + 1)],
                                         src[:, :, bass.ts(h, 256)]).then_inc(w_in[slot], 16)
                    else:
                        src = rows[:, 4096:6144].rearrange("(k p) c -> p k c", p=P)[:, :, bass.ts(h, 256)]
                        dst = w_raw[:, slot, 0:1024].rearrange("p (k c) -> p k c", k=4)
                        sp.dma_start(dst, src).then_inc(w_in[slot], 16)

            def load_b_head(c, h, more=0):
                for j in range(B_HEAD):
                    g, slot = j // 4, (c + j) % SLOTS
                    free_slot(c + j, more)
                    rows = b_w_qkv[0, 512 * (j % 4):512 * (j % 4 + 1), 4096 * g:4096 * (g + 1)]
                    dst = w_raw[:, slot, :].rearrange("p (k c) -> p k c", k=4)
                    for at, n, first in ((0, HD, 0), (HD, HD, 1024), (256, VD, 2048)):
                        src = rows[:, first:first + H * n].rearrange("(k p) c -> p k c", p=P)[:, :, bass.ts(h, n)]
                        sp.dma_start(dst[:, :, at:at + n], src).then_inc(w_in[slot], 16)

            def load_out(c, w):
                for j in range(OUT):
                    slot = (c + j) % SLOTS
                    free_slot(c + j)
                    src = w[0, 256 * (j % 8):256 * (j % 8 + 1), 1024 * (j // 8):1024 * (j // 8 + 1)].rearrange(
                        "(k p) c -> p k c", p=P)
                    dst = w_raw[:, slot, :].rearrange("p (k c) -> p k c", k=2)
                    n = loads_of(c + j)
                    pieces = [(slice(0, 1), slice(0, 1024)), (slice(1, 2), slice(0, 512)), (slice(1, 2), slice(512, 1024))]
                    if n == 2:
                        pieces[1:] = [(slice(1, 2), slice(0, 1024))]
                    if n == 1:
                        pieces = [(slice(0, 2), slice(0, 1024))]
                    for k, cols in pieces:
                        sp.dma_start(dst[:, k, cols], src[:, k, cols]).then_inc(w_in[slot], 16)

            def load_ffn(layer):
                c = UP0[layer]
                with sp.Fori(0, UP_PAIRS) as t:
                    for j in range(UP_PAIR):
                        slot = (c + j) % SLOTS
                        free_slot(c + j, t * UP_PAIR)
                        half = F * (j // 4)
                        src = f_w_up[layer, 512 * (j % 4):512 * (j % 4 + 1), half:half + F].rearrange(
                            "(k p) c -> p k c", p=P)[:, :, bass.ts(t, 512)]
                        dst = w_raw[:, slot, :].rearrange("p (k c) -> p k c", k=4)
                        sp.dma_start(dst, src).then_inc(w_in[slot], 16)
                c = DN0[layer]
                rows = f_w_down[layer].rearrange("(t j p) c -> p t j c", p=P, j=4)
                with sp.Fori(0, DOWN // 4) as t:
                    for j in range(4):
                        slot = (c + j) % SLOTS
                        free_slot(c + j, t * 4)
                        sp.dma_start(w_raw[:, slot, :], rows[:, bass.ts(t, 1), j, :].rearrange("p t c -> p (t c)")).then_inc(w_in[slot], 16)

            load_a_head(A0, 0)
            with sp.Fori(1, H) as h:
                load_a_head(A0 + A_HEAD, h, (h - 1) * A_HEAD)
            load_out(AO0, a_w_o)
            load_ffn(0)
            with sp.Fori(0, H) as h:
                load_b_head(B0, h, h * B_HEAD)
            load_out(BO0, b_w_o)
            load_ffn(1)
            for q in range(4):
                sp.wait_ge(r_add, 12 + q + 1)
                sp.dma_start(out[0].rearrange("(m p) d -> p m d", p=P)[:, :, 512 * q:512 * (q + 1)],
                             resid[:, :, 512 * q:512 * (q + 1)]).then_inc(out_done, 16)
            sp.wait_ge(out_done, 64)

        @block.gpsimd
        def _(pool):
            def tables(first, heads):
                return bass.AP(bias_wide, first * ROW + P - 1, [[H * ROW - 1, P], [ROW, heads], [1, SEQ]])

            pool.wait_ge(bias_rows_made, 1)
            pool.dma_start(bias_rows[:, :], t_rows[0:H, :]).then_inc(bias_rows_out, 16)
            pool.wait_ge(bias_rows_out, 16)
            pool.dma_start(bias_wide[:, :, :], bass.AP(bias_rows, 0, [[0, P], [ROW, H], [1, ROW]])).then_inc(bias_wide_out, 16)
            pool.wait_ge(bias_wide_out, 16)
            pool.dma_start(a_bias, tables(0, H)).then_inc(a_row_in, 16)
            pool.wait_ge(a_row_in, 16)
            pool.wait_ge(mask_in, 16)
            nc.gpsimd.tensor_tensor(a_bias, a_bias, t_mask.to_broadcast([P, H, SEQ]), ALU.add).then_inc(a_bias_ready, 1)

            pool.wait_ge(r_add, 8)
            pool.dma_start(b_mask, masks[:, 1:KINDS, :]).then_inc(b_mask_in, 16)
            pool.wait_ge(b_mask_in, 16)

            def b_head(h):
                if h > 0:
                    pool.wait_ge(b_bias_ready, h)
                pool.dma_start(b_row, tables(h, 1)).then_inc(b_row_in, 16)
                pool.wait_ge(b_row_in, 16 * h + 16)
                if h > 0:
                    pool.wait_ge(b_lg_ready, h)
                nc.gpsimd.tensor_tensor(b_bias, b_row.unsqueeze(1).to_broadcast([P, G, SEQ]), b_mask,
                                        ALU.add).then_inc(b_bias_ready, 1)
                pool.wait_ge(b_raw_act, 3 * h + 3)
                pool.wait_ge(b_raw_dve, 3 * h + 3)
                if h > 0:
                    pool.wait_ge(b_pv, h)
                nc.gpsimd.tensor_copy(b_v, b_raw[:, :, 256:512]).then_inc(b_vheld, 1)

            for h in range(H):
                b_head(h)

        @block.scalar
        def _(act):
            chain = Chain(act, act_chain)

            def split(c, more=0, width=W, rate=RATE):
                if c >= END:
                    return
                slot = c % SLOTS
                act.wait_ge(w_in[slot], landed(c) + more * rate)
                at_least(act, used, c - SLOTS + 1 + more)
                nc.scalar.activation(w_hi[:, slot, 0:width], w_raw[:, slot, 0:width], ACT.Copy).then_inc(hi_ready, 1)

            def a_width(j):
                return W if j % A_HEAD < 4 else W // 2

            def squares(n, q):
                for m in range(M):
                    ins = nc.scalar.activation(y[:, m, 512 * q:512 * (q + 1)], resid[:, m, 512 * q:512 * (q + 1)],
                                               ACT.Square, accum_out=ssp[:, 4 * m + q:4 * m + q + 1])
                ins.then_inc(r_sq, 1)

            def norm(n, gain):
                act.wait_ge(r_rstd, n + 1)
                for q in range(4):
                    nc.scalar.activation(y[:, 0, 512 * q:512 * (q + 1)], resid[:, 0, 512 * q:512 * (q + 1)], ACT.Copy,
                                         scale=r_r[:, 0:1]).then_inc(y_act, 1)
                for k in range(KB):
                    act.wait_ge(xT_ps, KB // 2 * n + k // 2 + 1)
                    at = 256 * (k % 2)
                    nc.scalar.activation(xT[:, k, 0, :], psum[:, 4 + k // 2 % 4, at:at + 256], ACT.Copy,
                                         scale=gains[:, gain + k:gain + k + 1]).then_inc(xT_hi, 1)

            def a_take_qk(c, h, more=0):
                chunk_used(act, c, more)
                at_least(act, a_tqk, h)
                nc.scalar.activation(a_qk[:, 0, :], psum[:, 0, :], ACT.Copy).then_inc(a_qk_act, 1)
                act.wait_ge(a_qk_act, h + 1)
                act.wait_ge(a_qk_dve, h + 1)
                nc.scalar.activation(a_sq, a_qk, ACT.Square).then_inc(a_sq_ready, 1)

            def a_take_q(h):
                act.wait_ge(a_tqk, h + 1)
                at_least(act, a_scores, h)
                nc.scalar.activation(a_qT, psum[:, 4, :].rearrange("p (a b) -> p a b", a=2), ACT.Copy,
                                     scale=gains[:, G_AQ:G_AQ + 1]).then_inc(a_qT_ready, 1)

            def a_take_v(c, h, more=0):
                chunk_used(act, c, more)
                at_least(act, a_pv, h)
                nc.scalar.activation(a_v[:, 0, :], psum[:, 2, 0:VD], ACT.Copy).then_inc(a_v_act, 1)

            def a_exp(h):
                act.wait_ge(a_nmx, h + 1)
                for i in range(2):
                    nc.scalar.activation(a_lg[:, 256 * i:256 * (i + 1)], a_lg[:, 256 * i:256 * (i + 1)], ACT.Exp,
                                         bias=nmx[:, i:i + 1], accum_out=den[:, i:i + 1])
                for i in range(2):
                    at = 512 + 128 * i
                    ins = nc.scalar.activation(a_lg[:, at:at + 128], a_lg[:, at:at + 128], ACT.Exp,
                                               bias=nmx[:, 2 + i:3 + i], accum_out=den[:, 2 + i:3 + i])
                ins.then_inc(a_probs, 1)

            def a_take_aT(h):
                act.wait_ge(a_ta, h + 1)
                at_least(act, a_pv, h)
                nc.scalar.activation(a_aT, psum[:, 4, 0:384].rearrange("p (a b) -> p a b", a=3),
                                     ACT.Copy).then_inc(a_aT_ready, 1)

            def a_norm_o(h):
                act.wait_ge(a_pv, h + 1)
                at_least(act, a_to, h)
                for b in range(M):
                    ins = nc.scalar.activation(a_o[:, b, :], psum[:, 5, VD * b:VD * (b + 1)], ACT.Square,
                                               accum_out=o_ss[:, b:b + 1])
                ins.then_inc(a_oss, 1)
                act.wait_ge(a_orstd, h + 1)
                for b in range(M):
                    ins = nc.scalar.activation(a_o[:, b, :], psum[:, 5, VD * b:VD * (b + 1)], ACT.Copy,
                                               scale=o_r[:, b:b + 1])
                ins.then_inc(a_on, 1)

            def a_take_oT(h):
                act.wait_ge(a_to, h + 1)
                nc.scalar.activation(a_oT[:, bass.ds(2 * h, 1), :], psum[:, 6, 0:SEQ].rearrange("p (a b) -> p a b", a=1),
                                     ACT.Copy, scale=sub_g[:, 0:1]).then_inc(a_oT_act, 1)

            def a_attend(j, h):
                if j == 1:
                    a_take_aT(h)
                if j == 2:
                    a_norm_o(h)
                if j == 3:
                    a_take_oT(h)

            def a_head(c, h, more=0):
                for j in range(A_HEAD):
                    split(c + j + LEAD, more, a_width(j + LEAD), A_RATE)
                    if j == 3:
                        a_take_qk(c + j, h, more)
                    if not isinstance(h, int) or h > 0:
                        a_attend(j, h - 1)
                    if j == 6:
                        a_take_q(h)
                    if j == 7:
                        a_take_v(c + j, h, more)
                        a_exp(h)

            def split_o(oT, oT_act, oT_dve, hd):
                act.wait_ge(oT_act, hd + 1)
                act.wait_ge(oT_dve, hd + 1)
                nc.scalar.activation(xT[:, 2 * hd:2 * hd + 2, 0, :], oT[:, 2 * hd:2 * hd + 2, :],
                                     ACT.Copy).then_inc(xs_hi, 1)

            def out_proj(c, n, oT, oT_act, oT_dve, attend):
                chunk_used(act, c - 1)
                split_o(oT, oT_act, oT_dve, 0)
                split_o(oT, oT_act, oT_dve, 1)
                for j in range(OUT):
                    split(c + j + LEAD)
                    attend(j, H - 1)
                    if j < 5:
                        split_o(oT, oT_act, oT_dve, j + 2)
                    if j == 6:
                        split_o(oT, oT_act, oT_dve, H - 1)
                    if j in (7, 15):
                        for q in (j // 8 * 2, j // 8 * 2 + 1):
                            act.wait_ge(r_add, 4 * (n - 1) + q + 1)
                            squares(n, q)

            def conv_init(c, more, layer, tile, low, ready, init, dst, t, tg):
                chunk_used(act, c, more)
                at_least(act, h_ready, tg)
                nc.scalar.activation(dst, psum[:, 4 * tile:4 * tile + 4, SEQ:2 * SEQ], ACT.Copy).then_inc(low, 1)
                act.wait_ge(ready, tg + 1)
                for b in range(4):
                    ch = bass.ds(t * 4 + (FB * tile + b), 1)
                    nc.scalar.activation(dst[:, b, :], u[:, b, 2:SEQ + 2], ACT.Identity,
                                         scale=conv[:, layer, 2, ch], bias=conv[:, layer, 3, ch]).then_inc(init, 1)

            def up_pair(layer, c, t, tg, more=0):
                for j in range(UP_PAIR):
                    split(c + j + LEAD, more)
                    if j == 3:
                        conv_init(c + j, more, layer, 0, gate_low, gate_read, gate_init, c_gate, t, tg)
                    if j == 4:
                        act.wait_ge(gate_taps, tg + 1)
                        nc.scalar.activation(c_gate, c_gate, ACT.Silu).then_inc(silu_ready, 1)
                    if j == 7:
                        conv_init(c + j, more, layer, 1, val_low, val_read, val_init, c_val, t, tg)

            def split_h(layer, b, t=0):
                slot = 4 * b if b == 0 else 4 + 4 * ((b - 1) % 2)
                nc.scalar.activation(xT[:, slot:slot + 4, 0, :], hT[:, bass.ds(4 * b + 8 * t, 4), :],
                                     ACT.Copy).then_inc(xs_hi, 1)

            def down(layer, c, n):
                act.wait_ge(h_ready, UP_PAIRS * (layer + 1))
                chunk_used(act, c - 1)
                split_h(layer, 0)
                split_h(layer, 1)
                for j in range(4):
                    split(c + j + LEAD)
                with act.Fori(0, 4) as t:
                    for j in range(8):
                        split(c + 4 + j + LEAD, t * 8)
                        if j == 1:
                            chunk_used(act, c + 3, t * 8)
                            split_h(layer, 2, t)
                        if j == 5:
                            chunk_used(act, c + 7, t * 8)
                            split_h(layer, 3, t)
                for j in range(8):
                    split(c + 36 + j + LEAD)
                    if j == 1:
                        chunk_used(act, c + 35)
                        split_h(layer, 10)
                if layer == 0:
                    for q in range(4):
                        act.wait_ge(r_add, 4 * (n - 1) + q + 1)
                        squares(n, q)

            def ffn(layer, n):
                norm(n, G_FFN + KB * layer)
                c = UP0[layer]
                up_pair(layer, c, 0, UP_PAIRS * layer)
                with act.Fori(1, UP_PAIRS) as t:
                    up_pair(layer, c + UP_PAIR, t, t + UP_PAIRS * layer, (t - 1) * UP_PAIR)
                down(layer, DN0[layer], n + 1)

            def b_take(c, g, h, more=0):
                chunk_used(act, c, more)
                at_least(act, b_tqk, h)
                at_least(act, b_vheld, h)
                nc.scalar.activation(b_raw[:, 2 * g, :], psum[:, 2 * (g % 2), :], ACT.Copy).then_inc(b_raw_act, 1)

            def b_squares(h):
                act.wait_ge(b_raw_act, 3 * h + 3)
                act.wait_ge(b_raw_dve, 3 * h + 3)
                nc.scalar.activation(b_sq, b_raw[:, :, 0:256], ACT.Square).then_inc(b_sq_ready, 1)

            def b_attend(j, h):
                if j == 1:
                    act.wait_ge(b_tqk, h + 1)
                    at_least(act, b_scores, h)
                    for g in range(G):
                        at = SEQ * (g % 2)
                        ins = nc.scalar.activation(b_qT[:, g, :], psum[:, 4 + g // 2, at:at + SEQ], ACT.Copy,
                                                   scale=gains[:, G_BQ + g:G_BQ + g + 1])
                    ins.then_inc(b_qT_ready, 1)
                if j == 2:
                    act.wait_ge(b_nmx, h + 1)
                    nc.scalar.activation(b_lg[:, 0:768], b_lg[:, 0:768], ACT.Exp, bias=nmx[:, 1:2],
                                         accum_out=den[:, 1:2])
                    nc.scalar.activation(b_lg[:, 768:1152], b_lg[:, 768:1152], ACT.Exp, bias=nmx[:, 0:1],
                                         accum_out=den[:, 0:1]).then_inc(b_probs, 1)
                if j == 4:
                    act.wait_ge(b_tp, h + 1)
                    at_least(act, b_pv, h)
                    nc.scalar.activation(b_pT[:, 0:4, :], psum[:, 4, :].rearrange("p (a b) -> p a b", a=4),
                                         ACT.Copy).then_inc(b_pT_act, 1)
                if j == 5:
                    act.wait_ge(b_pv, h + 1)
                    act.wait_ge(b_rden, h + 1)
                    at_least(act, b_to, h)
                    for b in range(M):
                        ins = nc.scalar.activation(b_o[:, b, :], psum[:, 7, VD * b:VD * (b + 1)], ACT.Copy,
                                                   scale=rden[:, b:b + 1])
                    ins.then_inc(b_on, 1)
                if j == 6:
                    act.wait_ge(b_to, h + 1)
                    nc.scalar.activation(b_oT[:, bass.ds(2 * h, 1), :],
                                         psum[:, 6, 0:SEQ].rearrange("p (a b) -> p a b", a=1),
                                         ACT.Copy).then_inc(b_oT_act, 1)

            def b_head(c, h, more=0):
                for j in range(B_HEAD):
                    split(c + j + LEAD, more, W, B_RATE)
                    if not isinstance(h, int) or h > 0:
                        b_attend(j, h - 1)
                    if j % 4 == 3:
                        b_take(c + j, j // 4, h, more)
                b_squares(h)

            act.dma_start(ident[:, :], identity).then_inc(ident_in, 16)
            for i, g in enumerate((ln_mix, ln_ffn)):
                act.dma_start(t_gain[32 * i:32 * (i + 1), :], g.rearrange("l (k e) -> (l k) e", e=P)).then_inc(gain_in, 16)
            for at, g in ((G_AQ, a_q_norm), (G_AK, a_k_norm), (G_BQ, b_q_norm[0]), (G_BK, b_k_norm[0]),
                          (G_SUB, a_subln.rearrange("l (k e) -> (l k) e", e=P))):
                act.dma_start(t_gain[at:at + g.shape[0], :], g).then_inc(gain_in, 16)
            act.dma_start(t_lam, a_lambda.partition_broadcast(P).rearrange("p l a e -> p (l a) e")).then_inc(lam_in, 16)
            act.dma_start(t_onehot[0:BUCKETS, :], onehot).then_inc(onehot_in, 16)
            act.dma_start(t_mask, masks[:, 0:1, :]).then_inc(mask_in, 16)
            act.dma_start(t_rel[0:BUCKETS, :], rel_bias).then_inc(rel_in, 16)
            for layer in range(2):
                act.dma_start(t_conv[0:2 * FB, 4 * layer:4 * layer + 3, :],
                              f_conv_w[layer].rearrange("t (j e) -> j t e", e=P)).then_inc(conv_in, 16)
                act.dma_start(t_conv[0:2 * FB, 4 * layer + 3, :],
                              f_conv_b[layer].rearrange("(j e) -> j e", e=P)).then_inc(conv_in, 16)
            act.wait_ge(x_in, 32)
            for q in range(4):
                squares(0, q)
            act.wait_ge(lam_prod, 1)
            nc.scalar.activation(lam_e, lam_s, ACT.Exp).then_inc(lam_exp, 1)
            split(0)
            split(1)
            act.wait_ge(gains_ready, 1)

            norm(0, G_MIX)
            a_head(A0, 0)
            with act.Fori(1, H) as h:
                a_head(A0 + A_HEAD, h, (h - 1) * A_HEAD)
            out_proj(AO0, 1, a_oT, a_oT_act, a_oT_dve, a_attend)
            ffn(0, 1)
            norm(2, G_MIX + KB)
            b_head(B0, 0)
            with act.Fori(1, H) as h:
                b_head(B0 + B_HEAD, h, (h - 1) * B_HEAD)
            out_proj(BO0, 3, b_oT, b_oT_act, b_oT_dve, b_attend)
            ffn(1, 3)

        @block.vector
        def _(dve):
            chain = Chain(dve, dve_chain)

            def split(c, more=0, width=W):
                if c >= END:
                    return
                slot = c % SLOTS
                dve.wait_ge(hi_ready, c + 1 + more)
                nc.vector.tensor_tensor(w_lo[:, slot, 0:width], w_raw[:, slot, 0:width], w_hi[:, slot, 0:width],
                                        ALU.subtract).then_inc(lo_ready, 1)

            def a_width(j):
                return W if j % A_HEAD < 4 else W // 2

            def rsqrt(dst, src, tmp, mean, ready):
                chain.settle()
                chain.step(nc.vector.tensor_scalar(src, src, mean, EPS, ALU.mult, ALU.add))
                chain.settle()
                chain.step(nc.vector.tensor_scalar(tmp.bitcast(I32), src.bitcast(I32), 1, None,
                                                   ALU.logical_shift_right))
                chain.settle()
                chain.step(nc.vector.tensor_scalar(dst.bitcast(I32), tmp.bitcast(I32), -1, MAGIC, ALU.mult, ALU.add))
                for i in range(NEWTON):
                    chain.settle()
                    chain.step(nc.vector.tensor_tensor(tmp, dst, dst, ALU.mult))
                    chain.settle()
                    chain.step(nc.vector.scalar_tensor_tensor(out=tmp, in0=tmp, scalar=-0.5, in1=src, op0=ALU.mult,
                                                              op1=ALU.mult))
                    chain.settle()
                    ins = nc.vector.scalar_tensor_tensor(out=dst, in0=tmp, scalar=1.5, in1=dst, op0=ALU.add,
                                                         op1=ALU.mult)
                    if i == NEWTON - 1 and ready is not None:
                        ins.then_inc(ready, 1)
                    else:
                        chain.step(ins)

            def norm(n, gain):
                dve.wait_ge(r_sq, 4 * (n + 1))
                chain.step(nc.vector.tensor_reduce(r_ss, ssp.rearrange("p (m q) -> p m q", m=M), AX.X, ALU.add))
                rsqrt(r_r, r_ss, r_t, 1.0 / D, r_rstd)
                dve.wait_ge(r_rstd, n + 1)
                for q in range(4):
                    nc.vector.tensor_scalar(y[:, 1, 512 * q:512 * (q + 1)], resid[:, 1, 512 * q:512 * (q + 1)],
                                            r_r[:, 1:2], None, ALU.mult).then_inc(y_dve, 1)
                for k in range(KB):
                    dve.wait_ge(xT_hi, KB * n + k // 2 * 2 + 2)
                    at = 256 * (k % 2)
                    nc.vector.scalar_tensor_tensor(
                        out=xT[:, k, 1, :], in0=psum[:, 4 + k // 2 % 4, at:at + 256],
                        scalar=gains[:, gain + k:gain + k + 1], in1=xT[:, k, 0, :], op0=ALU.mult,
                        op1=ALU.subtract).then_inc(xT_lo, 1)

            def add_quarter(q, banks):
                for m in range(M):
                    r = resid[:, m, 512 * q:512 * (q + 1)]
                    ins = nc.vector.tensor_tensor(r, psum[:, banks[m], :], r, ALU.add)
                ins.then_inc(r_add, 1)

            def a_take_qk(c, h, more=0):
                chunk_used(dve, c, more)
                at_least(dve, a_tqk, h)
                nc.vector.tensor_copy(a_qk[:, 1, :], psum[:, 1, :]).then_inc(a_qk_dve, 1)
                dve.wait_ge(a_sq_ready, h + 1)
                chain.step(nc.vector.tensor_reduce(n_ss[:, 0:8], a_sq.rearrange("p m (s e) -> p (m s) e", e=HD),
                                                   AX.X, ALU.add))
                rsqrt(n_r[:, 0:8], n_ss[:, 0:8], n_t[:, 0:8], 1.0 / HD, None)
                chain.settle()
                v = a_qk.rearrange("p m (s e) -> p (m s) e", e=HD)
                nc.vector.tensor_tensor(v, v, n_r[:, 0:8].unsqueeze(2).to_broadcast([P, 8, HD]),
                                        ALU.mult).then_inc(a_qkn, 1)

            def a_take_k(h):
                dve.wait_ge(a_tqk, h + 1)
                at_least(dve, a_scores, h)
                nc.vector.tensor_scalar(a_kT, psum[:, 5, :].rearrange("p (a b) -> p a b", a=2),
                                        gains[:, G_AK:G_AK + 1], None, ALU.mult).then_inc(a_kT_ready, 1)

            def a_take_v(c, h, more=0):
                chunk_used(dve, c, more)
                at_least(dve, a_pv, h)
                nc.vector.tensor_copy(a_v[:, 1, :], psum[:, 3, 0:VD]).then_inc(a_v_dve, 1)

            def a_softmax(h):
                dve.wait_ge(a_scores, h + 1)
                bias = a_bias[:, bass.ds(h, 1), :]
                lg1 = a_lg[:, 0:512].rearrange("p (a b) -> p a b", a=2)
                lg0 = a_lg[:, 512:768].rearrange("p (a b) -> p a b", a=2)
                nc.vector.scalar_tensor_tensor(
                    out=lg1, in0=psum[:, 6, :].rearrange("p (a b) -> p a b", a=2), scalar=SCALE,
                    in1=bias.to_broadcast([P, 2, SEQ]), op0=ALU.mult, op1=ALU.add)
                nc.vector.scalar_tensor_tensor(
                    out=lg0, in0=psum[:, 7, 0:256].rearrange("p (a b) -> p a b", a=2), scalar=SCALE,
                    in1=bias[:, :, P:SEQ].to_broadcast([P, 2, P]), op0=ALU.mult, op1=ALU.add).then_inc(a_lg_ready, 1)
                dve.wait_ge(a_lg_ready, h + 1)
                nc.vector.tensor_reduce(mx[:, 0:2], lg1, AX.X, ALU.max)
                chain.step(nc.vector.tensor_reduce(mx[:, 2:4], lg0, AX.X, ALU.max))
                chain.settle()
                nc.vector.tensor_scalar(nmx, mx, -1.0, None, ALU.mult).then_inc(a_nmx, 1)
                dve.wait_ge(a_probs, h + 1)
                chain.step(nc.vector.reciprocal(rden, den))
                chain.settle()
                for b, (at, n, col) in enumerate(((512, 128, 2), (0, 256, 0))):
                    nc.vector.tensor_scalar(rneg[:, b:b + 1], rden[:, col + 1:col + 2], nlam[:, 0:1], None, ALU.mult)
                    to = 0 if b == 0 else 128
                    chain.step(nc.vector.tensor_scalar(a_a[:, to:to + n], a_lg[:, at:at + n], rden[:, col:col + 1],
                                                       None, ALU.mult))
                chain.settle()
                for b, (at, n) in enumerate(((512, 128), (0, 256))):
                    to = 0 if b == 0 else 128
                    ins = nc.vector.scalar_tensor_tensor(
                        out=a_a[:, to:to + n], in0=a_lg[:, at + n:at + 2 * n], scalar=rneg[:, b:b + 1],
                        in1=a_a[:, to:to + n], op0=ALU.mult, op1=ALU.add)
                ins.then_inc(a_diff, 1)

            def a_attend(j, h):
                if j == 2:
                    dve.wait_ge(a_oss, h + 1)
                    rsqrt(o_r, o_ss, o_t, 1.0 / VD, a_orstd)
                if j == 3:
                    dve.wait_ge(a_to, h + 1)
                    nc.vector.tensor_scalar(a_oT[:, bass.ds(2 * h + 1, 1), :],
                                            psum[:, 7, 0:SEQ].rearrange("p (a b) -> p a b", a=1),
                                            sub_g[:, 1:2], None, ALU.mult).then_inc(a_oT_dve, 1)

            def a_head(c, h, more=0):
                for j in range(A_HEAD):
                    split(c + j + LEAD, more, a_width(j + LEAD))
                    if j == 3:
                        a_take_qk(c + j, h, more)
                    if not isinstance(h, int) or h > 0:
                        a_attend(j, h - 1)
                    if j == 6:
                        a_take_k(h)
                    if j == 7:
                        a_take_v(c + j, h, more)
                        a_softmax(h)

            splits = [0]

            def split_o(oT, hd):
                splits[0] += 1
                dve.wait_ge(xs_hi, splits[0])
                k = slice(2 * hd, 2 * hd + 2)
                nc.vector.tensor_tensor(xT[:, k, 1, :], oT[:, k, :], xT[:, k, 0, :], ALU.subtract).then_inc(xs_lo, 1)

            def out_proj(c, oT, attend):
                split_o(oT, 0)
                split_o(oT, 1)
                for j in range(OUT):
                    split(c + j + LEAD)
                    attend(j, H - 1)
                    if j < 5:
                        split_o(oT, j + 2)
                    if j == 6:
                        split_o(oT, H - 1)
                    if j in (7, 15):
                        half = j // 8
                        chunk_used(dve, c + j)
                        for q in range(2):
                            add_quarter(2 * half + q, (4 * half + 2 * q, 4 * half + 2 * q + 1))

            def taps(layer, tile, dst, init, t, tg, last):
                for b in range(4):
                    ch = bass.ds(t * 4 + (FB * tile + b), 1)
                    dve.wait_ge(init, 4 * tg + b + 1)
                    chain.step(nc.vector.scalar_tensor_tensor(
                        out=dst[:, b, :], in0=u[:, b, 1:SEQ + 1], scalar=conv[:, layer, 1, ch], in1=dst[:, b, :],
                        op0=ALU.mult, op1=ALU.add))
                chain.settle()
                for b in range(4):
                    ch = bass.ds(t * 4 + (FB * tile + b), 1)
                    ins = nc.vector.scalar_tensor_tensor(
                        out=dst[:, b, :], in0=u[:, b, 0:SEQ], scalar=conv[:, layer, 0, ch], in1=dst[:, b, :],
                        op0=ALU.mult, op1=ALU.add)
                last(ins)

            def up_pair(layer, c, t, tg, more=0):
                for j in range(UP_PAIR):
                    split(c + j + LEAD, more)
                    if j == 3 or j == 7:
                        tile = j // 4
                        chunk_used(dve, c + j, more)
                        acc = psum[:, 4 * tile:4 * tile + 4, :]
                        dve.wait_ge(val_low if tile else gate_low, tg + 1)
                        nc.vector.tensor_tensor(u[:, :, 2:SEQ + 2], acc[:, :, 0:SEQ], c_val if tile else c_gate,
                                                ALU.add).then_inc(val_read if tile else gate_read, 1)
                        dve.wait_ge(val_read if tile else gate_read, tg + 1)
                    if j == 3:
                        taps(layer, 0, c_gate, gate_init, t, tg, lambda ins: ins.then_inc(gate_taps, 1))
                    if j == 7:
                        taps(layer, 1, c_val, val_init, t, tg, chain.step)
                        chain.settle()
                        dve.wait_ge(silu_ready, tg + 1)
                        nc.vector.tensor_tensor(hT[:, bass.ds(t * 4, 4), :], c_gate, c_val,
                                                ALU.mult).then_inc(h_ready, 1)

            def split_h(layer, b, t=0):
                slot = 4 * b if b == 0 else 4 + 4 * ((b - 1) % 2)
                dve.wait_ge(xs_hi, splits[0] + b + 1 + 2 * t)
                nc.vector.tensor_tensor(xT[:, slot:slot + 4, 1, :], hT[:, bass.ds(4 * b + 8 * t, 4), :],
                                        xT[:, slot:slot + 4, 0, :], ALU.subtract).then_inc(xs_lo, 1)

            def down(layer, c):
                split_h(layer, 0)
                split_h(layer, 1)
                for j in range(4):
                    split(c + j + LEAD)
                with dve.Fori(0, 4) as t:
                    for j in range(8):
                        split(c + 4 + j + LEAD, t * 8)
                        if j == 1:
                            split_h(layer, 2, t)
                        if j == 5:
                            split_h(layer, 3, t)
                for j in range(8):
                    split(c + 36 + j + LEAD)
                    if j == 1:
                        split_h(layer, 10)
                splits[0] += DOWN // 4
                for q in range(4):
                    if q < 3:
                        dve.wait_ge(down_quarter, 3 * layer + q + 1)
                    else:
                        chunk_used(dve, c + DOWN - 1)
                    add_quarter(q, (2 * q, 2 * q + 1))

            def ffn(layer, n):
                norm(n, G_FFN + KB * layer)
                chain.step(nc.vector.memset(u[:, :, 0:2], 0.0))
                chain.settle()
                c = UP0[layer]
                up_pair(layer, c, 0, UP_PAIRS * layer)
                with dve.Fori(1, UP_PAIRS) as t, chain.loop(t - 1, UP_PAIRS - 1, 9):
                    up_pair(layer, c + UP_PAIR, t, t + UP_PAIRS * layer, (t - 1) * UP_PAIR)
                down(layer, DN0[layer])

            def b_take(c, g, h, more=0):
                chunk_used(dve, c, more)
                at_least(dve, b_tqk, h)
                at_least(dve, b_vheld, h)
                nc.vector.tensor_copy(b_raw[:, 2 * g + 1, :], psum[:, 2 * (g % 2) + 1, :]).then_inc(b_raw_dve, 1)

            def b_norm(h):
                dve.wait_ge(b_sq_ready, h + 1)
                chain.step(nc.vector.tensor_reduce(n_ss, b_sq.rearrange("p m (s e) -> p (m s) e", e=HD), AX.X, ALU.add))
                rsqrt(n_r, n_ss, n_t, 1.0 / HD, None)
                chain.settle()
                v = b_raw[:, :, 0:256].rearrange("p m (s e) -> p m s e", e=HD)
                r = n_r.rearrange("p (m s) -> p m s", s=2).unsqueeze(3).to_broadcast([P, G * M, 2, HD])
                nc.vector.tensor_tensor(v, v, r, ALU.mult).then_inc(b_qkn, 1)

            def b_attend(j, h):
                if j == 1:
                    dve.wait_ge(b_tqk, h + 1)
                    at_least(dve, b_scores, h)
                    for g in range(G):
                        at = SEQ * (g % 2)
                        ins = nc.vector.tensor_scalar(b_kT[:, g, :], psum[:, 6 + g // 2, at:at + SEQ],
                                                      gains[:, G_BK + g:G_BK + g + 1], None, ALU.mult)
                    ins.then_inc(b_kT_ready, 1)
                if j == 2:
                    dve.wait_ge(b_scores, h + 1)
                    dve.wait_ge(b_bias_ready, h + 1)
                    lg1 = b_lg[:, 0:768].rearrange("p (a b) -> p a b", a=3)
                    lg0 = b_lg[:, 768:1152].rearrange("p (a b) -> p a b", a=3)
                    for dst, src, bias in (
                            (lg1[:, 0:2, :], psum[:, 4, :].rearrange("p (a b) -> p a b", a=2), b_bias[:, 0:2, :]),
                            (lg1[:, 2:3, :], psum[:, 5, 0:256].rearrange("p (a b) -> p a b", a=1), b_bias[:, 2:3, :]),
                            (lg0, psum[:, 7, 0:384].rearrange("p (a b) -> p a b", a=3), b_bias[:, :, P:SEQ])):
                        ins = nc.vector.scalar_tensor_tensor(out=dst, in0=src, scalar=SCALE, in1=bias, op0=ALU.mult,
                                                             op1=ALU.add)
                    ins.then_inc(b_lg_ready, 1)
                    dve.wait_ge(b_lg_ready, h + 1)
                    nc.vector.tensor_reduce(mx[:, 1:2], b_lg[:, 0:768], AX.X, ALU.max)
                    chain.step(nc.vector.tensor_reduce(mx[:, 0:1], b_lg[:, 768:1152], AX.X, ALU.max))
                    chain.settle()
                    nc.vector.tensor_scalar(nmx[:, 0:2], mx[:, 0:2], -1.0, None, ALU.mult).then_inc(b_nmx, 1)
                    dve.wait_ge(b_probs, h + 1)
                    nc.vector.reciprocal(rden[:, 0:2], den[:, 0:2]).then_inc(b_rden, 1)
                if j == 4:
                    dve.wait_ge(b_tp, h + 1)
                    at_least(dve, b_pv, h)
                    nc.vector.tensor_copy(b_pT[:, 4:6, :], psum[:, 5, 0:256].rearrange("p (a b) -> p a b", a=2))
                    nc.vector.tensor_copy(b_pT[:, 6:9, :],
                                          psum[:, 6, 0:384].rearrange("p (a b) -> p a b", a=3)).then_inc(b_pT_dve, 1)
                if j == 6:
                    dve.wait_ge(b_to, h + 1)
                    nc.vector.tensor_copy(b_oT[:, bass.ds(2 * h + 1, 1), :],
                                          psum[:, 5, 0:SEQ].rearrange("p (a b) -> p a b", a=1)).then_inc(b_oT_dve, 1)

            def b_head(c, h, more=0):
                for j in range(B_HEAD):
                    split(c + j + LEAD, more)
                    if not isinstance(h, int) or h > 0:
                        b_attend(j, h - 1)
                    if j % 4 == 3:
                        b_take(c + j, j // 4, h, more)
                b_norm(h)

            dve.wait_ge(pe_setup, 1)
            nc.vector.tensor_copy(gains[:, :], psum[:, 0, 0:GAINS]).then_inc(gains_ready, 1)
            dve.wait_ge(lam_in, 16)
            for i in range(2):
                ins = nc.vector.tensor_tensor_reduce(t_prod[:, i, :], t_lam[:, 2 * i, :], t_lam[:, 2 * i + 1, :], 1.0, 0.0,
                                                     ALU.mult, ALU.add, lam_s[:, i:i + 1])
            ins.then_inc(lam_prod, 1)
            split(0)
            split(1)
            dve.wait_ge(gains_ready, 1)
            dve.wait_ge(pe_setup, 2)
            nc.vector.tensor_scalar(sub_g[:, :], gains[:, G_SUB:G_SUB + 2], 1.0 - LAM_INIT, None, ALU.mult)
            nc.vector.tensor_copy(t_rows[0:H, :], psum[0:H, 3, 0:ROW]).then_inc(bias_rows_made, 1)
            for layer in range(2):
                nc.vector.tensor_copy(conv[:, layer, :, :],
                                      psum[:, 1 + layer, 0:8 * FB].rearrange("p (a b) -> p a b", a=4))
            dve.wait_ge(lam_exp, 1)
            nc.vector.tensor_scalar(nlam[:, :], lam_e[:, 1:2], lam_e[:, 0:1], LAM_INIT, ALU.subtract,
                                    ALU.subtract).then_inc(consts_ready, 1)

            norm(0, G_MIX)
            dve.wait_ge(a_bias_ready, 1)
            dve.wait_ge(consts_ready, 1)
            a_head(A0, 0)
            with dve.Fori(1, H) as h, chain.loop(h - 1, H - 1, 1 + RSQRT_STEPS + 1 + 1 + 2 + RSQRT_STEPS - 1):
                a_head(A0 + A_HEAD, h, (h - 1) * A_HEAD)
            out_proj(AO0, a_oT, a_attend)
            ffn(0, 1)
            norm(2, G_MIX + KB)
            b_head(B0, 0)
            with dve.Fori(1, H) as h, chain.loop(h - 1, H - 1, 1 + RSQRT_STEPS + 1):
                b_head(B0 + B_HEAD, h, (h - 1) * B_HEAD)
            out_proj(BO0, b_oT, b_attend)
            ffn(1, 3)

        @block.tensor
        def _(pe):
            def part_of(ring, slot, at, n):
                return ring[:, slot, at:at + n]

            def transpose_y(n, ks):
                for k in ks:
                    if k % 4 == 0:
                        pe.wait_ge(y_act, 4 * n + k // 4 + 1)
                        pe.wait_ge(y_dve, 4 * n + k // 4 + 1)
                    if k >= 8 and k % 2 == 0:
                        pe.wait_ge(xT_lo, KB * n + k - 6)
                    for m in range(M):
                        at = 256 * (k % 2) + P * m
                        ins = pe.transpose(psum[:, 4 + k // 2 % 4, at:at + P], y[:, m, P * k:P * (k + 1)], ident[:, :])
                    if k % 2 == 1:
                        ins.then_inc(xT_ps, 1)

            def moving(c, more, blocks, n, outs, first, last):
                slot = c % SLOTS
                pe.wait_ge(lo_ready, c + 1 + more)
                for i, k in enumerate(blocks):
                    for t, banks in enumerate(outs):
                        at = (i * len(outs) + t) * n
                        hi, lo = part_of(w_hi, slot, at, n), part_of(w_lo, slot, at, n)
                        for m in range(M):
                            xh, xl = xT[:, k, 0, P * m:P * (m + 1)], xT[:, k, 1, P * m:P * (m + 1)]
                            o = psum[:, banks[m], 0:n]
                            pe.matmul(o, xh, hi, start=(first and i == 0), stop=False)
                            pe.matmul(o, xh, lo, start=False, stop=False)
                            ins = pe.matmul(o, xl, hi, start=False, stop=(last and i == len(blocks) - 1))
                ins.then_inc(used, 1)

            def a_transpose_qk(h):
                pe.wait_ge(a_qkn, h + 1)
                at_least(pe, a_aT_ready, h)
                at_least(pe, a_on, h)
                for s in range(2):
                    for i in range(2):
                        for m in range(M):
                            at = 256 * i + P * m
                            ins = pe.transpose(psum[:, 4 + s, at:at + P],
                                               a_qk[:, m, 256 * s + HD * i:256 * s + HD * (i + 1)], ident[:, :])
                ins.then_inc(a_tqk, 1)

            def a_score(h):
                pe.wait_ge(a_qT_ready, h + 1)
                pe.wait_ge(a_kT_ready, h + 1)
                at_least(pe, a_lg_ready, h)
                at_least(pe, a_oT_act, h)
                at_least(pe, a_oT_dve, h)
                for i in range(2):
                    pe.matmul(psum[:, 6, SEQ * i:SEQ * (i + 1)], a_qT[:, i, P:SEQ], a_kT[:, i, :], start=True, stop=True)
                for i in range(2):
                    ins = pe.matmul(psum[:, 7, P * i:P * (i + 1)], a_qT[:, i, 0:P], a_kT[:, i, 0:P], start=True, stop=True)
                ins.then_inc(a_scores, 1)

            def a_attend(j, h):
                if j == 1:
                    pe.wait_ge(a_diff, h + 1)
                    for i in range(3):
                        ins = pe.transpose(psum[:, 4, P * i:P * (i + 1)], a_a[:, P * i:P * (i + 1)], ident[:, :])
                    ins.then_inc(a_ta, 1)
                if j == 2:
                    pe.wait_ge(a_aT_ready, h + 1)
                    pe.wait_ge(a_v_act, h + 1)
                    pe.wait_ge(a_v_dve, h + 1)
                    pe.matmul(psum[:, 5, 0:VD], a_aT[:, 0, :], a_v[:, 0, :], start=True, stop=True)
                    pe.matmul(psum[:, 5, VD:2 * VD], a_aT[:, 1, :], a_v[:, 0, :], start=True, stop=False)
                    pe.matmul(psum[:, 5, VD:2 * VD], a_aT[:, 2, :], a_v[:, 1, :], start=False, stop=True).then_inc(a_pv, 1)
                if j == 3:
                    pe.wait_ge(a_on, h + 1)
                    for e in range(2):
                        for b in range(M):
                            ins = pe.transpose(psum[:, 6 + e, P * b:P * (b + 1)], a_o[:, b, P * e:P * (e + 1)], ident[:, :])
                    ins.then_inc(a_to, 1)

            def a_head(c, h, more=0):
                for j in range(A_HEAD):
                    ks = range(4 * (j % 4), 4 * (j % 4) + 4)
                    if j == 0:
                        at_least(pe, a_qk_act, h)
                        at_least(pe, a_qk_dve, h)
                    if j == 4:
                        at_least(pe, a_v_act, h)
                        at_least(pe, a_v_dve, h)
                    if isinstance(h, int) and j < 4:
                        pe.wait_ge(xT_lo, 4 * j + 4)
                    n = 512 if j < 4 else VD
                    moving(c + j, more, ks, n, [(0, 1) if j < 4 else (2, 3)], j % 4 == 0, j % 4 == 3)
                    if isinstance(h, int) and j == 0:
                        transpose_y(0, range(8, 16))
                    if not isinstance(h, int):
                        a_attend(j, h - 1)
                    if j == 6:
                        a_transpose_qk(h)
                    if j == 7:
                        a_score(h)

            splits = [0]

            def out_proj(c, raw_act, raw_dve, count, attend):
                pe.wait_ge(raw_act, count)
                pe.wait_ge(raw_dve, count)
                for j in range(OUT):
                    if j < 8:
                        splits[0] += 1
                        pe.wait_ge(xs_lo, splits[0])
                    b = 4 * (j // 8)
                    moving(c + j, 0, (2 * (j % 8), 2 * (j % 8) + 1), 512, [(b, b + 1), (b + 2, b + 3)],
                           j % 8 == 0, j % 8 == 7)
                    attend(j, H - 1)

            def up_chunk(c, more, j, bank):
                slot = c % SLOTS
                pe.wait_ge(lo_ready, c + 1 + more)
                for i in range(4):
                    k = 4 * j + i
                    for b in range(4):
                        at = 512 * i + P * b
                        both = psum[:, bank + b, :].rearrange("p (a b) -> p a b", a=2)

                        def high():
                            return pe.matmul(both, w_hi[:, slot, at:at + P], xT[:, k, :, :], start=(k == 0),
                                             stop=(k == KB - 1))

                        def low():
                            return pe.matmul(psum[:, bank + b, 0:SEQ], w_lo[:, slot, at:at + P], xT[:, k, 0, :],
                                             start=False, stop=False)

                        if k == 0:
                            high()
                            ins = low()
                        else:
                            low()
                            ins = high()
                ins.then_inc(used, 1)

            def up_pair(layer, n, c, tg, more=0):
                peeled = isinstance(tg, int)
                for j in range(UP_PAIR):
                    if j == 0:
                        at_least(pe, gate_read, tg)
                    if j == 4:
                        at_least(pe, val_read, tg)
                    if peeled and j < 4:
                        pe.wait_ge(xT_lo, KB * n + 4 * j + 4)
                    up_chunk(c + j, more, j % 4, 4 * (j // 4))
                    if peeled and j == 0:
                        transpose_y(n, range(8, 16))

            def down_chunk(c, more, slot_k, first=False, last=False):
                slot = c % SLOTS
                pe.wait_ge(lo_ready, c + 1 + more)
                for q in range(4):
                    hi, lo = part_of(w_hi, slot, 512 * q, 512), part_of(w_lo, slot, 512 * q, 512)
                    for m in range(M):
                        xh, xl = xT[:, slot_k, 0, P * m:P * (m + 1)], xT[:, slot_k, 1, P * m:P * (m + 1)]
                        o = psum[:, 2 * q + m, :]
                        pe.matmul(o, xh, hi, start=first, stop=False)
                        pe.matmul(o, xh, lo, start=False, stop=False)
                        ins = pe.matmul(o, xl, hi, start=False, stop=last)
                    if last and q < 3:
                        ins.then_inc(down_quarter, 1)
                ins.then_inc(used, 1)

            def down(layer, c):
                def block_ready(b, t=0):
                    pe.wait_ge(xs_lo, splits[0] + b + 1 + 2 * t)

                pe.wait_ge(val_read, UP_PAIRS * (layer + 1))
                block_ready(0)
                for j in range(4):
                    down_chunk(c + j, 0, j, first=(j == 0))
                with pe.Fori(0, 4) as t:
                    for j in range(8):
                        if j % 4 == 0:
                            block_ready(1 + j // 4, t)
                        down_chunk(c + 4 + j, t * 8, 4 + j)
                for j in range(8):
                    if j % 4 == 0:
                        block_ready(9 + j // 4)
                    down_chunk(c + 36 + j, 0, 4 + j, last=(j == 7))
                splits[0] += DOWN // 4

            def ffn(layer, n):
                transpose_y(n, range(8))
                c = UP0[layer]
                up_pair(layer, n, c, UP_PAIRS * layer)
                with pe.Fori(1, UP_PAIRS) as t:
                    up_pair(layer, n, c + UP_PAIR, t + UP_PAIRS * layer, (t - 1) * UP_PAIR)
                down(layer, DN0[layer])

            def b_attend(j, h):
                if j == 1:
                    pe.wait_ge(b_qkn, h + 1)
                    at_least(pe, b_on, h)
                    at_least(pe, b_oT_act, h)
                    at_least(pe, b_oT_dve, h)
                    for g in range(G):
                        for s in range(2):
                            for m in range(M):
                                at = SEQ * (g % 2) + P * m
                                ins = pe.transpose(psum[:, 4 + 2 * s + g // 2, at:at + P], b_raw[:, 2 * g + m, HD * s:HD * (s + 1)],
                                                   ident[:, :])
                    ins.then_inc(b_tqk, 1)
                if j == 2:
                    pe.wait_ge(b_qT_ready, h + 1)
                    pe.wait_ge(b_kT_ready, h + 1)
                    for g in range(G):
                        at = SEQ * (g % 2)
                        pe.matmul(psum[:, 4 + g // 2, at:at + SEQ], b_qT[:, g, P:SEQ], b_kT[:, g, :], start=True, stop=True)
                    for g in range(G):
                        ins = pe.matmul(psum[:, 7, P * g:P * (g + 1)], b_qT[:, g, 0:P], b_kT[:, g, 0:P],
                                        start=True, stop=True)
                    ins.then_inc(b_scores, 1)
                if j == 4:
                    pe.wait_ge(b_probs, h + 1)
                    for i in range(9):
                        bank, at = (4, P * i) if i < 4 else (5, P * (i - 4)) if i < 6 else (6, P * (i - 6))
                        ins = pe.transpose(psum[:, bank, at:at + P], b_lg[:, P * i:P * (i + 1)], ident[:, :])
                    ins.then_inc(b_tp, 1)
                if j == 5:
                    pe.wait_ge(b_pT_act, h + 1)
                    pe.wait_ge(b_pT_dve, h + 1)
                    pe.wait_ge(b_vheld, h + 1)
                    for g in range(G):
                        pe.matmul(psum[:, 7, 0:VD], b_pT[:, 6 + g, :], b_v[:, 2 * g, :], start=(g == 0), stop=(g == G - 1))
                    for i in range(2 * G):
                        ins = pe.matmul(psum[:, 7, VD:2 * VD], b_pT[:, i, :], b_v[:, i, :], start=(i == 0),
                                        stop=(i == 2 * G - 1))
                    ins.then_inc(b_pv, 1)
                if j == 6:
                    pe.wait_ge(b_on, h + 1)
                    for e in range(2):
                        for b in range(M):
                            ins = pe.transpose(psum[:, 6 - e, P * b:P * (b + 1)], b_o[:, b, P * e:P * (e + 1)], ident[:, :])
                    ins.then_inc(b_to, 1)

            def b_head(c, h, more=0):
                for j in range(B_HEAD):
                    g = j // 4
                    if j % 4 == 0:
                        free = 3 * h if g == 0 else 3 * h + g - 1
                        at_least(pe, b_raw_act, free)
                        at_least(pe, b_raw_dve, free)
                    if isinstance(h, int) and j < 4:
                        pe.wait_ge(xT_lo, KB * 2 + 4 * j + 4)
                    b = 2 * (g % 2)
                    moving(c + j, more, range(4 * (j % 4), 4 * (j % 4) + 4), 512, [(b, b + 1)], j % 4 == 0, j % 4 == 3)
                    if isinstance(h, int) and j == 0:
                        transpose_y(2, range(8, 16))
                    if not isinstance(h, int):
                        b_attend(j, h - 1)

            pe.wait_ge(ident_in, 16)
            pe.wait_ge(gain_in, 16 * 7)
            pe.transpose(psum[:, 0, 0:GAINS], t_gain[0:GAINS, :], ident[0:GAINS, 0:GAINS]).then_inc(pe_setup, 1)
            pe.wait_ge(conv_in, 16 * 4)
            for i in range(8):
                at = 2 * FB * (i % 4)
                pe.transpose(psum[:, 1 + i // 4, at:at + 2 * FB], t_conv[0:2 * FB, i, :], ident[0:2 * FB, 0:2 * FB])
            pe.wait_ge(onehot_in, 16)
            pe.wait_ge(rel_in, 16)
            pe.matmul(psum[0:H, 3, 0:ROW], t_rel[0:BUCKETS, :], t_onehot[0:BUCKETS, :], start=True,
                      stop=True).then_inc(pe_setup, 1)

            transpose_y(0, range(8))
            pe.wait_ge(consts_ready, 1)
            a_head(A0, 0)
            with pe.Fori(1, H) as h:
                a_head(A0 + A_HEAD, h, (h - 1) * A_HEAD)
            out_proj(AO0, a_v_act, a_v_dve, H, a_attend)
            ffn(0, 1)
            transpose_y(2, range(8))
            b_head(B0, 0)
            with pe.Fori(1, H) as h:
                b_head(B0 + B_HEAD, h, (h - 1) * B_HEAD)
            out_proj(BO0, b_raw_act, b_raw_dve, 3 * H, b_attend)
            ffn(1, 3)


INPUTS = ["x", "rel_bias", "ln_mix", "ln_ffn", "a_w_qkv", "a_q_norm", "a_k_norm", "a_lambda", "a_subln", "a_w_o",
          "b_w_qkv", "b_q_norm", "b_k_norm", "b_w_o", "f_w_up", "f_conv_w", "f_conv_b", "f_w_down"]


def kernel(**inputs):
    from concourse import bacc
    from concourse.bass_utils import run_bass_kernel_spmd

    nc = bacc.Bacc("TRN2", target_bir_lowering=False, num_devices=1)
    arrays = {name: np.ascontiguousarray(inputs[name]) for name in INPUTS}
    arrays.update(shape_tables())
    given = {n: nc.dram_tensor(f"in_{n}", a.shape, mybir.dt.from_np(a.dtype), kind="ExternalInput").ap()
             for n, a in arrays.items()}
    out = nc.dram_tensor("out", (1, SEQ, D), F32, kind="ExternalOutput").ap()
    trunk(nc, **given, out=out)
    run = run_bass_kernel_spmd(nc, [{f"in_{n}": a for n, a in arrays.items()}], core_ids=[0])
    return run.results[0]["out"]
```

```python
import math
from contextlib import ExitStack, contextmanager

import numpy as np

import concourse.bass as bass
from concourse import mybir

F32 = mybir.dt.float32
F32R = mybir.dt.float32r
I32 = mybir.dt.int32
ALU = mybir.AluOpType
ACT = mybir.ActivationFunctionType
AX = mybir.AxisListType

P = 128
SEQ, D = 256, 2048
M = SEQ // P
KB = D // P
H, HD, VD = 8, 128, 256
F = 5632
FB = F // P
EPS = 1e-6
SCALE = HD ** -0.5
BUCKETS, MAX_DISTANCE = 32, 2048
GROUPS = ((128, 1), (512, 4), (2048, 16))
G = len(GROUPS)
MASKED = -1e30
LAM_INIT = 0.8 - 0.6 * math.exp(-0.3 * 0)

W = 2048
SLOTS = 4
LEAD = 2

A_HEAD, B_HEAD, OUT, UP_PAIR, UP_PAIRS, DOWN = 8, 12, 16, 8, FB // 4, FB
A0 = 0
AO0 = A0 + H * A_HEAD
UP0 = (AO0 + OUT, 0)
DN0 = (UP0[0] + UP_PAIR * UP_PAIRS, 0)
B0 = DN0[0] + DOWN
BO0 = B0 + H * B_HEAD
UP0 = (UP0[0], BO0 + OUT)
DN0 = (DN0[0], UP0[1] + UP_PAIR * UP_PAIRS)
END = DN0[1] + DOWN
assert all(x % SLOTS == 0 for x in (AO0, *UP0, *DN0, B0, BO0, A_HEAD, B_HEAD, OUT, UP_PAIR, DOWN))



def loads_of(c):
    if A0 <= c < AO0:
        return 2 if (c - A0) % A_HEAD < 4 else 1
    if AO0 <= c < AO0 + LEAD:
        return 2
    if B0 <= c < BO0 + LEAD:
        return 3
    return 1


def landed(c):
    return 16 * sum(loads_of(i) for i in range(c % SLOTS, c + 1, SLOTS))


A_RATE, B_RATE, RATE = 16 * 3 // A_HEAD, 16 * 9 // B_HEAD, 16 // SLOTS

G_MIX, G_FFN, G_AQ, G_AK, G_BQ, G_BK, G_SUB = 0, 32, 64, 65, 66, 69, 72
GAINS = 74

ROW = 384
KINDS = 1 + G

A_STEPS = (0, 2, 4, 6)
B_STEPS = (2, 4, 6, 8, 9)
B_LAST_STEPS = (1, 2, 4, 5, 6)

MAGIC = 0x5F3759DF
NEWTON = 3
RSQRT_STEPS = 3 + 3 * NEWTON


def bucket_of(dist):
    exact = BUCKETS // 2
    n = max(dist, 0)
    if n < exact:
        return n
    return min(exact + int(math.log(n / exact) / math.log(MAX_DISTANCE / exact) * (BUCKETS - exact)), BUCKETS - 1)


def shape_tables():
    onehot = np.zeros((BUCKETS, ROW), np.float32)
    for i in range(ROW):
        onehot[bucket_of(SEQ - 1 - i), i] = 1.0
    dist = P + np.arange(P)[:, None] - np.arange(SEQ)[None, :]
    masks = np.zeros((P, KINDS, SEQ), np.float32)
    masks[:, 0][dist < 0] = MASKED
    for g, (_, dil) in enumerate(GROUPS):
        masks[:, 1 + g][(dist < 0) | (dist % dil != 0) | (dist > P * dil)] = MASKED
    return {"identity": np.eye(P, dtype=np.float32), "onehot": onehot, "masks": masks}


class Chain:

    def __init__(self, engine, sem):
        self.engine, self.sem, self.n, self.offset = engine, sem, 0, 0

    def step(self, instruction):
        instruction.then_inc(self.sem, 1)
        self.n += 1

    def settle(self):
        self.engine.wait_ge(self.sem, self.n + self.offset)

    @contextmanager
    def loop(self, turn, turns, steps):
        start, self.offset = self.n, turn * steps
        yield
        assert self.n - start == steps, (self.n - start, steps)
        self.n, self.offset = start + steps * turns, 0


def trunk(nc, x, rel_bias, ln_mix, ln_ffn, a_w_qkv, a_q_norm, a_k_norm, a_lambda, a_subln, a_w_o,
          b_w_qkv, b_q_norm, b_k_norm, b_w_o, f_w_up, f_conv_w, f_conv_b, f_w_down,
          identity, onehot, masks, out):
    bias_rows = nc.dram_tensor("bias_rows", (H, ROW), F32)
    bias_wide = nc.dram_tensor("bias_wide", (P, H, ROW), F32)

    with ExitStack() as ctx:
        def sb(name, shape, dt=F32):
            return ctx.enter_context(nc.sbuf_tensor(name, shape, dt))

        def sem(name):
            return ctx.enter_context(nc.semaphore(name))

        w_raw = sb("w_raw", [P, SLOTS, W])
        w_hi = sb("w_hi", [P, SLOTS, W], F32R)
        w_lo = sb("w_lo", [P, SLOTS, W], F32R)
        xT = sb("xT", [P, KB, 2, SEQ], F32R)
        resid = sb("resid", [P, M, D])
        ident = sb("ident", [P, P])
        gains = sb("gains", [P, GAINS])
        conv = sb("conv", [P, 2, 4, 2 * FB])
        sub_g = sb("sub_g", [P, 2])
        nlam = sb("nlam", [P, 1])
        small = sb("small", [P, 96])
        rstd_row = sb("rstd_row", [P, SEQ])
        psum = ctx.enter_context(nc.psum_tensor("psum", [P, 8, 512], F32))

        phase = sb("phase", [P, 14848])

        def part(at, *dims):
            n = int(np.prod(dims))
            assert at + n <= 14848
            v = phase[:, at:at + n]
            if len(dims) == 2:
                v = v.rearrange("p (a b) -> p a b", b=dims[1])
            if len(dims) == 3:
                v = v.rearrange("p (a b c) -> p a b c", b=dims[1], c=dims[2])
            return v

        squared = part(0, M, D)
        a_qk = part(0, M, 512)
        a_sq = part(1024, M, 512)
        a_qT = part(2048, 2, SEQ)
        a_kT = part(2560, 2, SEQ)
        a_v = part(3072, M, VD)
        a_lg = part(3584, 768)
        a_a = part(4352, 384)
        a_aT = part(4736, 3, P)
        a_o = part(5120, M, VD)
        a_oT = part(5632, KB, SEQ)
        a_bias = part(9728, H, SEQ)
        b_raw = part(0, G * M, 512)
        b_qT = part(3072, G, SEQ)
        b_kT = part(3840, G, SEQ)
        b_v = part(4608, G * M, VD)
        b_lg = part(6144, 1152)
        b_pT = part(7296, 9, P)
        b_o = part(8448, M, VD)
        b_sq = part(7296, G * M, 256)
        b_bias = part(8960, G, SEQ)
        b_mask = part(9728, G, SEQ)
        b_row = part(10496, SEQ)
        b_oT = part(10752, KB, SEQ)
        hT = part(0, FB, SEQ)
        u = part(11264, 4, SEQ + 2)
        c_gate = part(12296, 4, SEQ)
        c_val = part(13320, 4, SEQ)
        t_onehot = part(5632, ROW)
        t_mask = part(6016, 1, SEQ)
        t_rows = part(6272, ROW)
        t_rel = part(6656, H)
        t_lam = part(11776, 4, HD)
        t_gain = part(12288, P)
        t_conv = part(12416, 8, P)
        t_prod = part(13440, 2, HD)

        ssp = small[:, 0:8]
        r_ss, r_r, r_t = small[:, 8:10], small[:, 10:12], small[:, 12:14]
        n_ss, n_r, n_t = small[:, 16:28], small[:, 28:40], small[:, 40:52]
        mx, nmx = small[:, 52:56], small[:, 56:60]
        den, rden, rneg = small[:, 60:64], small[:, 64:68], small[:, 68:70]
        o_ss, o_r, o_t = small[:, 70:72], small[:, 72:74], small[:, 74:76]
        lam_s, lam_e = small[:, 76:78], small[:, 78:80]

        x_in = [sem(f"x_in{q}") for q in range(4)]
        ident_in, onehot_in, mask_in, rel_in, lam_in, gain_in, conv_in = (
            sem(n) for n in ("ident_in", "onehot_in", "mask_in", "rel_in", "lam_in", "gain_in", "conv_in"))
        pe_setup, bias_rows_made, bias_rows_out, bias_wide_out, a_row_in, a_bias_ready, b_mask_in, gains_ready, lam_prod, lam_exp, lam_ready, consts_ready = (
            sem(n) for n in ("pe_setup", "bias_rows_made", "bias_rows_out", "bias_wide_out", "a_row_in",
                             "a_bias_ready", "b_mask_in", "gains_ready", "lam_prod",
                             "lam_exp", "lam_ready", "consts_ready"))
        w_in = [sem(f"w_in{s}") for s in range(SLOTS)]
        hi_ready, lo_ready, used = sem("w_hi_ready"), sem("w_lo_ready"), sem("w_used")
        act_chain, dve_chain = sem("act_chain"), sem("dve_chain")
        r_add, r_sq, r_rstd, rstd_ps, rstd_row_ready = (sem(n) for n in (
            "r_add", "r_sq", "r_rstd", "rstd_ps", "rstd_row_ready"))
        xT_ps, xT_hi, xT_lo = sem("xT_ps"), sem("xT_hi"), sem("xT_lo")
        xs_hi, xs_lo = sem("xs_hi"), sem("xs_lo")
        (a_qk_act, a_qk_dve, a_sq_ready, a_qkn, a_tqk, a_qT_ready, a_kT_ready, a_v_act, a_v_dve, a_scores,
         a_lg_ready, a_nmx, a_probs, a_diff, a_ta, a_aT_ready, a_pv, a_oss, a_orstd, a_on, a_to, a_oT_act,
         a_oT_dve) = (sem(n) for n in (
             "a_qk_act", "a_qk_dve", "a_sq_ready", "a_qkn", "a_tqk", "a_qT_ready", "a_kT_ready", "a_v_act", "a_v_dve",
             "a_scores", "a_lg_ready", "a_nmx", "a_probs", "a_diff", "a_ta", "a_aT_ready", "a_pv", "a_oss", "a_orstd",
             "a_on", "a_to", "a_oT_act", "a_oT_dve"))
        (b_raw_act, b_raw_dve, b_sq_ready, b_qkn, b_vheld, b_tqk, b_qT_ready, b_kT_ready, b_scores, b_row_in, b_bias_ready,
         b_lg_ready, b_nmx, b_probs, b_rden, b_tp, b_pT_act, b_pT_dve, b_pv, b_on, b_to, b_oT_act,
         b_oT_dve) = (sem(n) for n in (
             "b_raw_act", "b_raw_dve", "b_sq_ready", "b_qkn", "b_vheld", "b_tqk", "b_qT_ready", "b_kT_ready",
             "b_scores", "b_row_in", "b_bias_ready", "b_lg_ready", "b_nmx", "b_probs", "b_rden", "b_tp", "b_pT_act", "b_pT_dve",
             "b_pv", "b_on", "b_to", "b_oT_act", "b_oT_dve"))
        gate_low, val_low, gate_read, val_read, gate_scaled, val_scaled, gate_init, val_init, gate_taps, silu_ready, h_ready = (sem(n) for n in (
            "gate_low", "val_low", "gate_read", "val_read", "gate_scaled", "val_scaled", "gate_init", "val_init", "gate_taps", "silu_ready", "h_ready"))
        down_quarter = sem("down_quarter")
        out_done = sem("out_done")

        block = ctx.enter_context(nc.Block())

        def at_least(engine, s, value):
            if not (isinstance(value, int) and value <= 0):
                engine.wait_ge(s, value)

        def xT_bank(n, k):
            return 4 + k // 2 % 4 if n == 0 else k // 2

        def chunk_used(engine, c, more=0):
            engine.wait_ge(used, c + 1 + more)

        @block.sync
        def _(sp):
            def load_x(q):
                cols = slice(512 * q, 512 * (q + 1))
                sp.dma_start(resid[:, :, cols], x[0].rearrange("(m p) d -> p m d", p=P)[:, :, cols]).then_inc(x_in[q], 16)

            def free_slot(c, more=0):
                at_least(sp, lo_ready, c - SLOTS + 1 + more)

            def load_a_head(c, h, more=0):
                for j in range(A_HEAD):
                    if isinstance(h, int) and j < 4:
                        load_x(j)
                    free_slot(c + j, more)
                    rows = a_w_qkv[0, 512 * (j % 4):512 * (j % 4 + 1), :]
                    slot = (c + j) % SLOTS
                    if j < 4:
                        tile = w_raw[:, slot, :].rearrange("p (k c) -> p k c", k=4)
                        for s in range(2):
                            src = rows[:, 2048 * s:2048 * (s + 1)].rearrange("(k p) c -> p k c", p=P)
                            sp.dma_start(tile[:, :, 256 * s:256 * (s + 1)],
                                         src[:, :, bass.ts(h, 256)]).then_inc(w_in[slot], 16)
                    else:
                        src = rows[:, 4096:6144].rearrange("(k p) c -> p k c", p=P)[:, :, bass.ts(h, 256)]
                        dst = w_raw[:, slot, 0:1024].rearrange("p (k c) -> p k c", k=4)
                        sp.dma_start(dst, src).then_inc(w_in[slot], 16)

            def load_b_head(c, h, more=0):
                for j in range(B_HEAD):
                    g, slot = j // 4, (c + j) % SLOTS
                    free_slot(c + j, more)
                    rows = b_w_qkv[0, 512 * (j % 4):512 * (j % 4 + 1), 4096 * g:4096 * (g + 1)]
                    dst = w_raw[:, slot, :].rearrange("p (k c) -> p k c", k=4)
                    for at, n, first in ((0, HD, 0), (HD, HD, 1024), (256, VD, 2048)):
                        src = rows[:, first:first + H * n].rearrange("(k p) c -> p k c", p=P)[:, :, bass.ts(h, n)]
                        sp.dma_start(dst[:, :, at:at + n], src).then_inc(w_in[slot], 16)

            def load_out(c, w):
                for j in range(OUT):
                    slot = (c + j) % SLOTS
                    free_slot(c + j)
                    src = w[0, 256 * (j % 8):256 * (j % 8 + 1), 1024 * (j // 8):1024 * (j // 8 + 1)].rearrange(
                        "(k p) c -> p k c", p=P)
                    dst = w_raw[:, slot, :].rearrange("p (k c) -> p k c", k=2)
                    n = loads_of(c + j)
                    pieces = [(slice(0, 1), slice(0, 1024)), (slice(1, 2), slice(0, 512)), (slice(1, 2), slice(512, 1024))]
                    if n == 2:
                        pieces[1:] = [(slice(1, 2), slice(0, 1024))]
                    if n == 1:
                        pieces = [(slice(0, 2), slice(0, 1024))]
                    for k, cols in pieces:
                        sp.dma_start(dst[:, k, cols], src[:, k, cols]).then_inc(w_in[slot], 16)

            def load_ffn(layer):
                c = UP0[layer]
                with sp.Fori(0, UP_PAIRS) as t:
                    for j in range(UP_PAIR):
                        slot = (c + j) % SLOTS
                        free_slot(c + j, t * UP_PAIR)
                        half = F * (j // 4)
                        src = f_w_up[layer, 512 * (j % 4):512 * (j % 4 + 1), half:half + F].rearrange(
                            "(k p) c -> p k c", p=P)[:, :, bass.ts(t, 512)]
                        dst = w_raw[:, slot, :].rearrange("p (k c) -> p k c", k=4)
                        sp.dma_start(dst, src).then_inc(w_in[slot], 16)
                c = DN0[layer]
                rows = f_w_down[layer].rearrange("(t j p) c -> p t j c", p=P, j=4)
                with sp.Fori(0, DOWN // 4) as t:
                    for j in range(4):
                        slot = (c + j) % SLOTS
                        free_slot(c + j, t * 4)
                        sp.dma_start(w_raw[:, slot, :], rows[:, bass.ts(t, 1), j, :].rearrange("p t c -> p (t c)")).then_inc(w_in[slot], 16)

            load_a_head(A0, 0)
            with sp.Fori(1, H) as h:
                load_a_head(A0 + A_HEAD, h, (h - 1) * A_HEAD)
            load_out(AO0, a_w_o)
            load_ffn(0)
            with sp.Fori(0, H) as h:
                load_b_head(B0, h, h * B_HEAD)
            load_out(BO0, b_w_o)
            load_ffn(1)
            for q in range(4):
                sp.wait_ge(r_add, 12 + q + 1)
                sp.dma_start(out[0].rearrange("(m p) d -> p m d", p=P)[:, :, 512 * q:512 * (q + 1)],
                             resid[:, :, 512 * q:512 * (q + 1)]).then_inc(out_done, 16)
            sp.wait_ge(out_done, 64)

        @block.gpsimd
        def _(pool):
            def tables(first, heads):
                return bass.AP(bias_wide, first * ROW + P - 1, [[H * ROW - 1, P], [ROW, heads], [1, SEQ]])

            pool.wait_ge(bias_rows_made, 1)
            pool.dma_start(bias_rows[:, :], t_rows[0:H, :]).then_inc(bias_rows_out, 16)
            pool.wait_ge(bias_rows_out, 16)
            pool.dma_start(bias_wide[:, :, :], bass.AP(bias_rows, 0, [[0, P], [ROW, H], [1, ROW]])).then_inc(bias_wide_out, 16)
            pool.wait_ge(bias_wide_out, 16)
            pool.dma_start(a_bias, tables(0, H)).then_inc(a_row_in, 16)
            pool.wait_ge(a_row_in, 16)
            pool.wait_ge(mask_in, 16)
            nc.gpsimd.tensor_tensor(a_bias, a_bias, t_mask.to_broadcast([P, H, SEQ]), ALU.add).then_inc(a_bias_ready, 1)

            pool.wait_ge(r_add, 8)
            pool.dma_start(b_mask, masks[:, 1:KINDS, :]).then_inc(b_mask_in, 16)
            pool.wait_ge(b_mask_in, 16)

            def b_head(h):
                if h > 0:
                    pool.wait_ge(b_bias_ready, h)
                pool.dma_start(b_row, tables(h, 1)).then_inc(b_row_in, 16)
                pool.wait_ge(b_row_in, 16 * h + 16)
                if h > 0:
                    pool.wait_ge(b_lg_ready, h)
                nc.gpsimd.tensor_tensor(b_bias, b_row.unsqueeze(1).to_broadcast([P, G, SEQ]), b_mask,
                                        ALU.add).then_inc(b_bias_ready, 1)
                pool.wait_ge(b_raw_act, 3 * h + 3)
                pool.wait_ge(b_raw_dve, 3 * h + 3)
                if h > 0:
                    pool.wait_ge(b_pv, h)
                nc.gpsimd.tensor_copy(b_v, b_raw[:, :, 256:512]).then_inc(b_vheld, 1)

            for h in range(H):
                b_head(h)

        @block.scalar
        def _(act):
            chain = Chain(act, act_chain)

            def split(c, more=0, width=W, rate=RATE):
                if c >= END:
                    return
                slot = c % SLOTS
                act.wait_ge(w_in[slot], landed(c) + more * rate)
                at_least(act, used, c - SLOTS + 1 + more)
                nc.scalar.activation(w_hi[:, slot, 0:width], w_raw[:, slot, 0:width], ACT.Copy).then_inc(hi_ready, 1)

            def a_width(j):
                return W if j % A_HEAD < 4 else W // 2

            def squares(n, q):
                for m in range(M):
                    ins = nc.scalar.activation(squared[:, m, 512 * q:512 * (q + 1)], resid[:, m, 512 * q:512 * (q + 1)],
                                               ACT.Square, accum_out=ssp[:, 4 * m + q:4 * m + q + 1])
                ins.then_inc(r_sq, 1)

            def take_xT(n, gain, q):
                for k in range(4 * q, 4 * q + 4):
                    act.wait_ge(xT_ps, KB // 2 * n + k // 2 + 1)
                    at = 256 * (k % 2)
                    nc.scalar.activation(xT[:, k, 0, :], psum[:, xT_bank(n, k), at:at + 256], ACT.Copy,
                                         scale=gains[:, gain + k:gain + k + 1]).then_inc(xT_hi, 1)

            def begin(n, gain, j, before):
                if j == 0:
                    take_xT(n, gain, 2)
                    take_xT(n, gain, 3)
                    for q in range(before, 4):
                        if n > 0:
                            act.wait_ge(r_add, 4 * (n - 1) + q + 1)
                        squares(n, q)

            def a_take_qk(c, h, more=0):
                chunk_used(act, c, more)
                at_least(act, a_tqk, h)
                if isinstance(h, int):
                    act.wait_ge(r_rstd, 1)
                nc.scalar.activation(a_qk[:, 0, :], psum[:, 0, :], ACT.Copy, scale=r_r[:, 0:1]).then_inc(a_qk_act, 1)
                act.wait_ge(a_qk_act, h + 1)
                act.wait_ge(a_qk_dve, h + 1)
                nc.scalar.activation(a_sq, a_qk, ACT.Square).then_inc(a_sq_ready, 1)

            def a_take_q(h):
                act.wait_ge(a_tqk, h + 1)
                at_least(act, a_scores, h)
                nc.scalar.activation(a_qT, psum[:, 4, :].rearrange("p (a b) -> p a b", a=2), ACT.Copy,
                                     scale=gains[:, G_AQ:G_AQ + 1]).then_inc(a_qT_ready, 1)

            def a_take_v(c, h, more=0):
                chunk_used(act, c, more)
                at_least(act, a_pv, h)
                nc.scalar.activation(a_v[:, 0, :], psum[:, 2, 0:VD], ACT.Copy, scale=r_r[:, 0:1]).then_inc(a_v_act, 1)

            def a_exp(h):
                act.wait_ge(a_nmx, h + 1)
                for i in range(2):
                    nc.scalar.activation(a_lg[:, 256 * i:256 * (i + 1)], a_lg[:, 256 * i:256 * (i + 1)], ACT.Exp,
                                         bias=nmx[:, i:i + 1], accum_out=den[:, i:i + 1])
                for i in range(2):
                    at = 512 + 128 * i
                    ins = nc.scalar.activation(a_lg[:, at:at + 128], a_lg[:, at:at + 128], ACT.Exp,
                                               bias=nmx[:, 2 + i:3 + i], accum_out=den[:, 2 + i:3 + i])
                ins.then_inc(a_probs, 1)

            def a_take_aT(h):
                act.wait_ge(a_ta, h + 1)
                at_least(act, a_pv, h)
                nc.scalar.activation(a_aT, psum[:, 4, 0:384].rearrange("p (a b) -> p a b", a=3),
                                     ACT.Copy).then_inc(a_aT_ready, 1)

            def a_norm_o(h):
                act.wait_ge(a_pv, h + 1)
                at_least(act, a_to, h)
                for b in range(M):
                    ins = nc.scalar.activation(a_o[:, b, :], psum[:, 5, VD * b:VD * (b + 1)], ACT.Square,
                                               accum_out=o_ss[:, b:b + 1])
                ins.then_inc(a_oss, 1)
                act.wait_ge(a_orstd, h + 1)
                for b in range(M):
                    ins = nc.scalar.activation(a_o[:, b, :], psum[:, 5, VD * b:VD * (b + 1)], ACT.Copy,
                                               scale=o_r[:, b:b + 1])
                ins.then_inc(a_on, 1)

            def a_take_oT(h):
                act.wait_ge(a_to, h + 1)
                nc.scalar.activation(a_oT[:, bass.ds(2 * h, 1), :], psum[:, 6, 0:SEQ].rearrange("p (a b) -> p a b", a=1),
                                     ACT.Copy, scale=sub_g[:, 0:1]).then_inc(a_oT_act, 1)

            def a_attend(j, h, steps):
                if j == steps[0]:
                    a_exp(h)
                if j == steps[1]:
                    a_take_aT(h)
                if j == steps[2]:
                    a_norm_o(h)
                if j == steps[3]:
                    a_take_oT(h)

            def a_head(c, h, more=0):
                for j in range(A_HEAD):
                    split(c + j + LEAD, more, a_width(j + LEAD), A_RATE)
                    if isinstance(h, int):
                        begin(0, G_MIX, j, 0)
                        if j == 2:
                            act.wait_ge(lam_prod, 1)
                            nc.scalar.activation(lam_e, lam_s, ACT.Exp).then_inc(lam_exp, 1)
                    if j == 3:
                        a_take_qk(c + j, h, more)
                    if not isinstance(h, int):
                        a_attend(j, h - 1, A_STEPS)
                    if j == 7:
                        a_take_v(c + j, h, more)
                        a_take_q(h)

            def split_o(oT, oT_act, oT_dve, hd):
                act.wait_ge(oT_act, hd + 1)
                act.wait_ge(oT_dve, hd + 1)
                nc.scalar.activation(xT[:, 2 * hd:2 * hd + 2, 0, :], oT[:, 2 * hd:2 * hd + 2, :],
                                     ACT.Copy).then_inc(xs_hi, 1)

            def out_proj(c, n, gain, oT, oT_act, oT_dve, attend, steps):
                chunk_used(act, c - 1)
                split_o(oT, oT_act, oT_dve, 0)
                split_o(oT, oT_act, oT_dve, 1)
                for j in range(OUT):
                    split(c + j + LEAD)
                    attend(j, H - 1, steps)
                    if j < 5:
                        split_o(oT, oT_act, oT_dve, j + 2)
                    if j == 6:
                        split_o(oT, oT_act, oT_dve, H - 1)
                    if j == 7:
                        for q in range(2):
                            act.wait_ge(r_add, 4 * (n - 1) + q + 1)
                            squares(n, q)
                    if j in (9, 11):
                        chunk_used(act, c + j)
                        take_xT(n, gain, (j - 9) // 2)

            def conv_init(c, more, layer, tile, low, ready, init, dst, t, tg):
                chunk_used(act, c, more)
                at_least(act, h_ready, tg)
                nc.scalar.activation(dst, psum[:, 4 * tile:4 * tile + 4, SEQ:2 * SEQ], ACT.Copy).then_inc(low, 1)
                act.wait_ge(ready, tg + 1)
                for b in range(4):
                    ch = bass.ds(t * 4 + (FB * tile + b), 1)
                    nc.scalar.activation(dst[:, b, :], u[:, b, 2:SEQ + 2], ACT.Identity,
                                         scale=conv[:, layer, 2, ch], bias=conv[:, layer, 3, ch]).then_inc(init, 1)

            def up_pair(layer, n, c, t, tg, more=0):
                for j in range(UP_PAIR):
                    split(c + j + LEAD, more)
                    if isinstance(t, int) and t == 0:
                        begin(n, G_FFN + KB * layer, j, 2)
                        if j == 2:
                            act.wait_ge(rstd_ps, layer + 1)
                            nc.scalar.activation(rstd_row[:, :], psum[:, 4, 0:SEQ], ACT.Copy).then_inc(rstd_row_ready, 1)
                    if isinstance(t, int) and t == UP_PAIRS - 1 and j in (5, 6):
                        chunk_used(act, c + j - 1)
                        split_h(layer, j - 5)
                    if j == 3:
                        conv_init(c + j, more, layer, 0, gate_low, gate_scaled, gate_init, c_gate, t, tg)
                    if j == 4:
                        act.wait_ge(gate_taps, tg + 1)
                        nc.scalar.activation(c_gate, c_gate, ACT.Silu).then_inc(silu_ready, 1)
                    if j == 7:
                        conv_init(c + j, more, layer, 1, val_low, val_scaled, val_init, c_val, t, tg)

            def split_h(layer, b, t=0):
                slot = 4 * b if b == 0 else 4 + 4 * ((b - 1) % 2)
                nc.scalar.activation(xT[:, slot:slot + 4, 0, :], hT[:, bass.ds(4 * b + 8 * t, 4), :],
                                     ACT.Copy).then_inc(xs_hi, 1)

            def down(layer, c, n):
                for j in range(4):
                    split(c + j + LEAD)
                act.wait_ge(h_ready, UP_PAIRS * (layer + 1))
                with act.Fori(0, 4) as t:
                    for j in range(8):
                        split(c + 4 + j + LEAD, t * 8)
                        if j == 1:
                            chunk_used(act, c + 3, t * 8)
                            split_h(layer, 2, t)
                        if j == 5:
                            chunk_used(act, c + 7, t * 8)
                            split_h(layer, 3, t)
                for j in range(8):
                    split(c + 36 + j + LEAD)
                    if j == 1:
                        chunk_used(act, c + 35)
                        split_h(layer, 10)
                if layer == 0:
                    take_xT(n, G_MIX + KB, 0)
                    take_xT(n, G_MIX + KB, 1)

            def ffn(layer, n):
                c = UP0[layer]
                up_pair(layer, n, c, 0, UP_PAIRS * layer)
                with act.Fori(1, UP_PAIRS - 1) as t:
                    up_pair(layer, n, c + UP_PAIR, t, t + UP_PAIRS * layer, (t - 1) * UP_PAIR)
                up_pair(layer, n, c + UP_PAIR * (UP_PAIRS - 1), UP_PAIRS - 1, UP_PAIRS * (layer + 1) - 1)
                down(layer, DN0[layer], n + 1)

            def b_take(c, g, h, more=0):
                chunk_used(act, c, more)
                at_least(act, b_tqk, h)
                at_least(act, b_vheld, h)
                if isinstance(h, int) and g == 0:
                    act.wait_ge(r_rstd, 3)
                nc.scalar.activation(b_raw[:, 2 * g, :], psum[:, 2 * (g % 2), :], ACT.Copy,
                                     scale=r_r[:, 0:1]).then_inc(b_raw_act, 1)

            def b_squares(h):
                act.wait_ge(b_raw_act, 3 * h + 3)
                act.wait_ge(b_raw_dve, 3 * h + 3)
                nc.scalar.activation(b_sq, b_raw[:, :, 0:256], ACT.Square).then_inc(b_sq_ready, 1)

            def b_attend(j, h, steps):
                if j == 0:
                    b_squares(h)
                if j == steps[0]:
                    act.wait_ge(b_tqk, h + 1)
                    at_least(act, b_scores, h)
                    for g in range(G):
                        at = SEQ * (g % 2)
                        ins = nc.scalar.activation(b_qT[:, g, :], psum[:, 4 + g // 2, at:at + SEQ], ACT.Copy,
                                                   scale=gains[:, G_BQ + g:G_BQ + g + 1])
                    ins.then_inc(b_qT_ready, 1)
                if j == steps[1]:
                    act.wait_ge(b_nmx, h + 1)
                    nc.scalar.activation(b_lg[:, 0:768], b_lg[:, 0:768], ACT.Exp, bias=nmx[:, 1:2],
                                         accum_out=den[:, 1:2])
                    nc.scalar.activation(b_lg[:, 768:1152], b_lg[:, 768:1152], ACT.Exp, bias=nmx[:, 0:1],
                                         accum_out=den[:, 0:1]).then_inc(b_probs, 1)
                if j == steps[2]:
                    act.wait_ge(b_tp, h + 1)
                    at_least(act, b_pv, h)
                    nc.scalar.activation(b_pT[:, 0:4, :], psum[:, 4, :].rearrange("p (a b) -> p a b", a=4),
                                         ACT.Copy).then_inc(b_pT_act, 1)
                if j == steps[3]:
                    act.wait_ge(b_pv, h + 1)
                    act.wait_ge(b_rden, h + 1)
                    at_least(act, b_to, h)
                    for b in range(M):
                        ins = nc.scalar.activation(b_o[:, b, :], psum[:, 7, VD * b:VD * (b + 1)], ACT.Copy,
                                                   scale=rden[:, b:b + 1])
                    ins.then_inc(b_on, 1)
                if j == steps[4]:
                    act.wait_ge(b_to, h + 1)
                    nc.scalar.activation(b_oT[:, bass.ds(2 * h, 1), :],
                                         psum[:, 6, 0:SEQ].rearrange("p (a b) -> p a b", a=1),
                                         ACT.Copy).then_inc(b_oT_act, 1)

            def b_head(c, h, more=0):
                for j in range(B_HEAD):
                    split(c + j + LEAD, more, W, B_RATE)
                    if isinstance(h, int):
                        begin(2, G_MIX + KB, j, 0)
                    else:
                        b_attend(j, h - 1, B_STEPS)
                    if j % 4 == 3:
                        b_take(c + j, j // 4, h, more)

            act.dma_start(ident[:, :], identity).then_inc(ident_in, 16)
            for i, g in enumerate((ln_mix, ln_ffn)):
                act.dma_start(t_gain[32 * i:32 * (i + 1), :], g.rearrange("l (k e) -> (l k) e", e=P)).then_inc(gain_in, 16)
            for at, g in ((G_AQ, a_q_norm), (G_AK, a_k_norm), (G_BQ, b_q_norm[0]), (G_BK, b_k_norm[0]),
                          (G_SUB, a_subln.rearrange("l (k e) -> (l k) e", e=P))):
                act.dma_start(t_gain[at:at + g.shape[0], :], g).then_inc(gain_in, 16)
            act.dma_start(t_lam, a_lambda.partition_broadcast(P).rearrange("p l a e -> p (l a) e")).then_inc(lam_in, 16)
            act.dma_start(t_onehot[0:BUCKETS, :], onehot).then_inc(onehot_in, 16)
            act.dma_start(t_mask, masks[:, 0:1, :]).then_inc(mask_in, 16)
            act.dma_start(t_rel[0:BUCKETS, :], rel_bias).then_inc(rel_in, 16)
            for layer in range(2):
                act.dma_start(t_conv[0:2 * FB, 4 * layer:4 * layer + 3, :],
                              f_conv_w[layer].rearrange("t (j e) -> j t e", e=P)).then_inc(conv_in, 16)
                act.dma_start(t_conv[0:2 * FB, 4 * layer + 3, :],
                              f_conv_b[layer].rearrange("(j e) -> j e", e=P)).then_inc(conv_in, 16)
            split(0)
            act.wait_ge(gains_ready, 1)
            take_xT(0, G_MIX, 0)
            split(1)
            take_xT(0, G_MIX, 1)

            a_head(A0, 0)
            with act.Fori(1, H) as h:
                a_head(A0 + A_HEAD, h, (h - 1) * A_HEAD)
            out_proj(AO0, 1, G_FFN, a_oT, a_oT_act, a_oT_dve, a_attend, A_STEPS)
            ffn(0, 1)
            b_head(B0, 0)
            with act.Fori(1, H) as h:
                b_head(B0 + B_HEAD, h, (h - 1) * B_HEAD)
            out_proj(BO0, 3, G_FFN + KB, b_oT, b_oT_act, b_oT_dve, b_attend, B_LAST_STEPS)
            ffn(1, 3)

        @block.vector
        def _(dve):
            chain = Chain(dve, dve_chain)

            def split(c, more=0, width=W):
                if c >= END:
                    return
                slot = c % SLOTS
                dve.wait_ge(hi_ready, c + 1 + more)
                nc.vector.tensor_tensor(w_lo[:, slot, 0:width], w_raw[:, slot, 0:width], w_hi[:, slot, 0:width],
                                        ALU.subtract).then_inc(lo_ready, 1)

            def a_width(j):
                return W if j % A_HEAD < 4 else W // 2

            def rsqrt(dst, src, tmp, mean, ready):
                chain.settle()
                chain.step(nc.vector.tensor_scalar(src, src, mean, EPS, ALU.mult, ALU.add))
                chain.settle()
                chain.step(nc.vector.tensor_scalar(tmp.bitcast(I32), src.bitcast(I32), 1, None,
                                                   ALU.logical_shift_right))
                chain.settle()
                chain.step(nc.vector.tensor_scalar(dst.bitcast(I32), tmp.bitcast(I32), -1, MAGIC, ALU.mult, ALU.add))
                for i in range(NEWTON):
                    chain.settle()
                    chain.step(nc.vector.tensor_tensor(tmp, dst, dst, ALU.mult))
                    chain.settle()
                    chain.step(nc.vector.scalar_tensor_tensor(out=tmp, in0=tmp, scalar=-0.5, in1=src, op0=ALU.mult,
                                                              op1=ALU.mult))
                    chain.settle()
                    ins = nc.vector.scalar_tensor_tensor(out=dst, in0=tmp, scalar=1.5, in1=dst, op0=ALU.add,
                                                         op1=ALU.mult)
                    if i == NEWTON - 1 and ready is not None:
                        ins.then_inc(ready, 1)
                    else:
                        chain.step(ins)

            def rstd(n):
                dve.wait_ge(r_sq, 4 * (n + 1))
                chain.step(nc.vector.tensor_reduce(r_ss, ssp.rearrange("p (m q) -> p m q", m=M), AX.X, ALU.add))
                rsqrt(r_r, r_ss, r_t, 1.0 / D, r_rstd)
                dve.wait_ge(r_rstd, n + 1)

            def take_xT(n, gain, q):
                for k in range(4 * q, 4 * q + 4):
                    dve.wait_ge(xT_hi, KB * n + k // 2 * 2 + 2)
                    at = 256 * (k % 2)
                    nc.vector.scalar_tensor_tensor(
                        out=xT[:, k, 1, :], in0=psum[:, xT_bank(n, k), at:at + 256],
                        scalar=gains[:, gain + k:gain + k + 1], in1=xT[:, k, 0, :], op0=ALU.mult,
                        op1=ALU.subtract).then_inc(xT_lo, 1)

            def begin(n, gain, j):
                if j == 0:
                    take_xT(n, gain, 2)
                    take_xT(n, gain, 3)
                if j == 1:
                    rstd(n)

            def add_quarter(q, banks):
                for m in range(M):
                    r = resid[:, m, 512 * q:512 * (q + 1)]
                    ins = nc.vector.tensor_tensor(r, psum[:, banks[m], :], r, ALU.add)
                ins.then_inc(r_add, 1)

            def a_take_qk(c, h, more=0):
                chunk_used(dve, c, more)
                at_least(dve, a_tqk, h)
                nc.vector.tensor_scalar(a_qk[:, 1, :], psum[:, 1, :], r_r[:, 1:2], None, ALU.mult).then_inc(a_qk_dve, 1)
                dve.wait_ge(a_sq_ready, h + 1)
                chain.step(nc.vector.tensor_reduce(n_ss[:, 0:8], a_sq.rearrange("p m (s e) -> p (m s) e", e=HD),
                                                   AX.X, ALU.add))
                rsqrt(n_r[:, 0:8], n_ss[:, 0:8], n_t[:, 0:8], 1.0 / HD, None)
                chain.settle()
                v = a_qk.rearrange("p m (s e) -> p (m s) e", e=HD)
                nc.vector.tensor_tensor(v, v, n_r[:, 0:8].unsqueeze(2).to_broadcast([P, 8, HD]),
                                        ALU.mult).then_inc(a_qkn, 1)

            def a_take_k(h):
                dve.wait_ge(a_tqk, h + 1)
                at_least(dve, a_scores, h)
                nc.vector.tensor_scalar(a_kT, psum[:, 5, :].rearrange("p (a b) -> p a b", a=2),
                                        gains[:, G_AK:G_AK + 1], None, ALU.mult).then_inc(a_kT_ready, 1)

            def a_take_v(c, h, more=0):
                chunk_used(dve, c, more)
                at_least(dve, a_pv, h)
                nc.vector.tensor_scalar(a_v[:, 1, :], psum[:, 3, 0:VD], r_r[:, 1:2], None, ALU.mult).then_inc(a_v_dve, 1)

            def a_softmax(h):
                dve.wait_ge(a_scores, h + 1)
                bias = a_bias[:, bass.ds(h, 1), :]
                lg1 = a_lg[:, 0:512].rearrange("p (a b) -> p a b", a=2)
                lg0 = a_lg[:, 512:768].rearrange("p (a b) -> p a b", a=2)
                nc.vector.scalar_tensor_tensor(
                    out=lg1, in0=psum[:, 6, :].rearrange("p (a b) -> p a b", a=2), scalar=SCALE,
                    in1=bias.to_broadcast([P, 2, SEQ]), op0=ALU.mult, op1=ALU.add)
                nc.vector.scalar_tensor_tensor(
                    out=lg0, in0=psum[:, 7, 0:256].rearrange("p (a b) -> p a b", a=2), scalar=SCALE,
                    in1=bias[:, :, P:SEQ].to_broadcast([P, 2, P]), op0=ALU.mult, op1=ALU.add).then_inc(a_lg_ready, 1)
                dve.wait_ge(a_lg_ready, h + 1)
                nc.vector.tensor_reduce(mx[:, 0:2], lg1, AX.X, ALU.max)
                chain.step(nc.vector.tensor_reduce(mx[:, 2:4], lg0, AX.X, ALU.max))
                chain.settle()
                nc.vector.tensor_scalar(nmx, mx, -1.0, None, ALU.mult).then_inc(a_nmx, 1)
                dve.wait_ge(a_probs, h + 1)
                chain.step(nc.vector.reciprocal(rden, den))
                chain.settle()
                for b, (at, n, col) in enumerate(((512, 128, 2), (0, 256, 0))):
                    nc.vector.tensor_scalar(rneg[:, b:b + 1], rden[:, col + 1:col + 2], nlam[:, 0:1], None, ALU.mult)
                    to = 0 if b == 0 else 128
                    chain.step(nc.vector.tensor_scalar(a_a[:, to:to + n], a_lg[:, at:at + n], rden[:, col:col + 1],
                                                       None, ALU.mult))
                chain.settle()
                for b, (at, n) in enumerate(((512, 128), (0, 256))):
                    to = 0 if b == 0 else 128
                    ins = nc.vector.scalar_tensor_tensor(
                        out=a_a[:, to:to + n], in0=a_lg[:, at + n:at + 2 * n], scalar=rneg[:, b:b + 1],
                        in1=a_a[:, to:to + n], op0=ALU.mult, op1=ALU.add)
                ins.then_inc(a_diff, 1)

            def a_attend(j, h, steps):
                if j == steps[0]:
                    a_softmax(h)
                if j == steps[2]:
                    dve.wait_ge(a_oss, h + 1)
                    rsqrt(o_r, o_ss, o_t, 1.0 / VD, a_orstd)
                if j == steps[3]:
                    dve.wait_ge(a_to, h + 1)
                    nc.vector.tensor_scalar(a_oT[:, bass.ds(2 * h + 1, 1), :],
                                            psum[:, 7, 0:SEQ].rearrange("p (a b) -> p a b", a=1),
                                            sub_g[:, 1:2], None, ALU.mult).then_inc(a_oT_dve, 1)

            def a_head(c, h, more=0):
                for j in range(A_HEAD):
                    split(c + j + LEAD, more, a_width(j + LEAD))
                    if isinstance(h, int):
                        begin(0, G_MIX, j)
                        if j == 2:
                            setup_rest()
                        if j == 7:
                            dve.wait_ge(a_bias_ready, 1)
                    if j == 3:
                        a_take_qk(c + j, h, more)
                    if not isinstance(h, int):
                        a_attend(j, h - 1, A_STEPS)
                    if j == 7:
                        a_take_v(c + j, h, more)
                        a_take_k(h)

            splits = [0]

            def split_o(oT, hd):
                splits[0] += 1
                dve.wait_ge(xs_hi, splits[0])
                k = slice(2 * hd, 2 * hd + 2)
                nc.vector.tensor_tensor(xT[:, k, 1, :], oT[:, k, :], xT[:, k, 0, :], ALU.subtract).then_inc(xs_lo, 1)

            def out_proj(c, n, gain, oT, attend, steps):
                split_o(oT, 0)
                split_o(oT, 1)
                for j in range(OUT):
                    split(c + j + LEAD)
                    attend(j, H - 1, steps)
                    if j < 5:
                        split_o(oT, j + 2)
                    if j == 6:
                        split_o(oT, H - 1)
                    if j in (7, 15):
                        half = j // 8
                        chunk_used(dve, c + j)
                        for q in range(2):
                            add_quarter(2 * half + q, (4 * half + 2 * q, 4 * half + 2 * q + 1))
                    if j in (9, 11):
                        take_xT(n, gain, (j - 9) // 2)

            def taps(layer, tile, dst, init, t, tg, last):
                for b in range(4):
                    ch = bass.ds(t * 4 + (FB * tile + b), 1)
                    dve.wait_ge(init, 4 * tg + b + 1)
                    chain.step(nc.vector.scalar_tensor_tensor(
                        out=dst[:, b, :], in0=u[:, b, 1:SEQ + 1], scalar=conv[:, layer, 1, ch], in1=dst[:, b, :],
                        op0=ALU.mult, op1=ALU.add))
                chain.settle()
                for b in range(4):
                    ch = bass.ds(t * 4 + (FB * tile + b), 1)
                    ins = nc.vector.scalar_tensor_tensor(
                        out=dst[:, b, :], in0=u[:, b, 0:SEQ], scalar=conv[:, layer, 0, ch], in1=dst[:, b, :],
                        op0=ALU.mult, op1=ALU.add)
                last(ins)

            def up_pair(layer, n, c, t, tg, more=0):
                for j in range(UP_PAIR):
                    split(c + j + LEAD, more)
                    if isinstance(t, int) and t == 0:
                        begin(n, G_FFN + KB * layer, j)
                    if isinstance(t, int) and t == UP_PAIRS - 1 and j in (5, 6):
                        split_h(layer, j - 5)
                    if j == 3 or j == 7:
                        tile = j // 4
                        chunk_used(dve, c + j, more)
                        acc = psum[:, 4 * tile:4 * tile + 4, :]
                        dve.wait_ge(val_low if tile else gate_low, tg + 1)
                        read, scaled = (val_read, val_scaled) if tile else (gate_read, gate_scaled)
                        inner = u[:, :, 2:SEQ + 2]
                        nc.vector.tensor_tensor(inner, acc[:, :, 0:SEQ], c_val if tile else c_gate,
                                                ALU.add).then_inc(read, 1)
                        dve.wait_ge(read, tg + 1)
                        if isinstance(t, int) and t == 0 and tile == 0:
                            dve.wait_ge(rstd_row_ready, layer + 1)
                        nc.vector.tensor_tensor(inner, inner, rstd_row[:, :].unsqueeze(1).to_broadcast([P, 4, SEQ]),
                                                ALU.mult).then_inc(scaled, 1)
                        dve.wait_ge(scaled, tg + 1)
                    if j == 3:
                        taps(layer, 0, c_gate, gate_init, t, tg, lambda ins: ins.then_inc(gate_taps, 1))
                    if j == 7:
                        taps(layer, 1, c_val, val_init, t, tg, chain.step)
                        chain.settle()
                        dve.wait_ge(silu_ready, tg + 1)
                        nc.vector.tensor_tensor(hT[:, bass.ds(t * 4, 4), :], c_gate, c_val,
                                                ALU.mult).then_inc(h_ready, 1)

            def split_h(layer, b, t=0):
                slot = 4 * b if b == 0 else 4 + 4 * ((b - 1) % 2)
                dve.wait_ge(xs_hi, splits[0] + b + 1 + 2 * t)
                nc.vector.tensor_tensor(xT[:, slot:slot + 4, 1, :], hT[:, bass.ds(4 * b + 8 * t, 4), :],
                                        xT[:, slot:slot + 4, 0, :], ALU.subtract).then_inc(xs_lo, 1)

            def down(layer, c):
                for j in range(4):
                    split(c + j + LEAD)
                with dve.Fori(0, 4) as t:
                    for j in range(8):
                        split(c + 4 + j + LEAD, t * 8)
                        if j == 1:
                            split_h(layer, 2, t)
                        if j == 5:
                            split_h(layer, 3, t)
                for j in range(8):
                    split(c + 36 + j + LEAD)
                    if j == 1:
                        split_h(layer, 10)
                splits[0] += DOWN // 4
                for q in range(4):
                    if q < 3:
                        dve.wait_ge(down_quarter, 3 * layer + q + 1)
                    else:
                        chunk_used(dve, c + DOWN - 1)
                    add_quarter(q, (2 * q, 2 * q + 1))
                    if q == 2 and layer == 0:
                        take_xT(2, G_MIX + KB, 0)
                if layer == 0:
                    take_xT(2, G_MIX + KB, 1)

            def ffn(layer, n):
                chain.step(nc.vector.memset(u[:, :, 0:2], 0.0))
                chain.settle()
                c = UP0[layer]
                up_pair(layer, n, c, 0, UP_PAIRS * layer)
                with dve.Fori(1, UP_PAIRS - 1) as t, chain.loop(t - 1, UP_PAIRS - 2, 9):
                    up_pair(layer, n, c + UP_PAIR, t, t + UP_PAIRS * layer, (t - 1) * UP_PAIR)
                up_pair(layer, n, c + UP_PAIR * (UP_PAIRS - 1), UP_PAIRS - 1, UP_PAIRS * (layer + 1) - 1)
                down(layer, DN0[layer])

            def b_take(c, g, h, more=0):
                chunk_used(dve, c, more)
                at_least(dve, b_tqk, h)
                at_least(dve, b_vheld, h)
                nc.vector.tensor_scalar(b_raw[:, 2 * g + 1, :], psum[:, 2 * (g % 2) + 1, :], r_r[:, 1:2], None,
                                        ALU.mult).then_inc(b_raw_dve, 1)

            def b_norm(h):
                dve.wait_ge(b_sq_ready, h + 1)
                chain.step(nc.vector.tensor_reduce(n_ss, b_sq.rearrange("p m (s e) -> p (m s) e", e=HD), AX.X, ALU.add))
                rsqrt(n_r, n_ss, n_t, 1.0 / HD, None)
                chain.settle()
                v = b_raw[:, :, 0:256].rearrange("p m (s e) -> p m s e", e=HD)
                r = n_r.rearrange("p (m s) -> p m s", s=2).unsqueeze(3).to_broadcast([P, G * M, 2, HD])
                nc.vector.tensor_tensor(v, v, r, ALU.mult).then_inc(b_qkn, 1)

            def b_attend(j, h, steps):
                if j == 0:
                    b_norm(h)
                if j == steps[0]:
                    dve.wait_ge(b_tqk, h + 1)
                    at_least(dve, b_scores, h)
                    for g in range(G):
                        at = SEQ * (g % 2)
                        ins = nc.vector.tensor_scalar(b_kT[:, g, :], psum[:, 6 + g // 2, at:at + SEQ],
                                                      gains[:, G_BK + g:G_BK + g + 1], None, ALU.mult)
                    ins.then_inc(b_kT_ready, 1)
                if j == steps[1]:
                    dve.wait_ge(b_scores, h + 1)
                    dve.wait_ge(b_bias_ready, h + 1)
                    lg1 = b_lg[:, 0:768].rearrange("p (a b) -> p a b", a=3)
                    lg0 = b_lg[:, 768:1152].rearrange("p (a b) -> p a b", a=3)
                    for dst, src, bias in (
                            (lg1[:, 0:2, :], psum[:, 4, :].rearrange("p (a b) -> p a b", a=2), b_bias[:, 0:2, :]),
                            (lg1[:, 2:3, :], psum[:, 5, 0:256].rearrange("p (a b) -> p a b", a=1), b_bias[:, 2:3, :]),
                            (lg0, psum[:, 7, 0:384].rearrange("p (a b) -> p a b", a=3), b_bias[:, :, P:SEQ])):
                        ins = nc.vector.scalar_tensor_tensor(out=dst, in0=src, scalar=SCALE, in1=bias, op0=ALU.mult,
                                                             op1=ALU.add)
                    ins.then_inc(b_lg_ready, 1)
                    dve.wait_ge(b_lg_ready, h + 1)
                    nc.vector.tensor_reduce(mx[:, 1:2], b_lg[:, 0:768], AX.X, ALU.max)
                    chain.step(nc.vector.tensor_reduce(mx[:, 0:1], b_lg[:, 768:1152], AX.X, ALU.max))
                    chain.settle()
                    nc.vector.tensor_scalar(nmx[:, 0:2], mx[:, 0:2], -1.0, None, ALU.mult).then_inc(b_nmx, 1)
                    dve.wait_ge(b_probs, h + 1)
                    nc.vector.reciprocal(rden[:, 0:2], den[:, 0:2]).then_inc(b_rden, 1)
                if j == steps[2]:
                    dve.wait_ge(b_tp, h + 1)
                    at_least(dve, b_pv, h)
                    nc.vector.tensor_copy(b_pT[:, 4:6, :], psum[:, 5, 0:256].rearrange("p (a b) -> p a b", a=2))
                    nc.vector.tensor_copy(b_pT[:, 6:9, :],
                                          psum[:, 6, 0:384].rearrange("p (a b) -> p a b", a=3)).then_inc(b_pT_dve, 1)
                if j == steps[4]:
                    dve.wait_ge(b_to, h + 1)
                    nc.vector.tensor_copy(b_oT[:, bass.ds(2 * h + 1, 1), :],
                                          psum[:, 5, 0:SEQ].rearrange("p (a b) -> p a b", a=1)).then_inc(b_oT_dve, 1)

            def b_head(c, h, more=0):
                for j in range(B_HEAD):
                    split(c + j + LEAD, more)
                    if isinstance(h, int):
                        begin(2, G_MIX + KB, j)
                    else:
                        b_attend(j, h - 1, B_STEPS)
                    if j % 4 == 3:
                        b_take(c + j, j // 4, h, more)

            def setup_rest():
                dve.wait_ge(lam_in, 16)
                for i in range(2):
                    ins = nc.vector.tensor_tensor_reduce(t_prod[:, i, :], t_lam[:, 2 * i, :], t_lam[:, 2 * i + 1, :], 1.0,
                                                         0.0, ALU.mult, ALU.add, lam_s[:, i:i + 1])
                ins.then_inc(lam_prod, 1)
                nc.vector.tensor_scalar(sub_g[:, :], gains[:, G_SUB:G_SUB + 2], 1.0 - LAM_INIT, None, ALU.mult)
                dve.wait_ge(lam_exp, 1)
                nc.vector.tensor_scalar(nlam[:, :], lam_e[:, 1:2], lam_e[:, 0:1], LAM_INIT, ALU.subtract,
                                        ALU.subtract).then_inc(lam_ready, 1)
                dve.wait_ge(lam_ready, 1)

            dve.wait_ge(pe_setup, 1)
            nc.vector.tensor_copy(gains[:, :], psum[:, 0, 0:GAINS]).then_inc(gains_ready, 1)
            dve.wait_ge(gains_ready, 1)
            split(0)
            take_xT(0, G_MIX, 0)
            split(1)
            take_xT(0, G_MIX, 1)
            dve.wait_ge(pe_setup, 2)
            nc.vector.tensor_copy(t_rows[0:H, :], psum[0:H, 3, 0:ROW]).then_inc(bias_rows_made, 1)
            for layer in range(2):
                ins = nc.vector.tensor_copy(conv[:, layer, :, :],
                                            psum[:, 1 + layer, 0:8 * FB].rearrange("p (a b) -> p a b", a=4))
            ins.then_inc(consts_ready, 1)

            a_head(A0, 0)
            with dve.Fori(1, H) as h, chain.loop(h - 1, H - 1, 1 + RSQRT_STEPS + 1 + 1 + 2 + RSQRT_STEPS - 1):
                a_head(A0 + A_HEAD, h, (h - 1) * A_HEAD)
            out_proj(AO0, 1, G_FFN, a_oT, a_attend, A_STEPS)
            ffn(0, 1)
            b_head(B0, 0)
            with dve.Fori(1, H) as h, chain.loop(h - 1, H - 1, 1 + RSQRT_STEPS + 1):
                b_head(B0 + B_HEAD, h, (h - 1) * B_HEAD)
            out_proj(BO0, 3, G_FFN + KB, b_oT, b_attend, B_LAST_STEPS)
            ffn(1, 3)

        @block.tensor
        def _(pe):
            def part_of(ring, slot, at, n):
                return ring[:, slot, at:at + n]

            def transpose_resid(n, q):
                if n == 0:
                    pe.wait_ge(x_in[q], 16)
                    if q == 2:
                        pe.wait_ge(xT_lo, 8)
                else:
                    pe.wait_ge(r_add, 4 * (n - 1) + q + 1)
                for k in range(4 * q, 4 * q + 4):
                    for m in range(M):
                        at = 256 * (k % 2) + P * m
                        ins = pe.transpose(psum[:, xT_bank(n, k), at:at + P], resid[:, m, P * k:P * (k + 1)], ident[:, :])
                    if k % 2 == 1:
                        ins.then_inc(xT_ps, 1)

            def begin(n, j):
                if j == 0:
                    transpose_resid(n, 2)
                    transpose_resid(n, 3)

            def moving(c, more, blocks, n, outs, first, last):
                slot = c % SLOTS
                pe.wait_ge(lo_ready, c + 1 + more)
                for i, k in enumerate(blocks):
                    for t, banks in enumerate(outs):
                        at = (i * len(outs) + t) * n
                        hi, lo = part_of(w_hi, slot, at, n), part_of(w_lo, slot, at, n)
                        for m in range(M):
                            xh, xl = xT[:, k, 0, P * m:P * (m + 1)], xT[:, k, 1, P * m:P * (m + 1)]
                            o = psum[:, banks[m], 0:n]
                            pe.matmul(o, xh, hi, start=(first and i == 0), stop=False)
                            pe.matmul(o, xh, lo, start=False, stop=False)
                            ins = pe.matmul(o, xl, hi, start=False, stop=(last and i == len(blocks) - 1))
                ins.then_inc(used, 1)

            def a_transpose_qk(h):
                pe.wait_ge(a_qkn, h + 1)
                at_least(pe, a_aT_ready, h)
                at_least(pe, a_on, h)
                for s in range(2):
                    for i in range(2):
                        for m in range(M):
                            at = 256 * i + P * m
                            ins = pe.transpose(psum[:, 4 + s, at:at + P],
                                               a_qk[:, m, 256 * s + HD * i:256 * s + HD * (i + 1)], ident[:, :])
                ins.then_inc(a_tqk, 1)

            def a_score(h):
                pe.wait_ge(a_qT_ready, h + 1)
                pe.wait_ge(a_kT_ready, h + 1)
                at_least(pe, a_lg_ready, h)
                at_least(pe, a_oT_act, h)
                at_least(pe, a_oT_dve, h)
                for i in range(2):
                    pe.matmul(psum[:, 6, SEQ * i:SEQ * (i + 1)], a_qT[:, i, P:SEQ], a_kT[:, i, :], start=True, stop=True)
                for i in range(2):
                    ins = pe.matmul(psum[:, 7, P * i:P * (i + 1)], a_qT[:, i, 0:P], a_kT[:, i, 0:P], start=True, stop=True)
                ins.then_inc(a_scores, 1)

            def a_attend(j, h, steps):
                if j == steps[0]:
                    a_score(h)
                if j == steps[1]:
                    pe.wait_ge(a_diff, h + 1)
                    for i in range(3):
                        ins = pe.transpose(psum[:, 4, P * i:P * (i + 1)], a_a[:, P * i:P * (i + 1)], ident[:, :])
                    ins.then_inc(a_ta, 1)
                if j == steps[2]:
                    pe.wait_ge(a_aT_ready, h + 1)
                    pe.wait_ge(a_v_act, h + 1)
                    pe.wait_ge(a_v_dve, h + 1)
                    pe.matmul(psum[:, 5, 0:VD], a_aT[:, 0, :], a_v[:, 0, :], start=True, stop=True)
                    pe.matmul(psum[:, 5, VD:2 * VD], a_aT[:, 1, :], a_v[:, 0, :], start=True, stop=False)
                    pe.matmul(psum[:, 5, VD:2 * VD], a_aT[:, 2, :], a_v[:, 1, :], start=False, stop=True).then_inc(a_pv, 1)
                if j == steps[3]:
                    pe.wait_ge(a_on, h + 1)
                    for e in range(2):
                        for b in range(M):
                            ins = pe.transpose(psum[:, 6 + e, P * b:P * (b + 1)], a_o[:, b, P * e:P * (e + 1)], ident[:, :])
                    ins.then_inc(a_to, 1)

            def a_head(c, h, more=0):
                for j in range(A_HEAD):
                    ks = range(4 * (j % 4), 4 * (j % 4) + 4)
                    if j == 0:
                        at_least(pe, a_qk_act, h)
                        at_least(pe, a_qk_dve, h)
                    if j == 4:
                        at_least(pe, a_v_act, h)
                        at_least(pe, a_v_dve, h)
                    if isinstance(h, int) and j < 4:
                        pe.wait_ge(xT_lo, 4 * j + 4)
                    n = 512 if j < 4 else VD
                    moving(c + j, more, ks, n, [(0, 1) if j < 4 else (2, 3)], j % 4 == 0, j % 4 == 3)
                    if isinstance(h, int):
                        begin(0, j)
                    else:
                        a_attend(j, h - 1, A_STEPS)
                    if j == 7:
                        a_transpose_qk(h)

            splits = [0]

            def out_proj(c, n, raw_act, raw_dve, count, attend, steps):
                pe.wait_ge(raw_act, count)
                pe.wait_ge(raw_dve, count)
                for j in range(OUT):
                    if j < 8:
                        splits[0] += 1
                        pe.wait_ge(xs_lo, splits[0])
                    b = 4 * (j // 8)
                    moving(c + j, 0, (2 * (j % 8), 2 * (j % 8) + 1), 512, [(b, b + 1), (b + 2, b + 3)],
                           j % 8 == 0, j % 8 == 7)
                    attend(j, H - 1, steps)
                    if j in (8, 9):
                        transpose_resid(n, j - 8)

            def up_chunk(c, more, j, bank):
                slot = c % SLOTS
                pe.wait_ge(lo_ready, c + 1 + more)
                for i in range(4):
                    k = 4 * j + i
                    for b in range(4):
                        at = 512 * i + P * b
                        both = psum[:, bank + b, :].rearrange("p (a b) -> p a b", a=2)

                        def high():
                            return pe.matmul(both, w_hi[:, slot, at:at + P], xT[:, k, :, :], start=(k == 0),
                                             stop=(k == KB - 1))

                        def low():
                            return pe.matmul(psum[:, bank + b, 0:SEQ], w_lo[:, slot, at:at + P], xT[:, k, 0, :],
                                             start=False, stop=False)

                        if k == 0:
                            high()
                            ins = low()
                        else:
                            low()
                            ins = high()
                ins.then_inc(used, 1)

            def up_pair(layer, n, c, tg, more=0):
                first = isinstance(tg, int) and tg % UP_PAIRS == 0
                for j in range(UP_PAIR):
                    if j == 0:
                        at_least(pe, gate_read, tg)
                    if j == 4:
                        at_least(pe, val_read, tg)
                        if first:
                            pe.wait_ge(rstd_row_ready, n // 2 + 1)
                    if first and j < 4:
                        pe.wait_ge(xT_lo, KB * n + 4 * j + 4)
                    up_chunk(c + j, more, j % 4, 4 * (j // 4))
                    if first:
                        begin(n, j)
                    if first and j == 2:
                        pe.wait_ge(r_rstd, n + 1)
                        pe.wait_ge(xT_lo, KB * (n + 1))
                        for m in range(M):
                            ins = pe.matmul(psum[:, 4, P * m:P * (m + 1)], r_r[:, m:m + 1].to_broadcast([P, P]),
                                            ident[:, :], start=True, stop=True)
                        ins.then_inc(rstd_ps, 1)

            def down_chunk(layer, c, more, slot_k, first=False, last=False):
                slot = c % SLOTS
                pe.wait_ge(lo_ready, c + 1 + more)
                for q in range(4):
                    if first and q == 0:
                        pe.wait_ge(gate_read, UP_PAIRS * (layer + 1))
                    if first and q == 2:
                        pe.wait_ge(val_read, UP_PAIRS * (layer + 1))
                    hi, lo = part_of(w_hi, slot, 512 * q, 512), part_of(w_lo, slot, 512 * q, 512)
                    for m in range(M):
                        xh, xl = xT[:, slot_k, 0, P * m:P * (m + 1)], xT[:, slot_k, 1, P * m:P * (m + 1)]
                        o = psum[:, 2 * q + m, :]
                        pe.matmul(o, xh, hi, start=first, stop=False)
                        pe.matmul(o, xh, lo, start=False, stop=False)
                        ins = pe.matmul(o, xl, hi, start=False, stop=last)
                    if last and q < 3:
                        ins.then_inc(down_quarter, 1)
                ins.then_inc(used, 1)

            def down(layer, c):
                def block_ready(b, t=0):
                    pe.wait_ge(xs_lo, splits[0] + b + 1 + 2 * t)

                block_ready(0)
                for j in range(4):
                    down_chunk(layer, c + j, 0, j, first=(j == 0))
                with pe.Fori(0, 4) as t:
                    for j in range(8):
                        if j % 4 == 0:
                            block_ready(1 + j // 4, t)
                        down_chunk(layer, c + 4 + j, t * 8, 4 + j)
                for j in range(8):
                    if j % 4 == 0:
                        block_ready(9 + j // 4)
                    down_chunk(layer, c + 36 + j, 0, 4 + j, last=(j == 7))
                splits[0] += DOWN // 4

            def ffn(layer, n):
                c = UP0[layer]
                up_pair(layer, n, c, UP_PAIRS * layer)
                with pe.Fori(1, UP_PAIRS - 1) as t:
                    up_pair(layer, n, c + UP_PAIR, t + UP_PAIRS * layer, (t - 1) * UP_PAIR)
                up_pair(layer, n, c + UP_PAIR * (UP_PAIRS - 1), UP_PAIRS * (layer + 1) - 1)
                down(layer, DN0[layer])

            def b_attend(j, h, steps):
                if j == steps[0]:
                    pe.wait_ge(b_qkn, h + 1)
                    at_least(pe, b_on, h)
                    at_least(pe, b_oT_act, h)
                    at_least(pe, b_oT_dve, h)
                    for g in range(G):
                        for s in range(2):
                            for m in range(M):
                                at = SEQ * (g % 2) + P * m
                                ins = pe.transpose(psum[:, 4 + 2 * s + g // 2, at:at + P], b_raw[:, 2 * g + m, HD * s:HD * (s + 1)],
                                                   ident[:, :])
                    ins.then_inc(b_tqk, 1)
                if j == steps[1]:
                    pe.wait_ge(b_qT_ready, h + 1)
                    pe.wait_ge(b_kT_ready, h + 1)
                    for g in range(G):
                        at = SEQ * (g % 2)
                        pe.matmul(psum[:, 4 + g // 2, at:at + SEQ], b_qT[:, g, P:SEQ], b_kT[:, g, :], start=True, stop=True)
                    for g in range(G):
                        ins = pe.matmul(psum[:, 7, P * g:P * (g + 1)], b_qT[:, g, 0:P], b_kT[:, g, 0:P],
                                        start=True, stop=True)
                    ins.then_inc(b_scores, 1)
                if j == steps[2]:
                    pe.wait_ge(b_probs, h + 1)
                    for i in range(9):
                        bank, at = (4, P * i) if i < 4 else (5, P * (i - 4)) if i < 6 else (6, P * (i - 6))
                        ins = pe.transpose(psum[:, bank, at:at + P], b_lg[:, P * i:P * (i + 1)], ident[:, :])
                    ins.then_inc(b_tp, 1)
                if j == steps[3]:
                    pe.wait_ge(b_pT_act, h + 1)
                    pe.wait_ge(b_pT_dve, h + 1)
                    pe.wait_ge(b_vheld, h + 1)
                    for g in range(G):
                        pe.matmul(psum[:, 7, 0:VD], b_pT[:, 6 + g, :], b_v[:, 2 * g, :], start=(g == 0), stop=(g == G - 1))
                    for i in range(2 * G):
                        ins = pe.matmul(psum[:, 7, VD:2 * VD], b_pT[:, i, :], b_v[:, i, :], start=(i == 0),
                                        stop=(i == 2 * G - 1))
                    ins.then_inc(b_pv, 1)
                if j == steps[4]:
                    pe.wait_ge(b_on, h + 1)
                    for e in range(2):
                        for b in range(M):
                            ins = pe.transpose(psum[:, 6 - e, P * b:P * (b + 1)], b_o[:, b, P * e:P * (e + 1)], ident[:, :])
                    ins.then_inc(b_to, 1)

            def b_head(c, h, more=0):
                for j in range(B_HEAD):
                    g = j // 4
                    if j % 4 == 0:
                        free = 3 * h if g == 0 else 3 * h + g - 1
                        at_least(pe, b_raw_act, free)
                        at_least(pe, b_raw_dve, free)
                    if isinstance(h, int) and j < 4:
                        pe.wait_ge(xT_lo, KB * 2 + 4 * j + 4)
                    b = 2 * (g % 2)
                    moving(c + j, more, range(4 * (j % 4), 4 * (j % 4) + 4), 512, [(b, b + 1)], j % 4 == 0, j % 4 == 3)
                    if isinstance(h, int):
                        begin(2, j)
                    else:
                        b_attend(j, h - 1, B_STEPS)

            pe.wait_ge(ident_in, 16)
            pe.wait_ge(gain_in, 16 * 7)
            pe.transpose(psum[:, 0, 0:GAINS], t_gain[0:GAINS, :], ident[0:GAINS, 0:GAINS]).then_inc(pe_setup, 1)
            transpose_resid(0, 0)
            pe.wait_ge(conv_in, 16 * 4)
            for i in range(8):
                at = 2 * FB * (i % 4)
                pe.transpose(psum[:, 1 + i // 4, at:at + 2 * FB], t_conv[0:2 * FB, i, :], ident[0:2 * FB, 0:2 * FB])
            pe.wait_ge(onehot_in, 16)
            pe.wait_ge(rel_in, 16)
            pe.matmul(psum[0:H, 3, 0:ROW], t_rel[0:BUCKETS, :], t_onehot[0:BUCKETS, :], start=True,
                      stop=True).then_inc(pe_setup, 1)

            transpose_resid(0, 1)
            pe.wait_ge(consts_ready, 1)
            a_head(A0, 0)
            with pe.Fori(1, H) as h:
                a_head(A0 + A_HEAD, h, (h - 1) * A_HEAD)
            out_proj(AO0, 1, a_v_act, a_v_dve, H, a_attend, A_STEPS)
            ffn(0, 1)
            transpose_resid(2, 0)
            transpose_resid(2, 1)
            b_head(B0, 0)
            with pe.Fori(1, H) as h:
                b_head(B0 + B_HEAD, h, (h - 1) * B_HEAD)
            out_proj(BO0, 3, b_raw_act, b_raw_dve, 3 * H, b_attend, B_LAST_STEPS)
            ffn(1, 3)


INPUTS = ["x", "rel_bias", "ln_mix", "ln_ffn", "a_w_qkv", "a_q_norm", "a_k_norm", "a_lambda", "a_subln", "a_w_o",
          "b_w_qkv", "b_q_norm", "b_k_norm", "b_w_o", "f_w_up", "f_conv_w", "f_conv_b", "f_w_down"]


def kernel(**inputs):
    from concourse import bacc
    from concourse.bass_utils import run_bass_kernel_spmd

    nc = bacc.Bacc("TRN2", target_bir_lowering=False, num_devices=1)
    arrays = {name: np.ascontiguousarray(inputs[name]) for name in INPUTS}
    arrays.update(shape_tables())
    given = {n: nc.dram_tensor(f"in_{n}", a.shape, mybir.dt.from_np(a.dtype), kind="ExternalInput").ap()
             for n, a in arrays.items()}
    out = nc.dram_tensor("out", (1, SEQ, D), F32, kind="ExternalOutput").ap()
    trunk(nc, **given, out=out)
    run = run_bass_kernel_spmd(nc, [{f"in_{n}": a for n, a in arrays.items()}], core_ids=[0])
    return run.results[0]["out"]
```

```python
import math
from contextlib import ExitStack, contextmanager

import numpy as np

import concourse.bass as bass
from concourse import mybir

F32 = mybir.dt.float32
F32R = mybir.dt.float32r
I32 = mybir.dt.int32
ALU = mybir.AluOpType
ACT = mybir.ActivationFunctionType
AX = mybir.AxisListType

P = 128
SEQ, D = 256, 2048
M = SEQ // P
KB = D // P
H, HD, VD = 8, 128, 256
F = 5632
FB = F // P
EPS = 1e-6
SCALE = HD ** -0.5
BUCKETS, MAX_DISTANCE = 32, 2048
GROUPS = ((128, 1), (512, 4), (2048, 16))
G = len(GROUPS)
MASKED = -1e30
LAM_INIT = 0.8 - 0.6 * math.exp(-0.3 * 0)

W = 2048
SLOTS = 4
LEAD = 2

A_HEAD, B_HEAD, OUT, UP_PAIR, UP_PAIRS, DOWN = 8, 12, 16, 8, FB // 4, FB
A0 = 0
AO0 = A0 + H * A_HEAD
UP0 = (AO0 + OUT, 0)
DN0 = (UP0[0] + UP_PAIR * UP_PAIRS, 0)
B0 = DN0[0] + DOWN
BO0 = B0 + H * B_HEAD
UP0 = (UP0[0], BO0 + OUT)
DN0 = (DN0[0], UP0[1] + UP_PAIR * UP_PAIRS)
END = DN0[1] + DOWN
assert all(x % SLOTS == 0 for x in (AO0, *UP0, *DN0, B0, BO0, A_HEAD, B_HEAD, OUT, UP_PAIR, DOWN))



def loads_of(c):
    if A0 <= c < AO0:
        return 2 if (c - A0) % A_HEAD < 4 else 1
    if B0 <= c < BO0:
        return 3
    return 1


def landed(c):
    return 16 * sum(loads_of(i) for i in range(c % SLOTS, c + 1, SLOTS))


A_RATE, B_RATE, RATE = 16 * 3 // A_HEAD, 16 * 9 // B_HEAD, 16 // SLOTS

G_MIX, G_FFN, G_AQ, G_AK, G_BQ, G_BK, G_SUB = 0, 32, 64, 65, 66, 69, 72
GAINS = 74

ROW = 384
KINDS = 1 + G

A_STEPS = (0, 2, 3, 6)
A_LAST_STEPS = (0, 2, 3, 5)
B_STEPS = (2, 4, 6, 8)
B_LAST_STEPS = (1, 2, 4, 5)

MAGIC = 0x5F3759DF
NEWTON = 3
RSQRT_STEPS = 3 + 3 * NEWTON


def bucket_of(dist):
    exact = BUCKETS // 2
    n = max(dist, 0)
    if n < exact:
        return n
    return min(exact + int(math.log(n / exact) / math.log(MAX_DISTANCE / exact) * (BUCKETS - exact)), BUCKETS - 1)


def shape_tables():
    onehot = np.zeros((BUCKETS, ROW), np.float32)
    for i in range(ROW):
        onehot[bucket_of(SEQ - 1 - i), i] = 1.0
    dist = P + np.arange(P)[:, None] - np.arange(SEQ)[None, :]
    masks = np.zeros((P, KINDS, SEQ), np.float32)
    masks[:, 0][dist < 0] = MASKED
    for g, (_, dil) in enumerate(GROUPS):
        masks[:, 1 + g][(dist < 0) | (dist % dil != 0) | (dist > P * dil)] = MASKED
    return {"identity": np.eye(P, dtype=np.float32), "onehot": onehot, "masks": masks}


class Chain:

    def __init__(self, engine, sem):
        self.engine, self.sem, self.n, self.offset = engine, sem, 0, 0

    def step(self, instruction):
        instruction.then_inc(self.sem, 1)
        self.n += 1

    def settle(self):
        self.engine.wait_ge(self.sem, self.n + self.offset)

    @contextmanager
    def loop(self, turn, turns, steps):
        start, self.offset = self.n, turn * steps
        yield
        assert self.n - start == steps, (self.n - start, steps)
        self.n, self.offset = start + steps * turns, 0


def trunk(nc, x, rel_bias, ln_mix, ln_ffn, a_w_qkv, a_q_norm, a_k_norm, a_lambda, a_subln, a_w_o,
          b_w_qkv, b_q_norm, b_k_norm, b_w_o, f_w_up, f_conv_w, f_conv_b, f_w_down,
          identity, onehot, masks, out):
    bias_rows = nc.dram_tensor("bias_rows", (H, ROW), F32)
    bias_wide = nc.dram_tensor("bias_wide", (P, H, ROW), F32)

    with ExitStack() as ctx:
        def sb(name, shape, dt=F32):
            return ctx.enter_context(nc.sbuf_tensor(name, shape, dt))

        def sem(name):
            return ctx.enter_context(nc.semaphore(name))

        w_raw = sb("w_raw", [P, SLOTS, W])
        w_hi = sb("w_hi", [P, SLOTS, W], F32R)
        w_lo = sb("w_lo", [P, SLOTS, W], F32R)
        xT = sb("xT", [P, KB, 2, SEQ], F32R)
        resid = sb("resid", [P, M, D])
        ident = sb("ident", [P, P])
        gains = sb("gains", [P, GAINS])
        conv = sb("conv", [P, 2, 4, 2 * FB])
        sub_g = sb("sub_g", [P, 2])
        nlam = sb("nlam", [P, 1])
        small = sb("small", [P, 96])
        rstd_row = sb("rstd_row", [P, SEQ])
        psum = ctx.enter_context(nc.psum_tensor("psum", [P, 8, 512], F32))

        phase = sb("phase", [P, 14848])

        def part(at, *dims):
            n = int(np.prod(dims))
            assert at + n <= 14848
            v = phase[:, at:at + n]
            if len(dims) == 2:
                v = v.rearrange("p (a b) -> p a b", b=dims[1])
            if len(dims) == 3:
                v = v.rearrange("p (a b c) -> p a b c", b=dims[1], c=dims[2])
            return v

        squared = part(0, M, D)
        a_qk = part(0, M, 512)
        a_sq = part(1024, M, 512)
        a_qT = part(2048, 2, SEQ)
        a_kT = part(2560, 2, SEQ)
        a_v = part(3072, M, VD)
        a_lg = part(3584, 768)
        a_a = part(4352, 384)
        a_aT = part(4736, 3, P)
        a_o = part(5120, M, VD)
        a_oT = part(5632, KB, SEQ)
        a_bias = part(9728, H, SEQ)
        b_raw = part(0, G * M, 512)
        b_qT = part(3072, G, SEQ)
        b_kT = part(3840, G, SEQ)
        b_v = part(4608, G * M, VD)
        b_lg = part(6144, 1152)
        b_pT = part(7296, 9, P)
        b_sq = part(7296, G * M, 256)
        b_bias = part(8960, G, SEQ)
        b_mask = part(9728, G, SEQ)
        b_row = part(10496, SEQ)
        b_oT = part(10752, KB, SEQ)
        hT = part(0, FB, SEQ)
        u = part(11264, 4, SEQ + 2)
        c_gate = part(12296, 4, SEQ)
        c_val = part(13320, 4, SEQ)
        t_onehot = part(5632, ROW)
        t_mask = part(6016, 1, SEQ)
        t_rows = part(6272, ROW)
        t_rel = part(6656, H)
        t_lam = part(11776, 4, HD)
        t_gain = part(12288, P)
        t_conv = part(12416, 8, P)
        t_prod = part(13440, 2, HD)

        ssp = small[:, 0:8]
        r_ss, r_r, r_t = small[:, 8:10], small[:, 10:12], small[:, 12:14]
        n_ss, n_r, n_t = small[:, 16:28], small[:, 28:40], small[:, 40:52]
        mx, nmx = small[:, 52:56], small[:, 56:60]
        den, rden, rneg = small[:, 60:64], small[:, 64:68], small[:, 68:70]
        o_ss, o_r = n_ss[:, 8:10], n_r[:, 8:10]
        lam_s, lam_e = small[:, 76:78], small[:, 78:80]

        x_in = [sem(f"x_in{q}") for q in range(4)]
        (
            ident_in, onehot_in, mask_in, rel_in, lam_in, gain_in, small_gain_in, conv_in
        ) = (sem(n) for n in (
            "ident_in", "onehot_in", "mask_in", "rel_in", "lam_in", "gain_in", "small_gain_in",
            "conv_in"))
        (
            pe_setup, bias_rows_made, bias_rows_out, bias_wide_out, a_row_in, a_bias_ready, b_mask_in,
            gains_ready, lam_prod, lam_exp, lam_ready, consts_ready
        ) = (sem(n) for n in (
            "pe_setup", "bias_rows_made", "bias_rows_out", "bias_wide_out", "a_row_in", "a_bias_ready",
            "b_mask_in", "gains_ready", "lam_prod", "lam_exp", "lam_ready", "consts_ready"))
        w_in = [sem(f"w_in{s}") for s in range(SLOTS)]
        hi_ready, lo_ready, used = sem("w_hi_ready"), sem("w_lo_ready"), sem("w_used")
        dve_chain = sem("dve_chain")
        r_add, r_sq, r_rstd, rstd_ps, rstd_row_ready = (sem(n) for n in (
            "r_add", "r_sq", "r_rstd", "rstd_ps", "rstd_row_ready"))
        xT_ps, xT_hi, xT_lo = sem("xT_ps"), sem("xT_hi"), sem("xT_lo")
        xs_hi, xs_lo = sem("xs_hi"), sem("xs_lo")
        (a_qk_act, a_qk_dve, a_sq_ready, a_qkn, a_tqk, a_qT_ready, a_kT_ready, a_v_act, a_v_dve, a_scores,
         a_lg_ready, a_nmx, a_probs, a_diff, a_ta, a_aT_ready, a_pv, a_rstd, a_on, a_to, a_oT_act,
         a_oT_dve) = (sem(n) for n in (
             "a_qk_act", "a_qk_dve", "a_sq_ready", "a_qkn", "a_tqk", "a_qT_ready", "a_kT_ready", "a_v_act", "a_v_dve",
             "a_scores", "a_lg_ready", "a_nmx", "a_probs", "a_diff", "a_ta", "a_aT_ready", "a_pv", "a_rstd",
             "a_on", "a_to", "a_oT_act", "a_oT_dve"))
        (b_raw_act, b_raw_dve, b_sq_ready, b_qkn, b_vheld, b_tqk, b_qT_ready, b_kT_ready, b_scores, b_row_in, b_bias_ready,
         b_lg_ready, b_nmx, b_exp, b_rden, b_probs, b_tp, b_pT_act, b_pT_dve, b_pv, b_oT_act,
         b_oT_dve) = (sem(n) for n in (
             "b_raw_act", "b_raw_dve", "b_sq_ready", "b_qkn", "b_vheld", "b_tqk", "b_qT_ready", "b_kT_ready",
             "b_scores", "b_row_in", "b_bias_ready", "b_lg_ready", "b_nmx", "b_exp", "b_rden", "b_probs", "b_tp",
             "b_pT_act", "b_pT_dve", "b_pv", "b_oT_act", "b_oT_dve"))
        (
            gate_low, val_low, gate_read, val_read, gate_scaled, val_scaled, gate_init, val_init,
            gate_taps, silu_ready, h_ready
        ) = (sem(n) for n in (
            "gate_low", "val_low", "gate_read", "val_read", "gate_scaled", "val_scaled", "gate_init",
            "val_init", "gate_taps", "silu_ready", "h_ready"))
        down_quarter = sem("down_quarter")
        out_done = sem("out_done")

        block = ctx.enter_context(nc.Block())

        def at_least(engine, s, value):
            if not (isinstance(value, int) and value <= 0):
                engine.wait_ge(s, value)

        def xT_bank(n, k):
            return 4 + k // 2 % 4 if n == 0 else k // 2

        def is_turn(turn, n):
            return isinstance(turn, int) and turn == n

        def b_bank(g, odd):
            return 2 * ((g + odd) % 2)

        def chunk_used(engine, c, more=0):
            engine.wait_ge(used, c + 1 + more)

        @block.sync
        def _(sp):
            def load_x(q):
                cols = slice(512 * q, 512 * (q + 1))
                src = x[0].rearrange("(m p) d -> p m d", p=P)[:, :, cols]
                sp.dma_start(resid[:, :, cols], src).then_inc(x_in[q], 16)

            def free_slot(c, more=0):
                at_least(sp, lo_ready, c - SLOTS + 1 + more)

            def load_a_head(c, h, more=0):
                for j in range(A_HEAD):
                    if isinstance(h, int) and j < 4:
                        load_x(j)
                    free_slot(c + j, more)
                    rows = a_w_qkv[0, 512 * (j % 4):512 * (j % 4 + 1), :]
                    slot = (c + j) % SLOTS
                    if j < 4:
                        tile = w_raw[:, slot, :].rearrange("p (k c) -> p k c", k=4)
                        for s in range(2):
                            src = rows[:, 2048 * s:2048 * (s + 1)].rearrange("(k p) c -> p k c", p=P)
                            sp.dma_start(tile[:, :, 256 * s:256 * (s + 1)],
                                         src[:, :, bass.ts(h, 256)]).then_inc(w_in[slot], 16)
                    else:
                        src = rows[:, 4096:6144].rearrange("(k p) c -> p k c", p=P)[:, :, bass.ts(h, 256)]
                        dst = w_raw[:, slot, 0:1024].rearrange("p (k c) -> p k c", k=4)
                        sp.dma_start(dst, src).then_inc(w_in[slot], 16)

            def load_b_head(c, h, more=0):
                for j in range(B_HEAD):
                    g, slot = j // 4, (c + j) % SLOTS
                    free_slot(c + j, more)
                    rows = b_w_qkv[0, 512 * (j % 4):512 * (j % 4 + 1), 4096 * g:4096 * (g + 1)]
                    dst = w_raw[:, slot, :].rearrange("p (k c) -> p k c", k=4)
                    for at, n, first in ((0, HD, 0), (HD, HD, 1024), (256, VD, 2048)):
                        src = rows[:, first:first + H * n].rearrange("(k p) c -> p k c", p=P)[:, :, bass.ts(h, n)]
                        sp.dma_start(dst[:, :, at:at + n], src).then_inc(w_in[slot], 16)

            def load_out(c, w):
                for j in range(OUT):
                    slot = (c + j) % SLOTS
                    free_slot(c + j)
                    src = w[0, 256 * (j % 8):256 * (j % 8 + 1), 1024 * (j // 8):1024 * (j // 8 + 1)].rearrange(
                        "(k p) c -> p k c", p=P)
                    dst = w_raw[:, slot, :].rearrange("p (k c) -> p k c", k=2)
                    sp.dma_start(dst, src).then_inc(w_in[slot], 16)

            def load_ffn(layer):
                c = UP0[layer]
                with sp.Fori(0, UP_PAIRS) as t:
                    for j in range(UP_PAIR):
                        slot = (c + j) % SLOTS
                        free_slot(c + j, t * UP_PAIR)
                        half = F * (j // 4)
                        src = f_w_up[layer, 512 * (j % 4):512 * (j % 4 + 1), half:half + F].rearrange(
                            "(k p) c -> p k c", p=P)[:, :, bass.ts(t, 512)]
                        dst = w_raw[:, slot, :].rearrange("p (k c) -> p k c", k=4)
                        sp.dma_start(dst, src).then_inc(w_in[slot], 16)
                c = DN0[layer]
                rows = f_w_down[layer].rearrange("(t j p) c -> p t j c", p=P, j=4)
                with sp.Fori(0, DOWN // 4) as t:
                    for j in range(4):
                        slot = (c + j) % SLOTS
                        free_slot(c + j, t * 4)
                        src = rows[:, bass.ts(t, 1), j, :].rearrange("p t c -> p (t c)")
                        sp.dma_start(w_raw[:, slot, :], src).then_inc(w_in[slot], 16)

            load_a_head(A0, 0)
            with sp.Fori(1, H) as h:
                load_a_head(A0 + A_HEAD, h, (h - 1) * A_HEAD)
            load_out(AO0, a_w_o)
            load_ffn(0)
            with sp.Fori(0, H) as h:
                load_b_head(B0, h, h * B_HEAD)
            load_out(BO0, b_w_o)
            load_ffn(1)
            for q in range(4):
                sp.wait_ge(r_add, 12 + q + 1)
                sp.dma_start(out[0].rearrange("(m p) d -> p m d", p=P)[:, :, 512 * q:512 * (q + 1)],
                             resid[:, :, 512 * q:512 * (q + 1)]).then_inc(out_done, 16)
            sp.wait_ge(out_done, 64)

        @block.gpsimd
        def _(pool):
            pool.dma_start(t_onehot[0:BUCKETS, :], onehot).then_inc(onehot_in, 16)
            pool.dma_start(t_rel[0:BUCKETS, :], rel_bias).then_inc(rel_in, 16)
            for at, g in ((G_AQ, a_q_norm), (G_AK, a_k_norm), (G_BQ, b_q_norm[0]), (G_BK, b_k_norm[0]),
                          (G_SUB, a_subln.rearrange("l (k e) -> (l k) e", e=P))):
                pool.dma_start(t_gain[at:at + g.shape[0], :], g).then_inc(small_gain_in, 16)
            for layer in range(2):
                pool.dma_start(t_conv[0:2 * FB, 4 * layer:4 * layer + 3, :],
                              f_conv_w[layer].rearrange("t (j e) -> j t e", e=P)).then_inc(conv_in, 16)
                pool.dma_start(t_conv[0:2 * FB, 4 * layer + 3, :],
                              f_conv_b[layer].rearrange("(j e) -> j e", e=P)).then_inc(conv_in, 16)
            pool.dma_start(t_lam, a_lambda.partition_broadcast(P).rearrange("p l a e -> p (l a) e")).then_inc(lam_in, 16)
            pool.dma_start(t_mask, masks[:, 0:1, :]).then_inc(mask_in, 16)

            def tables(first, heads):
                return bass.AP(bias_wide, first * ROW + P - 1, [[H * ROW - 1, P], [ROW, heads], [1, SEQ]])

            pool.wait_ge(bias_rows_made, 1)
            pool.dma_start(bias_rows[:, :], t_rows[0:H, :]).then_inc(bias_rows_out, 16)
            pool.wait_ge(bias_rows_out, 16)
            pool.dma_start(bias_wide[:, :, :],
                           bass.AP(bias_rows, 0, [[0, P], [ROW, H], [1, ROW]])).then_inc(bias_wide_out, 16)
            pool.wait_ge(bias_wide_out, 16)
            pool.dma_start(a_bias, tables(0, H)).then_inc(a_row_in, 16)
            pool.wait_ge(a_row_in, 16)
            pool.wait_ge(mask_in, 16)
            nc.gpsimd.tensor_tensor(a_bias, a_bias, t_mask.to_broadcast([P, H, SEQ]), ALU.add).then_inc(a_bias_ready, 1)

            pool.wait_ge(r_add, 8)
            pool.dma_start(b_mask, masks[:, 1:KINDS, :]).then_inc(b_mask_in, 16)
            pool.wait_ge(b_mask_in, 16)

            def b_head(h):
                if h > 0:
                    pool.wait_ge(b_bias_ready, h)
                pool.dma_start(b_row, tables(h, 1)).then_inc(b_row_in, 16)
                pool.wait_ge(b_row_in, 16 * h + 16)
                if h > 0:
                    pool.wait_ge(b_lg_ready, h)
                nc.gpsimd.tensor_tensor(b_bias, b_row.unsqueeze(1).to_broadcast([P, G, SEQ]), b_mask,
                                        ALU.add).then_inc(b_bias_ready, 1)
                pool.wait_ge(b_raw_act, 3 * h + 3)
                pool.wait_ge(b_raw_dve, 3 * h + 3)
                if h > 0:
                    pool.wait_ge(b_pv, h)
                nc.gpsimd.tensor_copy(b_v, b_raw[:, :, 256:512]).then_inc(b_vheld, 1)

            for h in range(H):
                b_head(h)

        @block.scalar
        def _(act):
            def split(c, more=0, width=W, rate=RATE):
                if c >= END:
                    return
                slot = c % SLOTS
                act.wait_ge(w_in[slot], landed(c) + more * rate)
                at_least(act, used, c - SLOTS + 1 + more)
                nc.scalar.activation(w_hi[:, slot, 0:width], w_raw[:, slot, 0:width], ACT.Copy).then_inc(hi_ready, 1)

            def a_width(j):
                return W if j % A_HEAD < 4 else W // 2

            def squares(n, q):
                for m in range(M):
                    ins = nc.scalar.activation(squared[:, m, 512 * q:512 * (q + 1)], resid[:, m, 512 * q:512 * (q + 1)],
                                               ACT.Square, accum_out=ssp[:, 4 * m + q:4 * m + q + 1])
                ins.then_inc(r_sq, 1)

            def take_xT(n, gain, q):
                for k in range(4 * q, 4 * q + 4):
                    act.wait_ge(xT_ps, KB // 2 * n + k // 2 + 1)
                    at = 256 * (k % 2)
                    nc.scalar.activation(xT[:, k, 0, :], psum[:, xT_bank(n, k), at:at + 256], ACT.Copy,
                                         scale=gains[:, gain + k:gain + k + 1]).then_inc(xT_hi, 1)

            def begin(n, gain, j, before):
                if j == 0:
                    take_xT(n, gain, 2)
                    take_xT(n, gain, 3)
                if j < 2:
                    for q in range(max(before, 2 * j), 2 * j + 2):
                        if n > 0:
                            act.wait_ge(r_add, 4 * (n - 1) + q + 1)
                        squares(n, q)

            def a_take_qk(c, h, more=0):
                chunk_used(act, c, more)
                at_least(act, a_tqk, h)
                if is_turn(h, 0):
                    act.wait_ge(r_rstd, 1)
                nc.scalar.activation(a_qk[:, 0, :], psum[:, 0, :], ACT.Copy, scale=r_r[:, 0:1]).then_inc(a_qk_act, 1)

            def a_squares(h):
                if not is_turn(h, H):
                    act.wait_ge(a_qk_act, h + 1)
                    act.wait_ge(a_qk_dve, h + 1)
                    for i in range(8):
                        m, cols = i // 4, slice(HD * (i % 4), HD * (i % 4 + 1))
                        ins = nc.scalar.activation(a_sq[:, m, cols], a_qk[:, m, cols], ACT.Square,
                                                   accum_out=n_ss[:, i:i + 1])
                if not is_turn(h, 0):
                    act.wait_ge(a_pv, h)
                    at_least(act, a_to, h - 1)
                    for b in range(M):
                        ins = nc.scalar.activation(a_o[:, b, :], psum[:, 5, VD * b:VD * (b + 1)], ACT.Square,
                                                   accum_out=o_ss[:, b:b + 1])
                ins.then_inc(a_sq_ready, 1)

            def a_take_q(h):
                act.wait_ge(a_tqk, h + 1)
                at_least(act, a_scores, h)
                nc.scalar.activation(a_qT, psum[:, 4, :].rearrange("p (a b) -> p a b", a=2), ACT.Copy,
                                     scale=gains[:, G_AQ:G_AQ + 1]).then_inc(a_qT_ready, 1)

            def a_take_v(c, h, more=0):
                chunk_used(act, c, more)
                at_least(act, a_pv, h)
                nc.scalar.activation(a_v[:, 0, :], psum[:, 2, 0:VD], ACT.Copy, scale=r_r[:, 0:1]).then_inc(a_v_act, 1)

            def a_exp(h):
                act.wait_ge(a_nmx, h + 1)
                for i in range(2):
                    nc.scalar.activation(a_lg[:, 256 * i:256 * (i + 1)], a_lg[:, 256 * i:256 * (i + 1)], ACT.Exp,
                                         bias=nmx[:, i:i + 1], accum_out=den[:, i:i + 1])
                for i in range(2):
                    at = 512 + 128 * i
                    ins = nc.scalar.activation(a_lg[:, at:at + 128], a_lg[:, at:at + 128], ACT.Exp,
                                               bias=nmx[:, 2 + i:3 + i], accum_out=den[:, 2 + i:3 + i])
                ins.then_inc(a_probs, 1)

            def a_take_aT(h):
                act.wait_ge(a_ta, h + 1)
                at_least(act, a_pv, h)
                nc.scalar.activation(a_aT, psum[:, 4, 0:384].rearrange("p (a b) -> p a b", a=3),
                                     ACT.Copy).then_inc(a_aT_ready, 1)

            def a_norm_o(h):
                act.wait_ge(a_rstd, h + 2)
                for b in range(M):
                    ins = nc.scalar.activation(a_o[:, b, :], psum[:, 5, VD * b:VD * (b + 1)], ACT.Copy,
                                               scale=o_r[:, b:b + 1])
                ins.then_inc(a_on, 1)

            def a_take_oT(h):
                act.wait_ge(a_to, h + 1)
                nc.scalar.activation(a_oT[:, bass.ds(2 * h, 1), :], psum[:, 6, 0:SEQ].rearrange("p (a b) -> p a b", a=1),
                                     ACT.Copy, scale=sub_g[:, 0:1]).then_inc(a_oT_act, 1)

            def a_attend(j, h, steps):
                if j == steps[0]:
                    a_exp(h)
                if j == steps[1]:
                    a_take_aT(h)
                if j == steps[2] + 1:
                    a_norm_o(h)
                if j == steps[3]:
                    a_take_oT(h)

            def a_head(c, h, more=0):
                for j in range(A_HEAD):
                    if is_turn(h, H - 1) and j == 6:
                        chunk_used(act, c + 4)
                        split_o(a_oT, a_oT_act, a_oT_dve, 0)
                        split_o(a_oT, a_oT_act, a_oT_dve, 1)
                    if j < 4:
                        split(c + j + LEAD, more, a_width(j + LEAD), A_RATE)
                    elif j < 7:
                        split(c + j + LEAD + 1, more, a_width(j + LEAD + 1), A_RATE)
                    if is_turn(h, 0):
                        begin(0, G_MIX, j, 0)
                        if j == 2:
                            act.wait_ge(lam_prod, 1)
                            nc.scalar.activation(lam_e, lam_s, ACT.Exp).then_inc(lam_exp, 1)
                            act.wait_ge(consts_ready, 1)
                    else:
                        a_attend(j, h - 1, A_STEPS)
                    if j == 3:
                        a_take_qk(c + j, h, more)
                        split(c + j + LEAD + 1, more, a_width(j + LEAD + 1), A_RATE)
                        a_squares(h)
                    if j == 7:
                        a_take_v(c + j, h, more)
                        a_take_q(h)

            def split_o(oT, oT_act, oT_dve, hd):
                act.wait_ge(oT_act, hd + 1)
                act.wait_ge(oT_dve, hd + 1)
                nc.scalar.activation(xT[:, 2 * hd:2 * hd + 2, 0, :], oT[:, 2 * hd:2 * hd + 2, :],
                                     ACT.Copy).then_inc(xs_hi, 1)

            def out_proj(c, n, gain, oT, oT_act, oT_dve, attend, steps):
                chunk_used(act, c - 1)
                for j in range(OUT):
                    split(c + j + LEAD)
                    if j < 5:
                        split_o(oT, oT_act, oT_dve, j + 2)
                    if j == 3 and n == 1:
                        a_squares(H)
                    attend(j, H - 1, steps)
                    if j == steps[-1]:
                        split_o(oT, oT_act, oT_dve, H - 1)
                    if j == 7:
                        for q in range(2):
                            act.wait_ge(r_add, 4 * (n - 1) + q + 1)
                            squares(n, q)
                    if j in (9, 11):
                        chunk_used(act, c + j)
                        take_xT(n, gain, (j - 9) // 2)

            def conv_init(c, more, layer, tile, low, ready, init, dst, t, tg):
                chunk_used(act, c, more)
                at_least(act, h_ready, tg)
                nc.scalar.activation(dst, psum[:, 4 * tile:4 * tile + 4, SEQ:2 * SEQ], ACT.Copy).then_inc(low, 1)
                split(c + LEAD + 1, more)
                act.wait_ge(ready, tg + 1)
                for b in range(4):
                    ch = bass.ds(t * 4 + (FB * tile + b), 1)
                    nc.scalar.activation(dst[:, b, :], u[:, b, 2:SEQ + 2], ACT.Identity,
                                         scale=conv[:, layer, 2, ch], bias=conv[:, layer, 3, ch]).then_inc(init, 1)

            def up_pair(layer, n, c, t, tg, more=0):
                for j in range(UP_PAIR):
                    if j % 4 or (j == 0 and is_turn(t, 0)):
                        split(c + j + LEAD, more)
                    if is_turn(t, 0):
                        begin(n, G_FFN + KB * layer, j, 2)
                        if j == 2:
                            act.wait_ge(rstd_ps, layer + 1)
                            nc.scalar.activation(rstd_row[:, :], psum[:, 4, 0:SEQ], ACT.Copy).then_inc(rstd_row_ready, 1)
                    if is_turn(t, UP_PAIRS - 1) and j in (5, 6):
                        chunk_used(act, c + j - 1)
                        split_h(layer, j - 5)
                    if j == 3:
                        conv_init(c + j, more, layer, 0, gate_low, gate_scaled, gate_init, c_gate, t, tg)
                    if j == 4:
                        act.wait_ge(gate_taps, tg + 1)
                        nc.scalar.activation(c_gate, c_gate, ACT.Silu).then_inc(silu_ready, 1)
                    if j == 7:
                        conv_init(c + j, more, layer, 1, val_low, val_scaled, val_init, c_val, t, tg)

            def split_h(layer, b, t=0):
                slot = 4 * b if b == 0 else 4 + 4 * ((b - 1) % 2)
                nc.scalar.activation(xT[:, slot:slot + 4, 0, :], hT[:, bass.ds(4 * b + 8 * t, 4), :],
                                     ACT.Copy).then_inc(xs_hi, 1)

            def down(layer, c, n):
                for j in range(1, 4):
                    split(c + j + LEAD)
                act.wait_ge(h_ready, UP_PAIRS * (layer + 1))
                with act.Fori(0, 4) as t:
                    for j in range(8):
                        split(c + 4 + j + LEAD, t * 8)
                        if j == 1:
                            chunk_used(act, c + 3, t * 8)
                            split_h(layer, 2, t)
                        if j == 5:
                            chunk_used(act, c + 7, t * 8)
                            split_h(layer, 3, t)
                for j in range(8):
                    split(c + 36 + j + LEAD)
                    if j == 1:
                        chunk_used(act, c + 35)
                        split_h(layer, 10)
                if layer == 0:
                    take_xT(n, G_MIX + KB, 0)
                    take_xT(n, G_MIX + KB, 1)

            def ffn(layer, n):
                c = UP0[layer]
                up_pair(layer, n, c, 0, UP_PAIRS * layer)
                with act.Fori(1, UP_PAIRS - 1) as t:
                    up_pair(layer, n, c + UP_PAIR, t, t + UP_PAIRS * layer, (t - 1) * UP_PAIR)
                up_pair(layer, n, c + UP_PAIR * (UP_PAIRS - 1), UP_PAIRS - 1, UP_PAIRS * (layer + 1) - 1)
                down(layer, DN0[layer], n + 1)

            def b_take(c, g, h, odd, more):
                chunk_used(act, c, more)
                at_least(act, b_tqk, h)
                at_least(act, b_vheld, h)
                if is_turn(h, 0) and g == 0:
                    act.wait_ge(r_rstd, 3)
                nc.scalar.activation(b_raw[:, 2 * g, :], psum[:, b_bank(g, odd), :], ACT.Copy,
                                     scale=r_r[:, 0:1]).then_inc(b_raw_act, 1)

            def b_squares(h):
                act.wait_ge(b_raw_act, 3 * h + 3)
                act.wait_ge(b_raw_dve, 3 * h + 3)
                nc.scalar.activation(b_sq, b_raw[:, :, 0:256], ACT.Square).then_inc(b_sq_ready, 1)

            def b_attend(j, h, steps):
                if j == 0:
                    b_squares(h)
                if j == steps[0]:
                    act.wait_ge(b_tqk, h + 1)
                    at_least(act, b_scores, h)
                    for g in range(G):
                        at = SEQ * (g % 2)
                        ins = nc.scalar.activation(b_qT[:, g, :], psum[:, 4 + g // 2, at:at + SEQ], ACT.Copy,
                                                   scale=gains[:, G_BQ + g:G_BQ + g + 1])
                    ins.then_inc(b_qT_ready, 1)
                if j == steps[1]:
                    act.wait_ge(b_nmx, h + 1)
                    nc.scalar.activation(b_lg[:, 0:768], b_lg[:, 0:768], ACT.Exp, bias=nmx[:, 1:2],
                                         accum_out=den[:, 1:2])
                    nc.scalar.activation(b_lg[:, 768:1152], b_lg[:, 768:1152], ACT.Exp, bias=nmx[:, 0:1],
                                         accum_out=den[:, 0:1]).then_inc(b_exp, 1)
                    act.wait_ge(b_rden, h + 1)
                    nc.scalar.activation(b_lg[:, 0:768], b_lg[:, 0:768], ACT.Copy, scale=rden[:, 1:2])
                    nc.scalar.activation(b_lg[:, 768:1152], b_lg[:, 768:1152], ACT.Copy,
                                         scale=rden[:, 0:1]).then_inc(b_probs, 1)
                if j == steps[2]:
                    act.wait_ge(b_tp, h + 1)
                    at_least(act, b_pv, h)
                    nc.scalar.activation(b_pT[:, 0:4, :], psum[:, 4, :].rearrange("p (a b) -> p a b", a=4),
                                         ACT.Copy).then_inc(b_pT_act, 1)
                if j == steps[3]:
                    act.wait_ge(b_pv, h + 1)
                    nc.scalar.activation(b_oT[:, bass.ds(2 * h, 1), :],
                                         psum[:, 7, 0:SEQ].rearrange("p (a b) -> p a b", a=1),
                                         ACT.Copy).then_inc(b_oT_act, 1)

            def b_head(c, h, odd, more=0):
                for j in range(B_HEAD):
                    split(c + j + LEAD, more, W, B_RATE)
                    if is_turn(h, 0):
                        begin(2, G_MIX + KB, j, 0)
                    else:
                        b_attend(j, h - 1, B_STEPS)
                    if is_turn(h, H - 1) and j == 10:
                        chunk_used(act, c + 8)
                        split_o(b_oT, b_oT_act, b_oT_dve, 0)
                        split_o(b_oT, b_oT_act, b_oT_dve, 1)
                    if j % 4 == 3:
                        b_take(c + j, j // 4, h, odd, more)

            act.dma_start(ident[:, :], identity).then_inc(ident_in, 16)
            for i, g in enumerate((ln_mix, ln_ffn)):
                act.dma_start(t_gain[32 * i:32 * (i + 1), :], g.rearrange("l (k e) -> (l k) e", e=P)).then_inc(gain_in, 16)
            split(0)
            act.wait_ge(gains_ready, 1)
            take_xT(0, G_MIX, 0)
            split(1)
            take_xT(0, G_MIX, 1)

            a_head(A0, 0)
            with act.Fori(0, H // 2 - 1) as t:
                for i in (1, 2):
                    a_head(A0 + i * A_HEAD, t * 2 + i, t * (2 * A_HEAD))
            a_head(A0 + (H - 1) * A_HEAD, H - 1)
            out_proj(AO0, 1, G_FFN, a_oT, a_oT_act, a_oT_dve, a_attend, A_LAST_STEPS)
            ffn(0, 1)
            b_head(B0, 0, 0)
            with act.Fori(0, H // 2 - 1) as t:
                for i in (1, 2):
                    b_head(B0 + i * B_HEAD, t * 2 + i, i % 2, t * (2 * B_HEAD))
            b_head(B0 + (H - 1) * B_HEAD, H - 1, 1)
            out_proj(BO0, 3, G_FFN + KB, b_oT, b_oT_act, b_oT_dve, b_attend, B_LAST_STEPS)
            ffn(1, 3)

        @block.vector
        def _(dve):
            chain = Chain(dve, dve_chain)

            def split(c, more=0, width=W):
                if c >= END:
                    return
                slot = c % SLOTS
                dve.wait_ge(hi_ready, c + 1 + more)
                nc.vector.tensor_tensor(w_lo[:, slot, 0:width], w_raw[:, slot, 0:width], w_hi[:, slot, 0:width],
                                        ALU.subtract).then_inc(lo_ready, 1)

            def a_width(j):
                return W if j % A_HEAD < 4 else W // 2

            def rsqrt(dst, src, tmp, means, ready):
                chain.settle()
                for i, (cols, mean) in enumerate(means):
                    ins = nc.vector.tensor_scalar(src[:, cols], src[:, cols], mean, EPS, ALU.mult, ALU.add)
                chain.step(ins)
                chain.settle()
                chain.step(nc.vector.tensor_scalar(tmp.bitcast(I32), src.bitcast(I32), 1, None,
                                                   ALU.logical_shift_right))
                chain.settle()
                chain.step(nc.vector.tensor_scalar(dst.bitcast(I32), tmp.bitcast(I32), -1, MAGIC, ALU.mult, ALU.add))
                for i in range(NEWTON):
                    chain.settle()
                    chain.step(nc.vector.tensor_tensor(tmp, dst, dst, ALU.mult))
                    chain.settle()
                    chain.step(nc.vector.scalar_tensor_tensor(out=tmp, in0=tmp, scalar=-0.5, in1=src, op0=ALU.mult,
                                                              op1=ALU.mult))
                    chain.settle()
                    ins = nc.vector.scalar_tensor_tensor(out=dst, in0=tmp, scalar=1.5, in1=dst, op0=ALU.add,
                                                         op1=ALU.mult)
                    if i == NEWTON - 1 and ready is not None:
                        ins.then_inc(ready, 1)
                    else:
                        chain.step(ins)

            def rstd(n):
                dve.wait_ge(r_sq, 4 * (n + 1))
                chain.step(nc.vector.tensor_reduce(r_ss, ssp.rearrange("p (m q) -> p m q", m=M), AX.X, ALU.add))
                rsqrt(r_r, r_ss, r_t, [(slice(0, 2), 1.0 / D)], r_rstd)
                dve.wait_ge(r_rstd, n + 1)

            def take_xT(n, gain, q):
                for k in range(4 * q, 4 * q + 4):
                    dve.wait_ge(xT_hi, KB * n + k // 2 * 2 + 2)
                    at = 256 * (k % 2)
                    nc.vector.scalar_tensor_tensor(
                        out=xT[:, k, 1, :], in0=psum[:, xT_bank(n, k), at:at + 256],
                        scalar=gains[:, gain + k:gain + k + 1], in1=xT[:, k, 0, :], op0=ALU.mult,
                        op1=ALU.subtract).then_inc(xT_lo, 1)

            def begin(n, gain, j):
                if j == 0:
                    take_xT(n, gain, 2)
                    take_xT(n, gain, 3)
                if j == 1:
                    rstd(n)

            def add_quarter(q, banks):
                for m in range(M):
                    r = resid[:, m, 512 * q:512 * (q + 1)]
                    ins = nc.vector.tensor_tensor(r, psum[:, banks[m], :], r, ALU.add)
                ins.then_inc(r_add, 1)

            def a_take_qk(c, h, more=0):
                chunk_used(dve, c, more)
                at_least(dve, a_tqk, h)
                nc.vector.tensor_scalar(a_qk[:, 1, :], psum[:, 1, :], r_r[:, 1:2], None, ALU.mult).then_inc(a_qk_dve, 1)

            def a_norms(h):
                first, last = is_turn(h, 0), is_turn(h, H)
                dve.wait_ge(a_sq_ready, h + 1)
                means = [] if last else [(slice(0, 8), 1.0 / HD)]
                if not first:
                    means.append((slice(0, 2) if last else slice(8, 10), 1.0 / VD))
                cols = slice(8, 10) if last else slice(0, 8) if first else slice(0, 10)
                rsqrt(n_r[:, cols], n_ss[:, cols], n_t[:, cols], means, a_rstd)

            def a_norm_qk(h):
                dve.wait_ge(a_rstd, h + 1)
                v = a_qk.rearrange("p m (s e) -> p (m s) e", e=HD)
                nc.vector.tensor_tensor(v, v, n_r[:, 0:8].unsqueeze(2).to_broadcast([P, 8, HD]),
                                        ALU.mult).then_inc(a_qkn, 1)

            def a_take_k(h):
                dve.wait_ge(a_tqk, h + 1)
                at_least(dve, a_scores, h)
                nc.vector.tensor_scalar(a_kT, psum[:, 5, :].rearrange("p (a b) -> p a b", a=2),
                                        gains[:, G_AK:G_AK + 1], None, ALU.mult).then_inc(a_kT_ready, 1)

            def a_take_v(c, h, more=0):
                chunk_used(dve, c, more)
                at_least(dve, a_pv, h)
                nc.vector.tensor_scalar(a_v[:, 1, :], psum[:, 3, 0:VD], r_r[:, 1:2], None, ALU.mult).then_inc(a_v_dve, 1)

            def a_softmax(h):
                dve.wait_ge(a_scores, h + 1)
                bias = a_bias[:, bass.ds(h, 1), :]
                lg1 = a_lg[:, 0:512].rearrange("p (a b) -> p a b", a=2)
                lg0 = a_lg[:, 512:768].rearrange("p (a b) -> p a b", a=2)
                nc.vector.scalar_tensor_tensor(
                    out=lg1, in0=psum[:, 6, :].rearrange("p (a b) -> p a b", a=2), scalar=SCALE,
                    in1=bias.to_broadcast([P, 2, SEQ]), op0=ALU.mult, op1=ALU.add)
                nc.vector.scalar_tensor_tensor(
                    out=lg0, in0=psum[:, 7, 0:256].rearrange("p (a b) -> p a b", a=2), scalar=SCALE,
                    in1=bias[:, :, P:SEQ].to_broadcast([P, 2, P]), op0=ALU.mult, op1=ALU.add).then_inc(a_lg_ready, 1)
                dve.wait_ge(a_lg_ready, h + 1)
                nc.vector.tensor_reduce(mx[:, 0:2], lg1, AX.X, ALU.max)
                chain.step(nc.vector.tensor_reduce(mx[:, 2:4], lg0, AX.X, ALU.max))
                chain.settle()
                nc.vector.tensor_scalar(nmx, mx, -1.0, None, ALU.mult).then_inc(a_nmx, 1)
                dve.wait_ge(a_probs, h + 1)
                chain.step(nc.vector.reciprocal(rden, den))
                chain.settle()
                for b, (at, n, col) in enumerate(((512, 128, 2), (0, 256, 0))):
                    nc.vector.tensor_scalar(rneg[:, b:b + 1], rden[:, col + 1:col + 2], nlam[:, 0:1], None, ALU.mult)
                    to = 0 if b == 0 else 128
                    chain.step(nc.vector.tensor_scalar(a_a[:, to:to + n], a_lg[:, at:at + n], rden[:, col:col + 1],
                                                       None, ALU.mult))
                chain.settle()
                for b, (at, n) in enumerate(((512, 128), (0, 256))):
                    to = 0 if b == 0 else 128
                    ins = nc.vector.scalar_tensor_tensor(
                        out=a_a[:, to:to + n], in0=a_lg[:, at + n:at + 2 * n], scalar=rneg[:, b:b + 1],
                        in1=a_a[:, to:to + n], op0=ALU.mult, op1=ALU.add)
                ins.then_inc(a_diff, 1)

            def a_attend(j, h, steps):
                if j == steps[0]:
                    a_softmax(h)
                if j == steps[3]:
                    dve.wait_ge(a_to, h + 1)
                    nc.vector.tensor_scalar(a_oT[:, bass.ds(2 * h + 1, 1), :],
                                            psum[:, 7, 0:SEQ].rearrange("p (a b) -> p a b", a=1),
                                            sub_g[:, 1:2], None, ALU.mult).then_inc(a_oT_dve, 1)

            def a_head(c, h, more=0):
                for j in range(A_HEAD):
                    if j == 4:
                        a_norms(h)
                    if j == 5:
                        a_norm_qk(h)
                    if is_turn(h, H - 1) and j == 6:
                        split_o(a_oT, 0)
                        split_o(a_oT, 1)
                    if j < 4:
                        split(c + j + LEAD, more, a_width(j + LEAD))
                    elif j < 6:
                        split(c + j + LEAD + 1, more, a_width(j + LEAD + 1))
                    if is_turn(h, 0):
                        begin(0, G_MIX, j)
                        if j == 0:
                            take_bias_rows()
                        if j == 1:
                            take_consts()
                        if j == 2:
                            make_lambda()
                        if j == 7:
                            dve.wait_ge(a_bias_ready, 1)
                    else:
                        a_attend(j, h - 1, A_STEPS)
                    if j == 3:
                        a_take_qk(c + j, h, more)
                        split(c + j + LEAD + 1, more, a_width(j + LEAD + 1))
                    if j == 7:
                        a_take_v(c + j, h, more)
                        split(c + j + LEAD, more)
                        a_take_k(h)

            splits = [0]

            def split_o(oT, hd):
                splits[0] += 1
                dve.wait_ge(xs_hi, splits[0])
                k = slice(2 * hd, 2 * hd + 2)
                nc.vector.tensor_tensor(xT[:, k, 1, :], oT[:, k, :], xT[:, k, 0, :], ALU.subtract).then_inc(xs_lo, 1)

            def out_proj(c, n, gain, oT, attend, steps):
                for j in range(OUT):
                    split(c + j + LEAD)
                    if j < 5:
                        split_o(oT, j + 2)
                    if j == 3 and n == 1:
                        a_norms(H)
                    attend(j, H - 1, steps)
                    if j == steps[-1]:
                        split_o(oT, H - 1)
                    if j in (7, 15):
                        half = j // 8
                        chunk_used(dve, c + j)
                        for q in range(2):
                            add_quarter(2 * half + q, (4 * half + 2 * q, 4 * half + 2 * q + 1))
                    if j in (9, 11):
                        take_xT(n, gain, (j - 9) // 2)

            def taps(layer, tile, dst, init, t, tg, last):
                for b in range(4):
                    ch = bass.ds(t * 4 + (FB * tile + b), 1)
                    dve.wait_ge(init, 4 * tg + b + 1)
                    chain.step(nc.vector.scalar_tensor_tensor(
                        out=dst[:, b, :], in0=u[:, b, 1:SEQ + 1], scalar=conv[:, layer, 1, ch], in1=dst[:, b, :],
                        op0=ALU.mult, op1=ALU.add))
                chain.settle()
                for b in range(4):
                    ch = bass.ds(t * 4 + (FB * tile + b), 1)
                    ins = nc.vector.scalar_tensor_tensor(
                        out=dst[:, b, :], in0=u[:, b, 0:SEQ], scalar=conv[:, layer, 0, ch], in1=dst[:, b, :],
                        op0=ALU.mult, op1=ALU.add)
                last(ins)

            def up_pair(layer, n, c, t, tg, more=0):
                for j in range(UP_PAIR):
                    if j % 4 or (j == 0 and is_turn(t, 0)):
                        split(c + j + LEAD, more)
                    if is_turn(t, 0):
                        begin(n, G_FFN + KB * layer, j)
                    if is_turn(t, UP_PAIRS - 1) and j in (5, 6):
                        split_h(layer, j - 5)
                    if j == 3 or j == 7:
                        tile = j // 4
                        chunk_used(dve, c + j, more)
                        acc = psum[:, 4 * tile:4 * tile + 4, :]
                        dve.wait_ge(val_low if tile else gate_low, tg + 1)
                        read, scaled = (val_read, val_scaled) if tile else (gate_read, gate_scaled)
                        inner = u[:, :, 2:SEQ + 2]
                        nc.vector.tensor_tensor(inner, acc[:, :, 0:SEQ], c_val if tile else c_gate,
                                                ALU.add).then_inc(read, 1)
                        dve.wait_ge(read, tg + 1)
                        if is_turn(t, 0) and tile == 0:
                            dve.wait_ge(rstd_row_ready, layer + 1)
                        nc.vector.tensor_tensor(inner, inner, rstd_row[:, :].unsqueeze(1).to_broadcast([P, 4, SEQ]),
                                                ALU.mult).then_inc(scaled, 1)
                        split(c + j + LEAD + 1, more)
                        dve.wait_ge(scaled, tg + 1)
                    if j == 3:
                        taps(layer, 0, c_gate, gate_init, t, tg, lambda ins: ins.then_inc(gate_taps, 1))
                    if j == 7:
                        taps(layer, 1, c_val, val_init, t, tg, chain.step)
                        chain.settle()
                        dve.wait_ge(silu_ready, tg + 1)
                        nc.vector.tensor_tensor(hT[:, bass.ds(t * 4, 4), :], c_gate, c_val,
                                                ALU.mult).then_inc(h_ready, 1)

            def split_h(layer, b, t=0):
                slot = 4 * b if b == 0 else 4 + 4 * ((b - 1) % 2)
                dve.wait_ge(xs_hi, splits[0] + b + 1 + 2 * t)
                nc.vector.tensor_tensor(xT[:, slot:slot + 4, 1, :], hT[:, bass.ds(4 * b + 8 * t, 4), :],
                                        xT[:, slot:slot + 4, 0, :], ALU.subtract).then_inc(xs_lo, 1)

            def down(layer, c):
                for j in range(1, 4):
                    split(c + j + LEAD)
                with dve.Fori(0, 4) as t:
                    for j in range(8):
                        split(c + 4 + j + LEAD, t * 8)
                        if j == 1:
                            split_h(layer, 2, t)
                        if j == 5:
                            split_h(layer, 3, t)
                for j in range(8):
                    split(c + 36 + j + LEAD)
                    if j == 1:
                        split_h(layer, 10)
                splits[0] += DOWN // 4
                for q in range(4):
                    if q < 3:
                        dve.wait_ge(down_quarter, 3 * layer + q + 1)
                    else:
                        chunk_used(dve, c + DOWN - 1)
                    add_quarter(q, (2 * q, 2 * q + 1))
                    if q == 2 and layer == 0:
                        take_xT(2, G_MIX + KB, 0)
                if layer == 0:
                    take_xT(2, G_MIX + KB, 1)

            def ffn(layer, n):
                chain.step(nc.vector.memset(u[:, :, 0:2], 0.0))
                chain.settle()
                c = UP0[layer]
                up_pair(layer, n, c, 0, UP_PAIRS * layer)
                with dve.Fori(1, UP_PAIRS - 1) as t, chain.loop(t - 1, UP_PAIRS - 2, 9):
                    up_pair(layer, n, c + UP_PAIR, t, t + UP_PAIRS * layer, (t - 1) * UP_PAIR)
                up_pair(layer, n, c + UP_PAIR * (UP_PAIRS - 1), UP_PAIRS - 1, UP_PAIRS * (layer + 1) - 1)
                down(layer, DN0[layer])

            def b_take(c, g, h, odd, more):
                chunk_used(dve, c, more)
                at_least(dve, b_tqk, h)
                at_least(dve, b_vheld, h)
                nc.vector.tensor_scalar(b_raw[:, 2 * g + 1, :], psum[:, b_bank(g, odd) + 1, :], r_r[:, 1:2], None,
                                        ALU.mult).then_inc(b_raw_dve, 1)

            def b_norm(h):
                dve.wait_ge(b_sq_ready, h + 1)
                chain.step(nc.vector.tensor_reduce(n_ss, b_sq.rearrange("p m (s e) -> p (m s) e", e=HD), AX.X, ALU.add))
                rsqrt(n_r, n_ss, n_t, [(slice(0, 12), 1.0 / HD)], None)
                chain.settle()
                v = b_raw[:, :, 0:256].rearrange("p m (s e) -> p m s e", e=HD)
                r = n_r.rearrange("p (m s) -> p m s", s=2).unsqueeze(3).to_broadcast([P, G * M, 2, HD])
                nc.vector.tensor_tensor(v, v, r, ALU.mult).then_inc(b_qkn, 1)

            def b_attend(j, h, steps):
                if j == 0:
                    b_norm(h)
                if j == steps[0]:
                    dve.wait_ge(b_tqk, h + 1)
                    at_least(dve, b_scores, h)
                    for g in range(G):
                        at = SEQ * (g % 2)
                        ins = nc.vector.tensor_scalar(b_kT[:, g, :], psum[:, 6 + g // 2, at:at + SEQ],
                                                      gains[:, G_BK + g:G_BK + g + 1], None, ALU.mult)
                    ins.then_inc(b_kT_ready, 1)
                if j == steps[1]:
                    dve.wait_ge(b_scores, h + 1)
                    dve.wait_ge(b_bias_ready, h + 1)
                    lg1 = b_lg[:, 0:768].rearrange("p (a b) -> p a b", a=3)
                    lg0 = b_lg[:, 768:1152].rearrange("p (a b) -> p a b", a=3)
                    for dst, src, bias in (
                            (lg1[:, 0:2, :], psum[:, 4, :].rearrange("p (a b) -> p a b", a=2), b_bias[:, 0:2, :]),
                            (lg1[:, 2:3, :], psum[:, 5, 0:256].rearrange("p (a b) -> p a b", a=1), b_bias[:, 2:3, :]),
                            (lg0, psum[:, 7, 0:384].rearrange("p (a b) -> p a b", a=3), b_bias[:, :, P:SEQ])):
                        ins = nc.vector.scalar_tensor_tensor(out=dst, in0=src, scalar=SCALE, in1=bias, op0=ALU.mult,
                                                             op1=ALU.add)
                    ins.then_inc(b_lg_ready, 1)
                    dve.wait_ge(b_lg_ready, h + 1)
                    nc.vector.tensor_reduce(mx[:, 1:2], b_lg[:, 0:768], AX.X, ALU.max)
                    chain.step(nc.vector.tensor_reduce(mx[:, 0:1], b_lg[:, 768:1152], AX.X, ALU.max))
                    chain.settle()
                    nc.vector.tensor_scalar(nmx[:, 0:2], mx[:, 0:2], -1.0, None, ALU.mult).then_inc(b_nmx, 1)
                    dve.wait_ge(b_exp, h + 1)
                    nc.vector.reciprocal(rden[:, 0:2], den[:, 0:2]).then_inc(b_rden, 1)
                if j == steps[2]:
                    dve.wait_ge(b_tp, h + 1)
                    at_least(dve, b_pv, h)
                    nc.vector.tensor_copy(b_pT[:, 4:6, :], psum[:, 5, 0:256].rearrange("p (a b) -> p a b", a=2))
                    nc.vector.tensor_copy(b_pT[:, 6:9, :],
                                          psum[:, 6, 0:384].rearrange("p (a b) -> p a b", a=3)).then_inc(b_pT_dve, 1)
                if j == steps[3]:
                    dve.wait_ge(b_pv, h + 1)
                    nc.vector.tensor_copy(b_oT[:, bass.ds(2 * h + 1, 1), :],
                                          psum[:, 5, 0:SEQ].rearrange("p (a b) -> p a b", a=1)).then_inc(b_oT_dve, 1)

            def b_head(c, h, odd, more=0):
                for j in range(B_HEAD):
                    split(c + j + LEAD, more)
                    if is_turn(h, 0):
                        begin(2, G_MIX + KB, j)
                    else:
                        b_attend(j, h - 1, B_STEPS)
                    if is_turn(h, H - 1) and j == 10:
                        split_o(b_oT, 0)
                        split_o(b_oT, 1)
                    if j % 4 == 3:
                        b_take(c + j, j // 4, h, odd, more)

            def take_bias_rows():
                dve.wait_ge(pe_setup, 2)
                nc.vector.tensor_copy(t_rows[0:H, :], psum[0:H, 3, 0:ROW]).then_inc(bias_rows_made, 1)

            def take_consts():
                dve.wait_ge(pe_setup, 3)
                nc.vector.tensor_copy(gains[:, G_AQ:], psum[:, 2, 8 * FB:8 * FB + GAINS - G_AQ])
                for layer in range(2):
                    ins = nc.vector.tensor_copy(conv[:, layer, :, :],
                                                psum[:, 2 + layer, 0:8 * FB].rearrange("p (a b) -> p a b", a=4))
                ins.then_inc(consts_ready, 1)

            def make_lambda():
                dve.wait_ge(lam_in, 16)
                for i in range(2):
                    ins = nc.vector.tensor_tensor_reduce(t_prod[:, i, :], t_lam[:, 2 * i, :], t_lam[:, 2 * i + 1, :], 1.0,
                                                         0.0, ALU.mult, ALU.add, lam_s[:, i:i + 1])
                ins.then_inc(lam_prod, 1)
                dve.wait_ge(consts_ready, 1)
                nc.vector.tensor_scalar(sub_g[:, :], gains[:, G_SUB:G_SUB + 2], 1.0 - LAM_INIT, None, ALU.mult)
                dve.wait_ge(lam_exp, 1)
                nc.vector.tensor_scalar(nlam[:, :], lam_e[:, 1:2], lam_e[:, 0:1], LAM_INIT, ALU.subtract,
                                        ALU.subtract).then_inc(lam_ready, 1)
                dve.wait_ge(lam_ready, 1)

            dve.wait_ge(pe_setup, 1)
            nc.vector.tensor_copy(gains[:, 0:G_AQ], psum[:, 0, 0:G_AQ]).then_inc(gains_ready, 1)
            split(0)
            dve.wait_ge(gains_ready, 1)
            take_xT(0, G_MIX, 0)
            split(1)
            take_xT(0, G_MIX, 1)

            a_head(A0, 0)
            with dve.Fori(0, H // 2 - 1) as t, chain.loop(t, H // 2 - 1, 2 * (RSQRT_STEPS - 1 + 4)):
                for i in (1, 2):
                    a_head(A0 + i * A_HEAD, t * 2 + i, t * (2 * A_HEAD))
            a_head(A0 + (H - 1) * A_HEAD, H - 1)
            out_proj(AO0, 1, G_FFN, a_oT, a_attend, A_LAST_STEPS)
            ffn(0, 1)
            b_head(B0, 0, 0)
            with dve.Fori(0, H // 2 - 1) as t, chain.loop(t, H // 2 - 1, 2 * (1 + RSQRT_STEPS + 1)):
                for i in (1, 2):
                    b_head(B0 + i * B_HEAD, t * 2 + i, i % 2, t * (2 * B_HEAD))
            b_head(B0 + (H - 1) * B_HEAD, H - 1, 1)
            out_proj(BO0, 3, G_FFN + KB, b_oT, b_attend, B_LAST_STEPS)
            ffn(1, 3)

        @block.tensor
        def _(pe):
            def part_of(ring, slot, at, n):
                return ring[:, slot, at:at + n]

            def transpose_resid(n, q):
                if n == 0:
                    pe.wait_ge(x_in[q], 16)
                    if q == 2:
                        pe.wait_ge(xT_lo, 8)
                else:
                    pe.wait_ge(r_add, 4 * (n - 1) + q + 1)
                for k in range(4 * q, 4 * q + 4):
                    for m in range(M):
                        at = 256 * (k % 2) + P * m
                        ins = pe.transpose(psum[:, xT_bank(n, k), at:at + P], resid[:, m, P * k:P * (k + 1)], ident[:, :])
                    if k % 2 == 1:
                        ins.then_inc(xT_ps, 1)

            def begin(n, j):
                if j == 0:
                    transpose_resid(n, 2)
                    transpose_resid(n, 3)

            def moving(c, more, blocks, n, outs, first, last, second_free=None):
                slot = c % SLOTS
                pe.wait_ge(lo_ready, c + 1 + more)
                for i, k in enumerate(blocks):
                    for t, banks in enumerate(outs):
                        at = (i * len(outs) + t) * n
                        hi, lo = part_of(w_hi, slot, at, n), part_of(w_lo, slot, at, n)
                        if second_free and (i, t) == (0, 1):
                            second_free()
                        for m in range(M):
                            xh, xl = xT[:, k, 0, P * m:P * (m + 1)], xT[:, k, 1, P * m:P * (m + 1)]
                            o = psum[:, banks[m], 0:n]
                            pe.matmul(o, xh, hi, start=(first and i == 0), stop=False)
                            pe.matmul(o, xh, lo, start=False, stop=False)
                            ins = pe.matmul(o, xl, hi, start=False, stop=(last and i == len(blocks) - 1))
                ins.then_inc(used, 1)

            def a_transpose_qk(h):
                pe.wait_ge(a_qkn, h + 1)
                at_least(pe, a_aT_ready, h)
                at_least(pe, a_on, h)
                for s in range(2):
                    for i in range(2):
                        for m in range(M):
                            at = 256 * i + P * m
                            ins = pe.transpose(psum[:, 4 + s, at:at + P],
                                               a_qk[:, m, 256 * s + HD * i:256 * s + HD * (i + 1)], ident[:, :])
                ins.then_inc(a_tqk, 1)

            def a_score(h):
                pe.wait_ge(a_qT_ready, h + 1)
                pe.wait_ge(a_kT_ready, h + 1)
                at_least(pe, a_lg_ready, h)
                at_least(pe, a_oT_act, h)
                at_least(pe, a_oT_dve, h)
                for i in range(2):
                    pe.matmul(psum[:, 6, SEQ * i:SEQ * (i + 1)], a_qT[:, i, P:SEQ], a_kT[:, i, :], start=True, stop=True)
                for i in range(2):
                    ins = pe.matmul(psum[:, 7, P * i:P * (i + 1)], a_qT[:, i, 0:P], a_kT[:, i, 0:P], start=True, stop=True)
                ins.then_inc(a_scores, 1)

            def a_attend(j, h, steps):
                if j == steps[0]:
                    a_score(h)
                if j == steps[1]:
                    pe.wait_ge(a_diff, h + 1)
                    for i in range(3):
                        ins = pe.transpose(psum[:, 4, P * i:P * (i + 1)], a_a[:, P * i:P * (i + 1)], ident[:, :])
                    ins.then_inc(a_ta, 1)
                if j == steps[2]:
                    pe.wait_ge(a_aT_ready, h + 1)
                    pe.wait_ge(a_v_act, h + 1)
                    pe.wait_ge(a_v_dve, h + 1)
                    pe.matmul(psum[:, 5, 0:VD], a_aT[:, 0, :], a_v[:, 0, :], start=True, stop=True)
                    pe.matmul(psum[:, 5, VD:2 * VD], a_aT[:, 1, :], a_v[:, 0, :], start=True, stop=False)
                    pe.matmul(psum[:, 5, VD:2 * VD], a_aT[:, 2, :], a_v[:, 1, :], start=False, stop=True).then_inc(a_pv, 1)
                if j == steps[3]:
                    pe.wait_ge(a_on, h + 1)
                    for e in range(2):
                        for b in range(M):
                            ins = pe.transpose(psum[:, 6 + e, P * b:P * (b + 1)], a_o[:, b, P * e:P * (e + 1)], ident[:, :])
                    ins.then_inc(a_to, 1)

            def a_head(c, h, more=0):
                for j in range(A_HEAD):
                    ks = range(4 * (j % 4), 4 * (j % 4) + 4)
                    if j == 0:
                        at_least(pe, a_qk_act, h)
                        at_least(pe, a_qk_dve, h)
                    if j == 4:
                        at_least(pe, a_v_act, h)
                        at_least(pe, a_v_dve, h)
                        if is_turn(h, 0):
                            pe.wait_ge(consts_ready, 1)
                    if is_turn(h, 0) and j < 4:
                        pe.wait_ge(xT_lo, 4 * j + 4)
                    n = 512 if j < 4 else VD
                    moving(c + j, more, ks, n, [(0, 1) if j < 4 else (2, 3)], j % 4 == 0, j % 4 == 3)
                    if is_turn(h, 0):
                        begin(0, j)
                        if j == 0:
                            make_bias_rows()
                        if j == 1:
                            make_consts()
                    else:
                        a_attend(j, h - 1, A_STEPS)
                    if j == 7:
                        a_transpose_qk(h)

            splits = [0]

            def out_proj(c, n, first_read, second_read, attend, steps):
                def read(semaphores, count):
                    for semaphore in semaphores:
                        pe.wait_ge(semaphore, count)

                read(*first_read)
                for j in range(OUT):
                    if j < 8:
                        splits[0] += 1
                        pe.wait_ge(xs_lo, splits[0])
                    b = 4 * (j // 8)
                    moving(c + j, 0, (2 * (j % 8), 2 * (j % 8) + 1), 512, [(b, b + 1), (b + 2, b + 3)],
                           j % 8 == 0, j % 8 == 7, (lambda: read(*second_read)) if j == 0 else None)
                    attend(j, H - 1, steps)
                    if j in (8, 9):
                        transpose_resid(n, j - 8)

            def up_chunk(c, more, j, bank):
                slot = c % SLOTS
                pe.wait_ge(lo_ready, c + 1 + more)
                for i in range(4):
                    k = 4 * j + i
                    for b in range(4):
                        at = 512 * i + P * b
                        both = psum[:, bank + b, :].rearrange("p (a b) -> p a b", a=2)

                        def high():
                            return pe.matmul(both, w_hi[:, slot, at:at + P], xT[:, k, :, :], start=(k == 0),
                                             stop=(k == KB - 1))

                        def low():
                            return pe.matmul(psum[:, bank + b, 0:SEQ], w_lo[:, slot, at:at + P], xT[:, k, 0, :],
                                             start=False, stop=False)

                        if k == 0:
                            high()
                            ins = low()
                        else:
                            low()
                            ins = high()
                ins.then_inc(used, 1)

            def up_pair(layer, n, c, tg, more=0):
                first = isinstance(tg, int) and tg % UP_PAIRS == 0
                for j in range(UP_PAIR):
                    if j == 0:
                        at_least(pe, gate_read, tg)
                    if j == 4:
                        at_least(pe, val_read, tg)
                        if first:
                            pe.wait_ge(rstd_row_ready, n // 2 + 1)
                    if first and j < 4:
                        pe.wait_ge(xT_lo, KB * n + 4 * j + 4)
                    up_chunk(c + j, more, j % 4, 4 * (j // 4))
                    if first:
                        begin(n, j)
                    if first and j == 2:
                        pe.wait_ge(r_rstd, n + 1)
                        pe.wait_ge(xT_lo, KB * (n + 1))
                        for m in range(M):
                            ins = pe.matmul(psum[:, 4, P * m:P * (m + 1)], r_r[:, m:m + 1].to_broadcast([P, P]),
                                            ident[:, :], start=True, stop=True)
                        ins.then_inc(rstd_ps, 1)

            def down_chunk(layer, c, more, slot_k, first=False, last=False):
                slot = c % SLOTS
                pe.wait_ge(lo_ready, c + 1 + more)
                for q in range(4):
                    if first and q == 0:
                        pe.wait_ge(gate_read, UP_PAIRS * (layer + 1))
                    if first and q == 2:
                        pe.wait_ge(val_read, UP_PAIRS * (layer + 1))
                    hi, lo = part_of(w_hi, slot, 512 * q, 512), part_of(w_lo, slot, 512 * q, 512)
                    for m in range(M):
                        xh, xl = xT[:, slot_k, 0, P * m:P * (m + 1)], xT[:, slot_k, 1, P * m:P * (m + 1)]
                        o = psum[:, 2 * q + m, :]
                        pe.matmul(o, xh, hi, start=first, stop=False)
                        pe.matmul(o, xh, lo, start=False, stop=False)
                        ins = pe.matmul(o, xl, hi, start=False, stop=last)
                    if last and q < 3:
                        ins.then_inc(down_quarter, 1)
                ins.then_inc(used, 1)

            def down(layer, c):
                def block_ready(b, t=0):
                    pe.wait_ge(xs_lo, splits[0] + b + 1 + 2 * t)

                block_ready(0)
                for j in range(4):
                    down_chunk(layer, c + j, 0, j, first=(j == 0))
                with pe.Fori(0, 4) as t:
                    for j in range(8):
                        if j % 4 == 0:
                            block_ready(1 + j // 4, t)
                        down_chunk(layer, c + 4 + j, t * 8, 4 + j)
                for j in range(8):
                    if j % 4 == 0:
                        block_ready(9 + j // 4)
                    down_chunk(layer, c + 36 + j, 0, 4 + j, last=(j == 7))
                splits[0] += DOWN // 4

            def ffn(layer, n):
                c = UP0[layer]
                up_pair(layer, n, c, UP_PAIRS * layer)
                with pe.Fori(1, UP_PAIRS - 1) as t:
                    up_pair(layer, n, c + UP_PAIR, t + UP_PAIRS * layer, (t - 1) * UP_PAIR)
                up_pair(layer, n, c + UP_PAIR * (UP_PAIRS - 1), UP_PAIRS * (layer + 1) - 1)
                down(layer, DN0[layer])

            def b_attend(j, h, steps):
                if j == steps[0]:
                    pe.wait_ge(b_qkn, h + 1)
                    at_least(pe, b_oT_act, h)
                    at_least(pe, b_oT_dve, h)
                    for g in range(G):
                        for s in range(2):
                            for m in range(M):
                                at = SEQ * (g % 2) + P * m
                                ins = pe.transpose(psum[:, 4 + 2 * s + g // 2, at:at + P],
                                                   b_raw[:, 2 * g + m, HD * s:HD * (s + 1)], ident[:, :])
                    ins.then_inc(b_tqk, 1)
                if j == steps[1]:
                    pe.wait_ge(b_qT_ready, h + 1)
                    pe.wait_ge(b_kT_ready, h + 1)
                    for g in range(G):
                        at = SEQ * (g % 2)
                        pe.matmul(psum[:, 4 + g // 2, at:at + SEQ], b_qT[:, g, P:SEQ], b_kT[:, g, :], start=True, stop=True)
                    for g in range(G):
                        ins = pe.matmul(psum[:, 7, P * g:P * (g + 1)], b_qT[:, g, 0:P], b_kT[:, g, 0:P],
                                        start=True, stop=True)
                    ins.then_inc(b_scores, 1)
                if j == steps[2]:
                    pe.wait_ge(b_probs, h + 1)
                    for i in range(9):
                        g = i // 3
                        src = P * (2 * G + g, 2 * g, 2 * g + 1)[i % 3]
                        bank, at = (4, P * i) if i < 4 else (5, P * (i - 4)) if i < 6 else (6, P * (i - 6))
                        ins = pe.transpose(psum[:, bank, at:at + P], b_lg[:, src:src + P], ident[:, :])
                    ins.then_inc(b_tp, 1)
                if j == steps[3]:
                    pe.wait_ge(b_pT_act, h + 1)
                    pe.wait_ge(b_pT_dve, h + 1)
                    pe.wait_ge(b_vheld, h + 1)
                    for e, bank in enumerate((7, 5)):
                        def keys(g, b):
                            return b_v[:, 2 * g + b, P * e:P * (e + 1)]

                        for g in range(G):
                            both = b_pT[:, 3 * g:3 * g + 2, :].rearrange("p a b -> p (a b)")
                            if g == G - 1:
                                for i in range(G):
                                    pe.matmul(psum[:, bank, P:SEQ], keys(i, 1), b_pT[:, 3 * i + 2, :], start=False,
                                              stop=False)
                            ins = pe.matmul(psum[:, bank, 0:SEQ], keys(g, 0), both, start=(g == 0), stop=(g == G - 1))
                    ins.then_inc(b_pv, 1)

            def b_head(c, h, odd, more=0):
                for j in range(B_HEAD):
                    g = j // 4
                    if j % 4 == 0:
                        at_least(pe, b_raw_act, 3 * h + g - 1)
                        at_least(pe, b_raw_dve, 3 * h + g - 1)
                    if is_turn(h, 0) and j < 4:
                        pe.wait_ge(xT_lo, KB * 2 + 4 * j + 4)
                    b = b_bank(g, odd)
                    moving(c + j, more, range(4 * (j % 4), 4 * (j % 4) + 4), 512, [(b, b + 1)], j % 4 == 0, j % 4 == 3)
                    if is_turn(h, 0):
                        begin(2, j)
                    else:
                        b_attend(j, h - 1, B_STEPS)

            def make_bias_rows():
                pe.wait_ge(onehot_in, 16)
                pe.wait_ge(rel_in, 16)
                pe.matmul(psum[0:H, 3, 0:ROW], t_rel[0:BUCKETS, :], t_onehot[0:BUCKETS, :], start=True,
                          stop=True).then_inc(pe_setup, 1)

            def make_consts():
                pe.wait_ge(small_gain_in, 16 * 5)
                pe.wait_ge(conv_in, 16 * 4)
                pe.wait_ge(bias_rows_made, 1)
                for i in range(8):
                    at = 2 * FB * (i % 4)
                    pe.transpose(psum[:, 2 + i // 4, at:at + 2 * FB], t_conv[0:2 * FB, i, :], ident[0:2 * FB, 0:2 * FB])
                pe.matmul(psum[:, 2, 8 * FB:8 * FB + GAINS - G_AQ], t_gain[0:GAINS, :], ident[0:GAINS, G_AQ:GAINS],
                          start=True, stop=True).then_inc(pe_setup, 1)

            pe.wait_ge(ident_in, 16)
            pe.wait_ge(gain_in, 16 * 2)
            pe.transpose(psum[:, 0, 0:G_AQ], t_gain[0:G_AQ, :], ident[0:G_AQ, 0:G_AQ]).then_inc(pe_setup, 1)
            transpose_resid(0, 0)
            transpose_resid(0, 1)
            pe.wait_ge(gains_ready, 1)
            a_head(A0, 0)
            with pe.Fori(0, H // 2 - 1) as t:
                for i in (1, 2):
                    a_head(A0 + i * A_HEAD, t * 2 + i, t * (2 * A_HEAD))
            a_head(A0 + (H - 1) * A_HEAD, H - 1)
            out_proj(AO0, 1, ((a_qk_act, a_qk_dve), H), ((a_v_act, a_v_dve), H), a_attend, A_LAST_STEPS)
            ffn(0, 1)
            transpose_resid(2, 0)
            transpose_resid(2, 1)
            b_head(B0, 0, 0)
            with pe.Fori(0, H // 2 - 1) as t:
                for i in (1, 2):
                    b_head(B0 + i * B_HEAD, t * 2 + i, i % 2, t * (2 * B_HEAD))
            b_head(B0 + (H - 1) * B_HEAD, H - 1, 1)
            out_proj(BO0, 3, ((b_raw_act, b_raw_dve), 3 * H - 1), ((b_raw_act, b_raw_dve), 3 * H), b_attend, B_LAST_STEPS)
            ffn(1, 3)


INPUTS = ["x", "rel_bias", "ln_mix", "ln_ffn", "a_w_qkv", "a_q_norm", "a_k_norm", "a_lambda", "a_subln", "a_w_o",
          "b_w_qkv", "b_q_norm", "b_k_norm", "b_w_o", "f_w_up", "f_conv_w", "f_conv_b", "f_w_down"]


def kernel(**inputs):
    from concourse import bacc
    from concourse.bass_utils import run_bass_kernel_spmd

    nc = bacc.Bacc("TRN2", target_bir_lowering=False, num_devices=1)
    arrays = {name: np.ascontiguousarray(inputs[name]) for name in INPUTS}
    arrays.update(shape_tables())
    given = {n: nc.dram_tensor(f"in_{n}", a.shape, mybir.dt.from_np(a.dtype), kind="ExternalInput").ap()
             for n, a in arrays.items()}
    out = nc.dram_tensor("out", (1, SEQ, D), F32, kind="ExternalOutput").ap()
    trunk(nc, **given, out=out)
    run = run_bass_kernel_spmd(nc, [{f"in_{n}": a for n, a in arrays.items()}], core_ids=[0])
    return run.results[0]["out"]
```
